# Optimizing a Trainium2 kernel written in Bass

```python
import jax, jax.numpy as jnp
from jax import lax
import numpy as np

D_MODEL = 1024
BATCH = 1
SEQ = 512
DEPTH = 1

DSA_HEADS = 8
DSA_HEAD_DIM = 64
DSA_WIDTH = DSA_HEADS * DSA_HEAD_DIM
IDX_HEADS = 8
IDX_DIM = 64
TOPK_MAX = 256
Q_BLOCK = 128
ROPE_THETA = 10000.0
GDN_HEADS = 8
GDN_DK = 64
GDN_DV = 64
GDN_QK_WIDTH = GDN_HEADS * GDN_DK
GDN_V_WIDTH = GDN_HEADS * GDN_DV
CONV_WIDTH = 4
CONV_CH = 2 * GDN_QK_WIDTH + GDN_V_WIDTH
CHUNK = 64
N_GROUPS = 4
EXPERTS_PER_GROUP = 4
N_EXPERTS = N_GROUPS * EXPERTS_PER_GROUP
TOP_K_IN_GROUP = 2
D_EXPERT = 256
NORM_EPS = 1e-6

SPLIT_SIZES = (DSA_WIDTH, DSA_WIDTH, DSA_WIDTH, IDX_HEADS * IDX_DIM, IDX_DIM, IDX_HEADS,
               GDN_QK_WIDTH, GDN_QK_WIDTH, GDN_V_WIDTH, GDN_V_WIDTH, GDN_HEADS, GDN_HEADS,
               D_MODEL, D_MODEL)
D_IN = sum(SPLIT_SIZES)

kernel_name = "hybrid_dsa_gdn_hmoe_block"

def rms_norm(x, w):
    xf = x.astype(jnp.float32)
    y = xf * lax.rsqrt(jnp.mean(xf * xf, axis=-1, keepdims=True) + NORM_EPS)
    return (y * w.astype(jnp.float32)).astype(x.dtype)

def l2_normalize(x):
    xf = x.astype(jnp.float32)
    return xf * lax.rsqrt(jnp.sum(xf * xf, axis=-1, keepdims=True) + NORM_EPS)

def rope_tables(positions, dim):
    inv_freq = ROPE_THETA ** (-jnp.arange(0, dim, 2, dtype=jnp.float32) / dim)
    ang = positions.astype(jnp.float32)[..., None] * inv_freq
    return jnp.cos(ang), jnp.sin(ang)

def apply_rope(x, cos, sin):
    x1, x2 = jnp.split(x.astype(jnp.float32), 2, axis=-1)
    return jnp.concatenate([x1 * cos - x2 * sin, x2 * cos + x1 * sin], axis=-1).astype(x.dtype)

def dsa_attention(q, k, v, qi, ki, wi, n_keep):
    B, S, H, Dh = q.shape
    nb = S // Q_BLOCK
    key_pos = jnp.arange(S)
    idx_scale = (IDX_HEADS * IDX_DIM) ** -0.5
    att_scale = Dh ** -0.5
    ki32 = ki.astype(jnp.float32)
    b_idx = jnp.arange(B)[:, None, None]

    def to_blocks(t):
        return t.reshape((B, nb, Q_BLOCK) + t.shape[2:]).swapaxes(0, 1)

    def block(args):
        q_b, qi_b, wi_b, start = args
        qpos = start + jnp.arange(Q_BLOCK)
        causal = key_pos[None, :] <= qpos[:, None]
        logits = jnp.einsum('bqhd,bsd->bqhs', qi_b.astype(jnp.float32), ki32)
        score = jnp.einsum('bqh,bqhs->bqs', wi_b.astype(jnp.float32), jax.nn.relu(logits)) * idx_scale
        score = jnp.where(causal[None], score, -jnp.inf)
        _, sel = lax.top_k(score, n_keep)
        k_sel = k[b_idx, sel].astype(jnp.float32)
        v_sel = v[b_idx, sel].astype(jnp.float32)
        valid = sel <= qpos[None, :, None]
        s = jnp.einsum('bqhd,bqkhd->bhqk', q_b.astype(jnp.float32), k_sel) * att_scale
        s = jnp.where(valid[:, None], s, -jnp.inf)
        p = jax.nn.softmax(s, axis=-1)
        o = jnp.einsum('bhqk,bqkhd->bqhd', p, v_sel)
        return o.astype(q.dtype)

    starts = jnp.arange(nb) * Q_BLOCK
    out = lax.map(block, (to_blocks(q), to_blocks(qi), to_blocks(wi), starts))
    return out.swapaxes(0, 1).reshape(B, S, H, Dh)

def causal_conv_silu(x, w):
    S = x.shape[1]
    xp = jnp.pad(x, ((0, 0), (CONV_WIDTH - 1, 0), (0, 0)))
    y = sum(xp[:, j:j + S] * w[j] for j in range(CONV_WIDTH))
    return jax.nn.silu(y)

def gated_delta_chunked(q, k, v, g, beta):
    B, S, H, dk = q.shape
    dv = v.shape[-1]
    N = S // CHUNK

    def chunks(t):
        t = jnp.moveaxis(t, 2, 1)
        t = t.reshape(t.shape[:2] + (N, CHUNK) + t.shape[3:])
        return jnp.moveaxis(t, 2, 0)

    q = chunks(q) * dk ** -0.5
    k, v, g, beta = chunks(k), chunks(v), chunks(g), chunks(beta)
    gc = jnp.cumsum(g, axis=-1)
    tri_incl = jnp.tril(jnp.ones((CHUNK, CHUNK), bool))
    tri_strict = jnp.tril(jnp.ones((CHUNK, CHUNK), bool), -1)
    diff = gc[..., :, None] - gc[..., None, :]
    decay = jnp.where(tri_incl, jnp.exp(jnp.where(tri_incl, diff, 0.0)), 0.0)
    kb = k * beta[..., None]
    vb = v * beta[..., None]
    lmat = jnp.where(tri_strict, jnp.einsum('nbhid,nbhjd->nbhij', kb, k) * decay, 0.0)
    a_mat = jnp.eye(CHUNK, dtype=jnp.float32) + lmat
    rhs = jnp.concatenate([vb, kb * jnp.exp(gc)[..., None]], axis=-1)
    sol = lax.linalg.triangular_solve(a_mat, rhs, left_side=True, lower=True, unit_diagonal=True)
    u, w = sol[..., :dv], sol[..., dv:]
    a_qk = jnp.einsum('nbhid,nbhjd->nbhij', q, k) * decay
    q_g = q * jnp.exp(gc)[..., None]
    k_dec = k * jnp.exp(gc[..., -1:] - gc)[..., None]
    g_last = jnp.exp(gc[..., -1])

    def step(state, xs):
        u_i, w_i, qg_i, aqk_i, kd_i, gl_i = xs
        v_new = u_i - jnp.einsum('bhck,bhkv->bhcv', w_i, state)
        o = jnp.einsum('bhck,bhkv->bhcv', qg_i, state) + jnp.einsum('bhij,bhjv->bhiv', aqk_i, v_new)
        state = state * gl_i[..., None, None] + jnp.einsum('bhck,bhcv->bhkv', kd_i, v_new)
        return state, o

    s0 = jnp.zeros((B, H, dk, dv), jnp.float32)
    _, o = lax.scan(step, s0, (u, w, q_g, a_qk, k_dec, g_last))
    o = jnp.moveaxis(o, 0, 2).reshape(B, H, S, dv)
    return jnp.moveaxis(o, 1, 2)

def hybrid_mixer(h, rope_a, rope_i, w_in, conv_w, a_log, dt_bias, gdn_norm,
                 w_branch_dsa, w_branch_gdn, w_out):
    B, S, _ = h.shape
    offsets = np.cumsum(SPLIT_SIZES)[:-1].tolist()
    (dq, dk_, dv_, iq, ik, iw, gq, gk, gv, gz, gb, ga, gate_a, gate_b) = jnp.split(h @ w_in, offsets, axis=-1)

    cos_a, sin_a = rope_a
    cos_i, sin_i = rope_i
    q = apply_rope(dq.reshape(B, S, DSA_HEADS, DSA_HEAD_DIM), cos_a[:, :, None], sin_a[:, :, None])
    k = apply_rope(dk_.reshape(B, S, DSA_HEADS, DSA_HEAD_DIM), cos_a[:, :, None], sin_a[:, :, None])
    v = dv_.reshape(B, S, DSA_HEADS, DSA_HEAD_DIM)
    qi = apply_rope(iq.reshape(B, S, IDX_HEADS, IDX_DIM), cos_i[:, :, None], sin_i[:, :, None])
    ki = apply_rope(ik, cos_i, sin_i)
    n_keep = min(TOPK_MAX, S // 4)
    y_a = dsa_attention(q, k, v, qi, ki, iw, n_keep).reshape(B, S, DSA_WIDTH)
    y_a = y_a @ w_branch_dsa

    qkv = causal_conv_silu(jnp.concatenate([gq, gk, gv], axis=-1), conv_w)
    cq, ck, cv = jnp.split(qkv, [GDN_QK_WIDTH, 2 * GDN_QK_WIDTH], axis=-1)
    qg = l2_normalize(cq.reshape(B, S, GDN_HEADS, GDN_DK))
    kg = l2_normalize(ck.reshape(B, S, GDN_HEADS, GDN_DK))
    vg = cv.reshape(B, S, GDN_HEADS, GDN_DV).astype(jnp.float32)
    beta = jax.nn.sigmoid(gb.astype(jnp.float32))
    g = -jnp.exp(a_log.astype(jnp.float32)) * jax.nn.softplus(ga.astype(jnp.float32) + dt_bias.astype(jnp.float32))
    o = gated_delta_chunked(qg, kg, vg, g, beta)
    z = gz.reshape(B, S, GDN_HEADS, GDN_DV).astype(jnp.float32)
    o = rms_norm(o, gdn_norm) * jax.nn.silu(z)
    y_b = o.reshape(B, S, GDN_V_WIDTH).astype(h.dtype) @ w_branch_gdn

    merged = jax.nn.sigmoid(gate_a) * y_a + jax.nn.sigmoid(gate_b) * y_b
    return merged @ w_out

def hierarchical_moe(h, w_rg, b_rg, w_re, b_re, w_eg, w_eu, w_ed):
    B, S, D = h.shape
    t = h.reshape(-1, D)
    grp_prob = jax.nn.softmax((t @ w_rg).astype(jnp.float32) + b_rg.astype(jnp.float32), axis=-1)
    g_w, g_id = lax.top_k(grp_prob, 1)
    e_logits = ((t @ w_re).astype(jnp.float32) + b_re.astype(jnp.float32)).reshape(-1, N_GROUPS, EXPERTS_PER_GROUP)
    in_grp = jnp.take_along_axis(e_logits, g_id[:, :, None], axis=1)[:, 0]
    e_prob = jax.nn.softmax(in_grp, axis=-1)
    e_w, e_local = lax.top_k(e_prob, TOP_K_IN_GROUP)
    e_w = e_w / jnp.sum(e_w, axis=-1, keepdims=True)
    e_id = g_id * EXPERTS_PER_GROUP + e_local
    gates = e_w * g_w
    dense_gate = jnp.sum(jax.nn.one_hot(e_id, N_EXPERTS, dtype=jnp.float32) * gates[..., None], axis=1)
    hg = jnp.einsum('td,edf->tef', t, w_eg)
    hu = jnp.einsum('td,edf->tef', t, w_eu)
    act = jax.nn.silu(hg) * hu * dense_gate[..., None].astype(t.dtype)
    y = jnp.einsum('tef,efd->td', act, w_ed)
    return y.reshape(B, S, D)

def setup_inputs(seed: int = 0) -> dict:
    key = jax.random.key(seed)
    ks = jax.random.split(key, 26)
    f32 = jnp.float32
    L, D = DEPTH, D_MODEL

    def nrm(k, shape, scale):
        return jax.random.normal(k, shape, f32) * scale

    dt = jax.random.uniform(ks[9], (L, GDN_HEADS), f32, 0.001, 0.1)
    return {
        "x": nrm(ks[0], (BATCH, SEQ, D), 1.0),
        "c": nrm(ks[1], (BATCH, D), 1.0),
        "positions": jnp.tile(jnp.arange(SEQ, dtype=jnp.int32)[None], (BATCH, 1)),
        "w_ada": nrm(ks[2], (L, D, 6 * D), 0.25 * D ** -0.5),
        "b_ada": nrm(ks[3], (L, 6 * D), 0.01),
        "mix_norm_pre": 1.0 + nrm(ks[4], (L, D), 0.02),
        "mix_norm_post": 1.0 + nrm(ks[5], (L, D), 0.02),
        "w_in": nrm(ks[6], (L, D, D_IN), D ** -0.5),
        "conv_w": nrm(ks[7], (L, CONV_WIDTH, CONV_CH), CONV_WIDTH ** -0.5),
        "a_log": jnp.log(jax.random.uniform(ks[8], (L, GDN_HEADS), f32, 1.0, 16.0)),
        "dt_bias": dt + jnp.log(-jnp.expm1(-dt)),
        "gdn_norm": 1.0 + nrm(ks[10], (L, GDN_DV), 0.02),
        "w_branch_dsa": nrm(ks[11], (L, DSA_WIDTH, D), DSA_WIDTH ** -0.5),
        "w_branch_gdn": nrm(ks[12], (L, GDN_V_WIDTH, D), GDN_V_WIDTH ** -0.5),
        "w_out": nrm(ks[13], (L, D, D), D ** -0.5),
        "ffn_norm_pre": 1.0 + nrm(ks[14], (L, D), 0.02),
        "ffn_norm_post": 1.0 + nrm(ks[15], (L, D), 0.02),
        "w_router_group": nrm(ks[16], (L, D, N_GROUPS), D ** -0.5),
        "b_router_group": nrm(ks[17], (L, N_GROUPS), 0.01),
        "w_router_expert": nrm(ks[18], (L, D, N_EXPERTS), D ** -0.5),
        "b_router_expert": nrm(ks[19], (L, N_EXPERTS), 0.01),
        "w_expert_gate": nrm(ks[20], (L, N_EXPERTS, D, D_EXPERT), D ** -0.5),
        "w_expert_up": nrm(ks[21], (L, N_EXPERTS, D, D_EXPERT), D ** -0.5),
        "w_expert_down": nrm(ks[22], (L, N_EXPERTS, D_EXPERT, D), D_EXPERT ** -0.5),
    }

def reference(x, c, positions, w_ada, b_ada, mix_norm_pre, mix_norm_post, w_in, conv_w, a_log,
              dt_bias, gdn_norm, w_branch_dsa, w_branch_gdn, w_out, ffn_norm_pre, ffn_norm_post,
              w_router_group, b_router_group, w_router_expert, b_router_expert,
              w_expert_gate, w_expert_up, w_expert_down):
    rope_a = rope_tables(positions, DSA_HEAD_DIM)
    rope_i = rope_tables(positions, IDX_DIM)
    c_act = jax.nn.silu(c)
    for l in range(DEPTH):
        mod = (c_act @ w_ada[l] + b_ada[l])[:, None, :]
        shift1, scale1, gate1, shift2, scale2, gate2 = jnp.split(mod, 6, axis=-1)
        h = rms_norm(x, mix_norm_pre[l]) * (1.0 + scale1) + shift1
        y = hybrid_mixer(h, rope_a, rope_i, w_in[l], conv_w[l], a_log[l], dt_bias[l], gdn_norm[l],
                         w_branch_dsa[l], w_branch_gdn[l], w_out[l])
        x = x + gate1 * rms_norm(y, mix_norm_post[l])
        h = rms_norm(x, ffn_norm_pre[l]) * (1.0 + scale2) + shift2
        y = hierarchical_moe(h, w_router_group[l], b_router_group[l], w_router_expert[l],
                             b_router_expert[l], w_expert_gate[l], w_expert_up[l], w_expert_down[l])
        x = (x + gate2 * rms_norm(y, ffn_norm_post[l])).astype(x.dtype)
    return x


_drawn_inputs = setup_inputs


def setup_inputs(seed=0):
    import zlib

    import numpy as np

    out = dict(_drawn_inputs(seed))
    spreads = {}
    factors = {'mix_norm_pre': 3.607,
     'mix_norm_post': 6.695,
     'gdn_norm': 6.878,
     'ffn_norm_post': 8.0,
     'b_router_group': 6.336,
     'b_router_expert': 7.885}
    for name, (base, spread) in spreads.items():
        noise = np.random.default_rng([zlib.crc32(name.encode()), seed]).standard_normal(out[name].shape)
        drawn = base * np.exp(spread * noise) if base else spread * noise
        out[name] = __import__('jax').numpy.asarray(drawn.astype(out[name].dtype))
    for name, factor in factors.items():
        out[name] = (out[name] * factor).astype(out[name].dtype)
    return out
```

```python
from contextlib import ExitStack

import numpy as np
import concourse.bass as bass
from concourse import mybir
from concourse.alu_op_type import AluOpType as ALU

F32 = mybir.dt.float32
I32 = mybir.dt.int32
ACT = mybir.ActivationFunctionType
AX = mybir.AxisListType

P = 128
D, T = 1024, 512
KD, TB = D // P, T // P
H, DH = 8, 64
HW = H * DH
NKEEP = 128
NEG = -1e30
FAR = -3e38
EPS = 1e-6
NE, DE, NG, EG = 16, 256, 4, 4
BANKS = 8
LEVELS = 7

C_Q, C_K, C_V, C_IQ = 0, HW, 2 * HW, 3 * HW
C_IK = 4 * HW
C_IW = C_IK + DH
C_GQ = C_IW + H
C_Z = C_GQ + 3 * HW
C_B = C_Z + HW
C_GA = C_B + 2 * H
C_GB = C_GA + D

(M_ID, M_UPPER, M_HEADS, M_CAUSAL, M_LOWER, M_SWAP, M_LEVEL) = range(7)
N_SQ = M_LEVEL + LEVELS
(K_FREQ, K_SIGN, K_HALFPI, K_EPS, K_ONE, K_TIE) = range(6)
N_COL = K_TIE + 4
(R_C, R_PRE1, R_PRE2, R_CONV) = (0, KD, 2 * KD, 3 * KD)
N_ROWS = R_CONV + 4 * 12


def constants():
    i = np.arange(P)
    sq = np.zeros((P, N_SQ, P), np.float32)
    sq[:, M_ID] = np.eye(P)
    sq[:, M_UPPER] = i[:, None] <= i[None, :]
    sq[:, M_HEADS] = i[:, None] // DH == i[None, :] // DH
    sq[:, M_CAUSAL] = np.where(i[None, :] <= i[:, None], 0, NEG)
    sq[:, M_LOWER] = i[:, None] > i[None, :]
    sq[:, M_SWAP] = (i[:, None] ^ (DH // 2)) == i[None, :]
    for k in range(LEVELS):
        b = 1 << k
        same = i[:, None] // (2 * b) == i[None, :] // (2 * b)
        sq[:, M_LEVEL + k] = same & (i[:, None] % (2 * b) >= b) & (i[None, :] % (2 * b) < b)
    col = np.zeros((P, N_COL), np.float32)
    half = DH // 2
    freq = np.float32(10000.0) ** (-np.arange(0, DH, 2, dtype=np.float32) / np.float32(DH))
    col[:, K_FREQ] = freq[i % half]
    col[:, K_SIGN] = np.where(i % DH < half, -1, 1)
    col[:, K_HALFPI] = np.pi / 2
    col[:, K_EPS] = EPS
    col[:, K_ONE] = 1
    col[:, K_TIE:K_TIE + 4] = [4, 3, 2, 1]
    return sq.reshape(P, N_SQ * P), col


def rotated():
    return [("q", m) for m in range(4)] + [("k", m) for m in range(4)] + [("iq", m) for m in range(4)] + [("ik", 0)]


def plan_products():
    plan = [(("rows",), "v")]
    for n in range(4):
        plan += [(("ada", n), "a"), (("adac", n), "v")]
    plan += [(("h1", f), "va"[f % 2]) for f in range(KD)]
    seq = rotated()
    for n, it in enumerate(seq):
        plan.append((("rope",) + it, "a"))
        if n >= 1:
            plan.append((("swap",) + seq[n - 1], "v"))
        if it == ("k", 3):
            plan += [(("v", t), "a") for t in range(TB)]
    plan.append((("swap",) + seq[-1], "v"))
    plan.append((("small",), "v"))
    for m in range(12):
        plan.append((("conv", m), "a"))
        if m % 3 == 2:
            for n in (4 + 2 * (m // 3), 5 + 2 * (m // 3)):
                col = 6 <= n < 10
                plan.append((("ada", n), "a" if col else "v"))
                if col:
                    plan.append((("adac", n), "v"))
    plan += [(("z", t), "a") for t in range(TB)]
    plan += [(("norm", m), "a") for m in range(8)]
    plan += [(("ktok", t), "a") for t in range(TB)] + [(("vtok", t), "a") for t in range(TB)]
    plan.append((("gc",), "v"))
    plan += [(("idx", b, h), "a") for b in range(1, TB) for h in range(H)]
    for c in range(TB):
        for g in range(2):
            plan += [(("gcb", c, g), "a"), (("qk", c, g), "v"), (("kk", c, g), "v")]
        plan += [(("T", c, 0, g), "a") for g in range(2)]
        for lv in range(1, LEVELS):
            plan += [(("Y", c, lv, g), "v") for g in range(2)]
            plan += [(("Z", c, lv, g), "v") for g in range(2)]
            plan += [(("T", c, lv, g), "a") for g in range(2)]
        for g in range(2):
            plan += [(("nw", c, g), "a")]
        for g in range(2):
            plan += [(("vn", c, g), "v"), (("o", c, g), "a")]
            if c < TB - 1:
                plan += [(("st", c, g), "v")]
    todo = [(b, h) for b in range(TB) for h in range(H)]
    for n in range(len(todo) + 2):
        if n < len(todo):
            plan.append((("s",) + todo[n], "v"))
        if 1 <= n <= len(todo):
            plan.append((("pt",) + todo[n - 1], "a"))
        if n >= 2:
            plan.append((("pv",) + todo[n - 2], "v"))
    plan += [(("ot", k, f), "av"[k]) for k in range(2) for f in range(4)]
    for f in range(KD):
        plan += [(("ga", f), "a"), (("ya", f), "v"), (("gb", f), "a"), (("yb", f), "v")]
    plan += [(("y", t, u), "v") for t in range(TB) for u in range(2)]
    plan += [(("h2", f), "va"[f % 2]) for f in range(KD)]
    plan.append((("router",), "v"))
    return plan


def layer_kernel(nc, x, cond, positions, w_ada, b_ada, mix_pre, mix_post, w_in, conv_w, a_log, dt_bias, gdn_norm,
                 w_bd, w_bg, w_out, ffn_pre, ffn_post, w_rg, b_rg, w_re, b_re, w_eg, w_eu, w_ed, sq_c, col_c, out):
    PLAN = plan_products()
    ORDER = {name: n for n, (name, _) in enumerate(PLAN)}
    TURN, seen = {}, {"v": 0, "a": 0}
    for name, who in PLAN:
        seen[who] += 1
        TURN[name] = (who, seen[who])

    with ExitStack() as ctx:
        def sb(name, shape, dt=F32):
            return ctx.enter_context(nc.sbuf_tensor(name, shape, dt))

        def sem(name):
            return ctx.enter_context(nc.semaphore(name))

        sq = sb("sq", [P, N_SQ, P])
        col = sb("col", [P, N_COL])
        rows = sb("rows", [N_ROWS, P])
        cols = sb("cols", [P, N_ROWS])
        mod = sb("mod", [P, 32])
        modrow = sb("modrow", [1, 2, 512])
        acol = sb("acol", [P, 2, KD])
        ccol = sb("ccol", [P, KD])
        bada = sb("bada", [12, 512])
        ones = sb("ones", [P, P])
        bsel = sb("bsel", [12, 12, P])
        wroute = sb("wroute", [P, KD, 20])
        small_in = sb("small_in", [P, 20 + 64 + 16])
        X = sb("X", [P, TB, D])
        XN = sb("XN", [P, TB, D])
        HT = sb("HT", [P, KD, T])
        QKI = sb("QKI", [P, 12, T])
        KI = sb("KI", [P, T])
        V = sb("V", [P, TB, HW])
        C = sb("C", [P, 12, T])
        SZ = sb("SZ", [P, TB, HW])
        W = sb("W", [P, 3, KD, 512])
        AR = sb("AR", [P, 2, KD, 256])
        g1p = sb("g1p", [P, D])
        g2p = sb("g2p", [P, D])
        IS = sb("IS", [P, 1152])
        IW = sb("IW", [P, 1152])
        sc = sb("sc", [P, 16, 32])
        st = sb("st", [P, 40])
        S = sb("S", [P, 4, DH])
        small = sb("small", [P, TB, 24])

        ps = [ctx.enter_context(nc.psum_tensor(f"ps{n}", [P, 512], F32)) for n in range(BANKS)]

        ident = sq[:, M_ID, :]
        QT, KT, IQ = QKI[:, 0:4, :], QKI[:, 4:8, :], QKI[:, 8:12, :]
        cosT, sinT = SZ[:, 0, :], SZ[:, 1, :]
        ropeT = SZ[:, 2:4, :]
        KTOK = XN[:, 0:2, :].rearrange("p a (b n) -> p (a b) n", n=HW)
        VTOK = XN[:, 2:4, :].rearrange("p a (b n) -> p (a b) n", n=HW)
        Xf = X[:, :, :].rearrange("p a n -> p (a n)")
        ARf = AR[:, :, :, :].rearrange("p a k n -> p (a k n)")
        raw = IS[:, 0:1024].rearrange("p (a n) -> p a n", n=512)
        acc = V

        consts_in, rows_in, x_in, pos_in, bias_in, small_sem = (sem(n) for n in (
            "consts_in", "rows_in", "x_in", "pos_in", "bias_in", "small_sem"))
        post1_in, post2_in = sem("post1_in"), sem("post2_in")
        weights_in = [sem(f"weights_in{n}") for n in range(3)]
        ada_in = [sem(f"ada_in{n}") for n in range(2)]
        product_done, vector_took, scalar_took = sem("product_done"), sem("vector_took"), sem("scalar_took")
        vector_step, scalar_step, pool_step = sem("vector_step"), sem("scalar_step"), sem("pool_step")
        weights_used, ada_used = sem("weights_used"), sem("ada_used")
        names = ("ones_set bsel_set ccol_done ada_summed modrow_set mod_set stats1 rms1 rstd1 xn_done acol_done h_set "
                 "angle_set trig_set raw_set cos_part rope_set v_set small_set conv_raw conv_sum conv_set "
                 "z_set square_set root_set normed tok_set gate_exp gate_e gate_ln gbeta_set gcum_set egc_set beg_set relu_set relu_used scores_set "
                 "diff_set clip_set decay_set eg_set decay_masked qg_set aq_set l_set lm_set x0_set inv_set invt_set y_set "
                 "kd_set nw_set vn_set state_set state_fix o_set g_operands neg_set prob_set pt_set dsa_set gdn_sq gdn_sum gdn_root gdn_r gdn_set "
                 "ot_set sig_set merged_set x_again y_copied y_stat y_root y_set xn2_done h2_set "
                 "route_exp route_set out_done post_norm mse_done mse_root x1_done").split()
        s = {n: sem(n) for n in dict.fromkeys(names)}

        def bank(name):
            return ps[ORDER[name] % BANKS][:, :]

        def product_ready(eng, name):
            eng.wait_ge(product_done, ORDER[name] + 1)

        def took(name, ins):
            who, turn = TURN[name]
            ins.then_inc(vector_took if who == "v" else scalar_took, 1)

        def wcols(c0, n=512):
            return w_in.rearrange("(k p) n -> p k n", p=P)[:, :, c0:c0 + n]

        WBLOCKS = ["q", "k", "v", "iq", "small", "gq", "gk", "gv", "z",
                   "ga0", "gb0", "br0", "ga1", "gb1", "br1", "out0", "out1"]
        WAT = {n: i for i, n in enumerate(WBLOCKS)}
        NW_BLOCKS = len(WBLOCKS)
        WPARTS = {"small": 3, "br0": 2, "br1": 2}
        WREADY = {}
        fill = [0, 0, 0]
        for i, n in enumerate(WBLOCKS):
            fill[i % 3] += 16 * (4 if n == "small" else WPARTS.get(n, 1))
            WREADY[n] = (i % 3, fill[i % 3])
        MOE_READY0 = list(fill)

        def wslot(name):
            return W[:, WAT[name] % 3]

        def weights_ready(eng, name):
            slot, v = WREADY[name]
            eng.wait_ge(weights_in[slot], v)

        Wf = W[:, :, :, :].rearrange("p a k n -> p (a k n)")
        HALF = 3 * KD * 512 // 2
        def expert_gu(slot):
            return Wf[:, slot * HALF:slot * HALF + KD * 512].rearrange("p (u k f) -> p u k f", u=2, k=KD)
        def expert_d(slot):
            return Wf[:, slot * HALF + KD * 512:(slot + 1) * HALF].rearrange("p (k n) -> p k n", k=2)
        expert_in = [sem(f"expert_in{n}") for n in range(2)]
        expert_used = [sem(f"expert_used{n}") for n in range(2)]
        gu_done, silu_done, act_done, down_done, sum_done = (sem(n) for n in (
            "gu_done", "silu_done", "act_done", "down_done", "sum_done"))

        block = ctx.enter_context(nc.Block())

        @block.sync
        def _(sp):
            def ada(n):
                for k in (2 * n, 2 * n + 1):
                    if k >= 2:
                        sp.wait_ge(ada_used, k - 1)
                    sp.dma_start(AR[:, k % 2], w_ada.rearrange("(k p) n -> p k n", p=P)[:, :, 256 * k:256 * k + 256])\
                      .then_inc(ada_in[k % 2], 16)

            def weights(name):
                i = WAT[name]
                if i >= 3:
                    sp.wait_ge(weights_used, i - 2)
                dst, done = wslot(name), weights_in[i % 3]
                if name == "small":
                    for at, c0, n in ((0, C_IK, DH), (DH, C_IK, DH), (2 * DH, C_IW, H), (2 * DH + H, C_B, 2 * H)):
                        sp.dma_start(dst[:, :, at:at + n], wcols(c0, n)).then_inc(done, 16)
                elif name.startswith("br"):
                    u = int(name[2]) * 512
                    for k, w in enumerate((w_bd, w_bg)):
                        sp.dma_start(dst[:, 4 * k:4 * k + 4, :], w.rearrange("(k p) n -> p k n", p=P)[:, :, u:u + 512])\
                          .then_inc(done, 16)
                elif name.startswith("out"):
                    u = int(name[3]) * 512
                    sp.dma_start(dst, w_out.rearrange("(k p) n -> p k n", p=P)[:, :, u:u + 512]).then_inc(done, 16)
                else:
                    at = {"q": C_Q, "k": C_K, "v": C_V, "iq": C_IQ, "gq": C_GQ, "gk": C_GQ + HW, "gv": C_GQ + 2 * HW,
                          "z": C_Z, "ga0": C_GA, "ga1": C_GA + 512, "gb0": C_GB, "gb1": C_GB + 512}[name]
                    sp.dma_start(dst, wcols(at)).then_inc(done, 16)

            sp.dma_start(X[:, 0:2, :], x[0:256, :].rearrange("(t p) d -> p t d", p=P)).then_inc(x_in, 16)
            sp.dma_start(X[:, 2:4, :], x[256:512, :].rearrange("(t p) d -> p t d", p=P)).then_inc(x_in, 16)
            for n in range(4):
                ada(n)
                if n == 1:
                    weights("q")
            for name in ("k", "v"):
                weights(name)
            for before, name in (((), "iq"), ((), "small"), ((), "gq"), ((4, 5), "gk"), ((6, 7), "gv"), ((8, 9), "z")):
                for n in before:
                    ada(n)
                weights(name)
            ada(10)
            ada(11)
            for name in WBLOCKS[WAT["ga0"]:]:
                weights(name)
                if name == "ga1":
                    sp.wait_ge(s["dsa_set"], TB * H)
                    sp.dma_start(X[:, :, :], x.rearrange("(t p) d -> p t d", p=P)).then_inc(s["x_again"], 16)
            sp.wait_ge(weights_used, NW_BLOCKS)
            def expert(e, slot):
                gu, dn = expert_gu(slot), expert_d(slot)
                sp.dma_start(gu[:, 0], w_eg[e].rearrange("(k p) f -> p k f", p=P)).then_inc(expert_in[slot], 16)
                sp.dma_start(gu[:, 1], w_eu[e].rearrange("(k p) f -> p k f", p=P)).then_inc(expert_in[slot], 16)
                sp.dma_start(dn, w_ed[e].rearrange("(k p) n -> p k n", p=P)).then_inc(expert_in[slot], 16)
            for slot in range(2):
                expert(slot, slot)
            eg2, eu2, ed2 = (w.rearrange("(i s) a b -> i s a b", s=2) for w in (w_eg, w_eu, w_ed))
            with sp.Fori(1, NE // 2) as i:
                for slot in range(2):
                    sp.wait_ge(expert_used[slot], i)
                    gu, dn = expert_gu(slot), expert_d(slot)
                    for u, w in enumerate((eg2, eu2)):
                        sp.dma_start(gu[:, u], w[bass.ds(i, 1), slot].rearrange("i (k p) f -> p (i k) f", p=P))\
                          .then_inc(expert_in[slot], 16)
                    sp.dma_start(dn, ed2[bass.ds(i, 1), slot].rearrange("i (k p) n -> p (i k) n", p=P))\
                      .then_inc(expert_in[slot], 16)
            for t in range(TB):
                sp.wait_ge(s["post_norm"], t + 1)
                sp.dma_start(out[t * P:(t + 1) * P, :], XN[:, t, :]).then_inc(s["out_done"], 16)
            sp.wait_ge(s["out_done"], 16 * TB)

        yacc = QKI[:, 0:8, :].rearrange("p (t u) n -> p t (u n)", u=2)
        C_raw = IS[:, 0:2 * 515 + 2]
        def conv_raw(m):
            return IS[:, (m % 2) * 516:(m % 2) * 516 + 515]
        ada_acc = V
        ada_sum = IW[:, 0:1024].rearrange("p (a n) -> p a n", n=512)
        cos_out = AR

        def gspace(g):
            base = Xf[:, g * 2048:(g + 1) * 2048]
            b2 = ARf[:, g * 2048:(g + 1) * 2048]
            b3 = C[:, 8 + 2 * g:10 + 2 * g, :].rearrange("p a n -> p (a n)")
            return {
                "E1": base[:, 0:512], "E2": base[:, 512:1024], "XU": base[:, 1024:1536], "XL": base[:, 1536:2048],
                "D": b2[:, 0:512], "LM": b2[:, 512:1024], "EG": b2[:, 1024:1536],
                "QG": ARf[:, 1536:2048], "NW": ARf[:, 3584:4096],
                "KBG": b3[:, 0:256], "VB": b3[:, 256:512], "KDEC": b3[:, 512:768], "VN": b3[:, 768:1024],
            }
        G = [gspace(g) for g in range(2)]

        def heads(ap, n=4):
            return ap.rearrange("p (h n) -> p h n", h=n)

        def of_group(ap, g):
            return ap.rearrange("p (m k n) -> p m k n", k=2, n=DH)[:, :, g, :]

        def scal(name, c, g):
            return GSC[name][:, 8 * c + g:8 * c + 8:2]

        OG = IQ
        OD = C[:, 0:4, :]
        OAT, OGT = C[:, 4:8, :], C[:, 8:12, :]
        MT = QKI[:, 0:8, :]
        YS = XN
        SM = [Xf[:, n * 512:(n + 1) * 512] for n in range(3)]
        PR = [Xf[:, (3 + n) * 512:(4 + n) * 512] for n in range(2)]
        PT = [Xf[:, (5 + n) * 512:(6 + n) * 512] for n in range(2)]
        AOFF = {1: 0, 2: 256, 3: 640}
        def scores(t, b):
            return t[:, AOFF[b]:AOFF[b] + P * (b + 1)]
        TODO = [(b, h) for b in range(TB) for h in range(H)]

        GSC = {n: sc[:, i, :] for i, n in enumerate(
            "beta g gc egc bgc nbgc t0 t1 t2 t3 osum orr wsc".split())}
        ssq, rstd = st[:, 0:4], st[:, 4:8]
        negm, rsum, rinv, rmax = st[:, 8:12], st[:, 12:16], st[:, 16:20], st[:, 20:24]

        @block.gpsimd
        def _(pool):
            done = [0]

            def link(ins):
                done[0] += 1
                ins.then_inc(pool_step, 1)
                pool.wait_ge(pool_step, done[0])

            pool.memset(ones[:, :], 1.0).then_inc(s["ones_set"], 1)
            pool.wait_ge(consts_in, 32)
            pool.tensor_copy(bsel[:, :, :], sq[0:12, M_ID, 0:12].unsqueeze(2).to_broadcast([12, 12, P]))\
                .then_inc(s["bsel_set"], 1)
            pool.wait_ge(s["trig_set"], 2)
            for n in range(13):
                pool.wait_ge(s["raw_set"], n + 1)
                if n >= 2:
                    pool.wait_ge(s["rope_set"], n - 1)
                pool.tensor_tensor(ropeT[:, n % 2, :], raw[:, n % 2, :], cosT, ALU.mult).then_inc(s["cos_part"], 1)

            for c in range(TB):
                for g in range(2):
                    u = 2 * c + g
                    A = G[g]
                    if u == 0:
                        pool.wait_ge(s["tok_set"], 8)
                        pool.wait_ge(s["beg_set"], 2)
                    if c > 0:
                        pool.wait_ge(s["vn_set"], u - 1)
                        pool.wait_ge(s["nw_set"], u - 1)
                    pool.tensor_tensor(heads(A["KBG"]), of_group(KTOK[:, c, :], g),
                                       scal("nbgc", c, g).unsqueeze(2).to_broadcast([P, 4, DH]), ALU.mult)\
                        .then_inc(s["g_operands"], 1)
                    pool.tensor_tensor(heads(A["VB"]), of_group(VTOK[:, c, :], g),
                                       scal("beta", c, g).unsqueeze(2).to_broadcast([P, 4, DH]), ALU.mult)\
                        .then_inc(s["g_operands"], 1)
                    pool.wait_ge(s["decay_set"], 2 * u + 2)
                    if c > 0:
                        pool.wait_ge(s["state_set"], u - 1) if c < TB else None
                    pool.tensor_tensor(heads(A["KDEC"]), of_group(KTOK[:, c, :], g),
                                       heads(A["E1"])[:, :, P - 1:P].to_broadcast([P, 4, DH]), ALU.mult)\
                        .then_inc(s["kd_set"], 1)
                    pool.wait_ge(s["kd_set"], u + 1)
                    pool.tensor_tensor(heads(A["E1"]), heads(A["E1"]),
                                       sq[:, M_UPPER, :].unsqueeze(1).to_broadcast([P, 4, P]), ALU.mult)\
                        .then_inc(s["decay_masked"], 1)
                    link(pool.tensor_tensor(heads(A["E2"]), heads(A["E2"]),
                                            sq[:, M_LOWER, :].unsqueeze(1).to_broadcast([P, 4, P]), ALU.mult))
                    pool.tensor_tensor(heads(A["E2"]), heads(A["E2"]),
                                       scal("beta", c, g).unsqueeze(2).to_broadcast([P, 4, P]), ALU.mult)\
                        .then_inc(s["decay_masked"], 1)
                for g in range(2):
                    A = G[g]
                    pool.wait_ge(s["l_set"], 2 * c + g + 1)
                    link(pool.tensor_tensor(heads(A["LM"]), heads(A["E2"]),
                                            sq[:, M_LEVEL, :].unsqueeze(1).to_broadcast([P, 4, P]), ALU.mult))
                    pool.tensor_tensor(heads(A["XL"]), ident.unsqueeze(1).to_broadcast([P, 4, P]), heads(A["LM"]),
                                       ALU.subtract).then_inc(s["x0_set"], 1)
                for lv in range(1, LEVELS):
                    for g in range(2):
                        A = G[g]
                        if lv == 1:
                            pool.wait_ge(s["x0_set"], 2 * c + g + 1)
                        else:
                            pool.wait_ge(product_done, ORDER[("Y", c, lv - 1, g)] + 1)
                        pool.tensor_tensor(heads(A["LM"]), heads(A["E2"]),
                                           sq[:, M_LEVEL + lv, :].unsqueeze(1).to_broadcast([P, 4, P]), ALU.mult)\
                            .then_inc(s["lm_set"], 1)

        @block.scalar
        def _(act):
            done = [0]

            def link(ins):
                done[0] += 1
                ins.then_inc(scalar_step, 1)
                act.wait_ge(scalar_step, done[0])

            bc = lambda ap, n: ap.unsqueeze(0).to_broadcast([P, n])
            act.dma_start(rows[R_C:R_C + KD, :], cond.rearrange("(k n) -> k n", n=P)).then_inc(rows_in, 16)
            act.dma_start(rows[R_PRE1:R_PRE1 + KD, :], mix_pre.rearrange("(k n) -> k n", n=P)).then_inc(rows_in, 16)
            act.dma_start(rows[R_PRE2:R_PRE2 + KD, :], ffn_pre.rearrange("(k n) -> k n", n=P)).then_inc(rows_in, 16)
            act.dma_start(rows[R_CONV:N_ROWS, :], conv_w.rearrange("j (m n) -> (j m) n", n=P)).then_inc(rows_in, 16)
            act.dma_start(sq[:, :, :], sq_c.rearrange("p (a n) -> p a n", n=P)).then_inc(consts_in, 16)
            act.dma_start(col[:, :], col_c).then_inc(consts_in, 16)
            act.dma_start(HT[:, 0, :].bitcast(I32), bc(positions, T)).then_inc(pos_in, 16)
            act.dma_start(bada[:, :], b_ada.rearrange("(k n) -> k n", n=512)).then_inc(bias_in, 16)
            act.dma_start(small_in[:, 0:4], bc(b_rg, NG)).then_inc(small_sem, 16)
            act.dma_start(small_in[:, 4:20], bc(b_re, NE)).then_inc(small_sem, 16)
            act.dma_start(small_in[:, 20:84], bc(gdn_norm, DH)).then_inc(small_sem, 16)
            act.dma_start(small_in[:, 84:92], bc(a_log, H)).then_inc(small_sem, 16)
            act.dma_start(small_in[:, 92:100], bc(dt_bias, H)).then_inc(small_sem, 16)
            act.dma_start(wroute[:, :, 0:4], w_rg.rearrange("(k p) n -> p k n", p=P)).then_inc(small_sem, 16)
            act.dma_start(wroute[:, :, 4:20], w_re.rearrange("(k p) n -> p k n", p=P)).then_inc(small_sem, 16)
            act.dma_start(g1p[:, :], bc(mix_post, D)).then_inc(post1_in, 16)
            act.dma_start(g2p[:, :], bc(ffn_post, D)).then_inc(post2_in, 16)

            act.wait_ge(vector_took, TURN[("rows",)][1])
            act.activation(ccol[:, :], cols[:, R_C:R_C + KD], ACT.Silu).then_inc(s["ccol_done"], 1)
            act.wait_ge(x_in, 32)
            for t in range(TB):
                act.activation(XN[:, t, :], X[:, t, :], ACT.Square, accum_out=ssq[:, t:t + 1]).then_inc(s["stats1"], 1)
            act.wait_ge(s["stats1"], TB)
            act.wait_ge(consts_in, 32)
            act.activation(rstd, ssq, ACT.Sqrt, bias=col[:, K_EPS:K_EPS + 1], scale=1.0 / D).then_inc(s["rms1"], 1)
            act.wait_ge(s["rstd1"], 1)
            for t in range(TB):
                act.activation(XN[:, t, :], X[:, t, :], ACT.Copy, scale=rstd[:, t:t + 1]).then_inc(s["xn_done"], 1)
            act.wait_ge(s["angle_set"], 1)
            act.activation(sinT, HT[:, 1, :], ACT.Sin, scale=col[:, K_SIGN:K_SIGN + 1]).then_inc(s["trig_set"], 1)
            act.activation(cosT, HT[:, 2, :], ACT.Sin, scale=-1.0, bias=col[:, K_HALFPI:K_HALFPI + 1])\
                .then_inc(s["trig_set"], 1)

            def mod_row(n, k):
                product_ready(act, ("ada", n))
                if k >= 2:
                    m = [0, 1, 2, 3, 6, 7, 8, 9][k - 2]
                    act.wait_ge(product_done, ORDER[("adac", m)] + 1)
                ins = act.activation(modrow[0:1, k % 2, :], bank(("ada", n))[0:1, :], ACT.Copy)
                took(("ada", n), ins)

            for n in range(4):
                mod_row(n, n)
            act.wait_ge(s["acol_done"], 1)
            for f in range(1, KD, 2):
                name = ("h1", f)
                product_ready(act, name)
                if f < 3:
                    act.wait_ge(s["trig_set"], 2)
                ins = act.activation(HT[:, f, :], bank(name), ACT.Identity, scale=acol[:, 0, f:f + 1],
                                     bias=mod[:, f:f + 1])
                took(name, ins)

            seq = rotated()
            for n, it in enumerate(seq):
                name = ("rope",) + it
                product_ready(act, name)
                if n >= 2:
                    act.wait_ge(product_done, ORDER[("swap",) + seq[n - 2]] + 1)
                    act.wait_ge(s["cos_part"], n - 1)
                ins = act.activation(raw[:, n % 2, :], bank(name), ACT.Copy)
                took(name, ins)
                act.wait_ge(scalar_took, TURN[name][1])
                act.engine_nop().then_inc(s["raw_set"], 1) if False else act.sem_inc(s["raw_set"], 1)
                if it == ("k", 3):
                    for t in range(TB):
                        product_ready(act, ("v", t))
                        took(("v", t), act.activation(V[:, t, :], bank(("v", t)), ACT.Copy))
            def conv_silu(m):
                act.wait_ge(s["conv_sum"], m + 1)
                act.activation(C[:, m, :], C[:, m, :], ACT.Silu).then_inc(s["conv_set"], 1)
            k = 4
            act.wait_ge(s["cos_part"], 13)
            act.wait_ge(product_done, ORDER[("swap", "ik", 0)] + 1)
            for m in range(12):
                product_ready(act, ("conv", m))
                act.wait_ge(s["conv_raw"], 1)
                if m >= 2:
                    act.wait_ge(s["conv_sum"], m - 1)
                took(("conv", m), act.activation(conv_raw(m)[:, 3:515], bank(("conv", m)), ACT.Copy))
                if m >= 1:
                    conv_silu(m - 1)
                if m % 3 == 2:
                    for n in (4 + 2 * (m // 3), 5 + 2 * (m // 3)):
                        if 6 <= n < 10:
                            mod_row(n, k)
                            k += 1
            conv_silu(11)
            for t in range(TB):
                product_ready(act, ("z", t))
                if t == 0:
                    act.wait_ge(s["rope_set"], 13)
                took(("z", t), act.activation(SZ[:, t, :], bank(("z", t)), ACT.Silu))
            act.wait_ge(s["conv_set"], 12)
            act.wait_ge(s["conv_sum"], 12)
            for m in range(9):
                if m < 8:
                    if m >= 2:
                        act.wait_ge(product_done, ORDER[("norm", m - 2)] + 1)
                    act.activation(raw[:, m % 2, :], C[:, m, :], ACT.Square).then_inc(s["square_set"], 1)
                if m >= 1:
                    name = ("norm", m - 1)
                    product_ready(act, name)
                    if m >= 3:
                        act.wait_ge(s["normed"], m - 2)
                    took(name, act.activation(ada_sum[:, (m - 1) % 2, :], bank(name), ACT.Sqrt,
                                              bias=col[:, K_EPS:K_EPS + 1]))
            for t in range(TB):
                product_ready(act, ("ktok", t))
                ins = act.activation(KTOK[:, t, :], bank(("ktok", t)), ACT.Copy)
                took(("ktok", t), ins)
            for t in range(TB):
                product_ready(act, ("vtok", t))
                took(("vtok", t), act.activation(VTOK[:, t, :], bank(("vtok", t)), ACT.Copy))
            act.wait_ge(scalar_took, TURN[("vtok", 3)][1])
            act.sem_inc(s["tok_set"], 8)
            act.wait_ge(s["gate_e"], 1)
            act.activation(GSC["t1"], GSC["t0"], ACT.Exp, scale=-1.0).then_inc(s["gate_exp"], 1)
            act.activation(GSC["beta"], small[:, :, 8:16], ACT.Exp, scale=-1.0).then_inc(s["gate_exp"], 1)
            act.activation(small_in[:, 84:92], small_in[:, 84:92], ACT.Exp).then_inc(s["gate_exp"], 1)
            act.wait_ge(s["gate_exp"], 1)
            act.activation(GSC["t2"], GSC["t1"], ACT.Ln, bias=1.0).then_inc(s["gate_ln"], 1)
            act.wait_ge(s["gcum_set"], 1)
            act.activation(GSC["egc"], GSC["gc"], ACT.Exp).then_inc(s["egc_set"], 1)
            n = 0
            for b in range(1, TB):
                for h in range(H):
                    name = ("idx", b, h)
                    product_ready(act, name)
                    if n >= 2:
                        act.wait_ge(s["relu_used"], n - 1)
                    w = P * (b + 1)
                    took(name, act.activation(Xf[:, (n % 2) * 512:(n % 2) * 512 + w], bank(name)[:, 0:w], ACT.Relu))
                    n += 1
            for c in range(TB):
                for g in range(2):
                    u, A = 2 * c + g, G[g]
                    act.wait_ge(s["clip_set"], 2 * u + 2)
                    if u == 0:
                        act.wait_ge(s["relu_used"], 24)
                    act.activation(A["E1"], A["XU"], ACT.Exp).then_inc(s["decay_set"], 1)
                    act.activation(A["E2"], A["XL"], ACT.Exp, scale=-1.0).then_inc(s["decay_set"], 1)
                    name = ("gcb", c, g)
                    if c > 0:
                        act.wait_ge(s["state_set"], u - 1)
                        act.wait_ge(s["qg_set"], u - 1)
                    took(name, act.activation(A["EG"], bank(name), ACT.Exp))
                for lv in range(LEVELS):
                    for g in range(2):
                        A, name = G[g], ("T", c, lv, g)
                        product_ready(act, name)
                        took(name, act.activation(A["XU"], bank(name), ACT.Copy))
                for g in range(2):
                    A, name = G[g], ("nw", c, g)
                    product_ready(act, name)
                    b = bank(name)
                    rw = slice(64 * g, 64 * g + 64)
                    ins = act.activation(A["NW"][rw, :], b[rw, :], ACT.Copy)
                    took(name, ins)
                    act.wait_ge(scalar_took, TURN[name][1])
                    act.sem_inc(s["nw_set"], 1)
                for g in range(2):
                    name = ("o", c, g)
                    product_ready(act, name)
                    took(name, act.activation(of_group(OG[:, c, :], g), heads(bank(name)[:, 0:256]), ACT.Copy))
            for n in range(len(TODO) + 1):
                if n < len(TODO):
                    b, h = TODO[n]
                    w = P * (b + 1)
                    act.wait_ge(s["neg_set"], n + 1)
                    if n >= 2:
                        product_ready(act, ("pt",) + TODO[n - 2])
                    act.activation(PR[n % 2][:, 0:w], SM[n % 3][:, 0:w], ACT.Exp, scale=DH ** -0.5,
                                   bias=negm[:, n % 4:n % 4 + 1], accum_out=rsum[:, n % 4:n % 4 + 1])\
                        .then_inc(s["prob_set"], 1)
                if n >= 1:
                    b, h = TODO[n - 1]
                    w = P * (b + 1)
                    name = ("pt", b, h)
                    product_ready(act, name)
                    if n >= 3:
                        product_ready(act, ("pv",) + TODO[n - 3])
                    took(name, act.activation(PT[(n - 1) % 2][:, 0:w], bank(name)[:, 0:w], ACT.Copy))
            act.wait_ge(scalar_took, TURN[("o", 3, 1)][1])
            product_ready(act, ("pv",) + TODO[-1])
            act.activation(V[:, :, :], OG, ACT.Square).then_inc(s["gdn_sq"], 1)
            act.wait_ge(s["gdn_sum"], 1)
            act.activation(GSC["orr"], GSC["osum"], ACT.Sqrt, scale=1.0 / DH, bias=col[:, K_EPS:K_EPS + 1])\
                .then_inc(s["gdn_root"], 1)
            for f in range(4):
                product_ready(act, ("ot", 0, f))
                took(("ot", 0, f), act.activation(OAT[:, f, :], bank(("ot", 0, f)), ACT.Copy))
            for f in range(KD):
                for k, nm in enumerate(("ga", "gb")):
                    i = 2 * f + k
                    product_ready(act, (nm, f))
                    if i >= 2:
                        act.wait_ge(s["merged_set"], i - 1)
                    took((nm, f), act.activation(SZ[:, i % 2, :], bank((nm, f)), ACT.Sigmoid))
            for t in range(TB):
                act.wait_ge(s["y_copied"], 2 * t + 2)
                act.activation(SZ[:, 2:4, :].rearrange("p a n -> p (a n)"), YS[:, t, :], ACT.Square,
                               accum_out=ssq[:, t:t + 1]).then_inc(s["y_stat"], 1)
                act.wait_ge(s["y_stat"], t + 1)
            act.activation(rstd, ssq, ACT.Sqrt, bias=col[:, K_EPS:K_EPS + 1], scale=1.0 / D).then_inc(s["y_root"], 1)
            act.wait_ge(s["x1_done"], TB)
            for t in range(TB):
                act.activation(SZ[:, 2:4, :].rearrange("p a n -> p (a n)"), X[:, t, :], ACT.Square,
                               accum_out=ssq[:, t:t + 1]).then_inc(s["mse_done"], 1)
                act.wait_ge(s["mse_done"], t + 1)
            act.activation(rstd, ssq, ACT.Sqrt, bias=col[:, K_EPS:K_EPS + 1], scale=1.0 / D).then_inc(s["mse_root"], 1)
            act.wait_ge(s["xn2_done"], 1)
            for t in range(TB):
                act.activation(XN[:, t, :], X[:, t, :], ACT.Copy, scale=rstd[:, t:t + 1]).then_inc(s["xn_done"], 1)
            for f in range(1, KD, 2):
                name = ("h2", f)
                product_ready(act, name)
                took(name, act.activation(HT[:, f, :], bank(name), ACT.Identity, scale=acol[:, 1, f:f + 1],
                                          bias=mod[:, 16 + f:17 + f]))
            act.wait_ge(s["route_exp"], 1)
            act.activation(GSC["t2"], GSC["t1"], ACT.Exp).then_inc(s["gate_exp"], 1)
            act.wait_ge(s["route_exp"], 2)
            act.activation(GSC["t3"][:, 0:4], GSC["t0"][:, 0:4], ACT.Exp).then_inc(s["gate_exp"], 1)
            with act.Fori(0, NE // 2) as i:
                for slot in range(2):
                    for f in range(2):
                        act.wait_ge(gu_done, i * 8 + (4 * slot + 2 * f + 1))
                        act.wait_ge(act_done, i * 4 + (2 * slot + f + 1))
                        ins = act.activation(SZ[:, f, :], ps[2 * f][:, :], ACT.Silu)
                        ins.then_inc(silu_done, 1)
            act.wait_ge(sum_done, 8 * NE + 4)
            for t in range(TB):
                act.activation(SZ[:, 2:4, :].rearrange("p a n -> p (a n)"), yacc[:, t, :], ACT.Square,
                               accum_out=ssq[:, t:t + 1]).then_inc(s["mse_done"], 1)
                act.wait_ge(s["mse_done"], TB + t + 1)
            act.activation(rstd, ssq, ACT.Sqrt, bias=col[:, K_EPS:K_EPS + 1], scale=1.0 / D).then_inc(s["mse_root"], 1)

        @block.vector
        def _(dve):
            done = [0]

            def link(ins):
                done[0] += 1
                ins.then_inc(vector_step, 1)
                dve.wait_ge(vector_step, done[0])

            def own(name):
                dve.wait_ge(vector_took, TURN[name][1])

            product_ready(dve, ("rows",))
            took(("rows",), dve.tensor_copy(cols[:, :], bank(("rows",))[:, 0:N_ROWS]))
            dve.wait_ge(pos_in, 16)
            dve.wait_ge(consts_in, 32)
            h = [HT[:, n, :] for n in range(5)]
            link(dve.tensor_copy(h[3], h[0].bitcast(I32)))
            link(dve.tensor_scalar(h[3], h[3], col[:, K_FREQ:K_FREQ + 1], None, ALU.mult))
            big = 1.5 * 2.0 ** 23
            link(dve.tensor_scalar(h[4], h[3], 1.0 / (2 * np.pi), big, ALU.mult, ALU.add))
            link(dve.tensor_scalar(h[4], h[4], big, None, ALU.subtract))
            c1 = 6.28125
            c2 = float(np.float32(2 * np.pi - c1).view(np.uint32) & np.uint32(0xFFFFF000)) if False else 0.0019340515136718750
            c3 = 2 * np.pi - c1 - c2
            for k in (c1, c2, c3):
                link(dve.scalar_tensor_tensor(h[3], h[4], -k, h[3], ALU.mult, ALU.add))
            lim = 3.1415925
            link(dve.tensor_scalar(h[1], h[3], lim, -lim, ALU.min, ALU.max))
            dve.scalar_tensor_tensor(h[2], h[1], -1.0, h[1], ALU.mult, ALU.max).then_inc(s["angle_set"], 1)

            def ada_sum_block(n):
                for u in range(2):
                    k = 2 * n + u
                    dve.wait_ge(ada_in[k % 2], 16 * (k // 2 + 1))
                    dst = ada_sum[:, n % 2, 256 * u:256 * u + 256]
                    for j in range(KD):
                        w = AR[:, k % 2, j, :]
                        if j == 0:
                            ins = dve.tensor_scalar(dst, w, ccol[:, 0:1], None, ALU.mult)
                        else:
                            ins = dve.scalar_tensor_tensor(dst, w, ccol[:, j:j + 1], dst, ALU.mult, ALU.add)
                        if j == KD - 1:
                            ins.then_inc(ada_used, 1)
                        else:
                            link(ins)
                dve.wait_ge(ada_used, 2 * n + 2)
                dve.sem_inc(s["ada_summed"], 1)

            def mod_cols(n):
                j = n if n < 4 else n - 2
                product_ready(dve, ("adac", n))
                took(("adac", n), dve.tensor_copy(mod[:, 4 * j:4 * j + 4], bank(("adac", n))[:, 0:4]))

            dve.wait_ge(s["ccol_done"], 1)
            for n in range(4):
                if n >= 2:
                    product_ready(dve, ("ada", n - 2))
                ada_sum_block(n)
                if n == 1:
                    dve.wait_ge(s["rms1"], 1)
                    dve.reciprocal(rstd, rstd).then_inc(s["rstd1"], 1)
                if n >= 1:
                    mod_cols(n - 1)
            mod_cols(3)
            own(("adac", 3))
            dve.scalar_tensor_tensor(acol[:, 0, :], mod[:, 8:16], 1.0, cols[:, R_PRE1:R_PRE1 + KD], ALU.add, ALU.mult)\
                .then_inc(s["acol_done"], 1)
            dve.wait_ge(s["acol_done"], 1)
            dve.wait_ge(s["trig_set"], 2)
            for f in range(0, KD, 2):
                name = ("h1", f)
                product_ready(dve, name)
                took(name, dve.tensor_scalar(HT[:, f, :], bank(name), acol[:, 0, f:f + 1], mod[:, f:f + 1],
                                             ALU.mult, ALU.add))
            dests = [QKI[:, n, :] for n in range(12)] + [KI[:, :]]
            for n, it in enumerate(rotated()):
                name = ("swap",) + it
                product_ready(dve, name)
                ins = dve.tensor_tensor(dests[n], bank(name), sinT, ALU.mult)
                took(name, ins)
                own(name)
                dve.wait_ge(s["cos_part"], n + 1)
                dve.tensor_tensor(dests[n], dests[n], ropeT[:, n % 2, :], ALU.add).then_inc(s["rope_set"], 1)
            product_ready(dve, ("small",))
            took(("small",), dve.tensor_copy(small[:, :, :], bank(("small",))[:, 0:128].rearrange(
                "p (t n) -> p t n", n=32)[:, :, 0:24]))
            dve.wait_ge(s["cos_part"], 13)
            product_ready(dve, ("swap", "ik", 0))
            for m in range(2):
                ins = dve.memset(conv_raw(m)[:, 0:3], 0.0)
                link(ins) if m == 0 else ins.then_inc(s["conv_raw"], 1)
            for m in range(12):
                dve.wait_ge(scalar_took, TURN[("conv", m)][1])
                r = conv_raw(m)
                for j in range(4):
                    w = cols[:, R_CONV + 12 * j + m:R_CONV + 12 * j + m + 1]
                    if j == 0:
                        ins = dve.tensor_scalar(C[:, m, :], r[:, 0:T], w, None, ALU.mult)
                    else:
                        ins = dve.scalar_tensor_tensor(C[:, m, :], r[:, j:j + T], w, C[:, m, :], ALU.mult, ALU.add)
                    link(ins) if j < 3 else ins.then_inc(s["conv_sum"], 1)
                if m % 3 == 0:
                    for n in (4 + 2 * (m // 3), 5 + 2 * (m // 3)):
                        product_ready(dve, ("ada", n - 2))
                        ada_sum_block(n)
                if m % 3 == 2:
                    for n in (4 + 2 * (m // 3), 5 + 2 * (m // 3)):
                        if 6 <= n < 10:
                            mod_cols(n)
                            continue
                        product_ready(dve, ("ada", n))
                        dst = (g1p if n < 6 else g2p)[:, (n % 2) * 512:(n % 2) * 512 + 512]
                        dve.wait_ge(post1_in if n < 6 else post2_in, 16)
                        took(("ada", n), dve.tensor_tensor(dst, bank(("ada", n)), dst, ALU.mult))
            own(("adac", 9))
            link(dve.scalar_tensor_tensor(acol[:, 1, :], mod[:, 24:32], 1.0, cols[:, R_PRE2:R_PRE2 + KD],
                                          ALU.add, ALU.mult))
            for m in range(8):
                name = ("norm", m)
                dve.wait_ge(scalar_took, TURN[name][1])
                r = ada_sum[:, m % 2, :]
                link(dve.reciprocal(r, r))
                dve.scalar_tensor_tensor(C[:, m, :], C[:, m, :], DH ** -0.5 if m < 4 else 1.0, r, ALU.mult, ALU.mult)\
                   .then_inc(s["normed"], 1)
            dve.wait_ge(small_sem, 16 * 7)
            t3 = lambda n: GSC[n].rearrange("p (t h) -> p t h", h=H)
            own(("small",))
            link(dve.tensor_tensor(t3("t3"), small[:, :, 16:24], small_in[:, 92:100].unsqueeze(1).to_broadcast([P, TB, H]),
                                   ALU.add))
            dve.scalar_tensor_tensor(GSC["t0"], GSC["t3"], -1.0, GSC["t3"], ALU.mult, ALU.max).then_inc(s["gate_e"], 1)
            dve.wait_ge(s["gate_exp"], 3)
            link(dve.tensor_scalar(GSC["beta"], GSC["beta"], 1.0, None, ALU.add))
            dve.reciprocal(GSC["beta"], GSC["beta"]).then_inc(s["beg_set"], 1)
            dve.wait_ge(s["gate_ln"], 1)
            link(dve.scalar_tensor_tensor(GSC["t3"], GSC["t3"], 0.0, GSC["t2"], ALU.max, ALU.add))
            dve.scalar_tensor_tensor(t3("g"), t3("t3"), -1.0, small_in[:, 84:92].unsqueeze(1).to_broadcast([P, TB, H]),
                                     ALU.mult, ALU.mult).then_inc(s["gbeta_set"], 1)
            product_ready(dve, ("gc",))
            took(("gc",), dve.tensor_copy(GSC["gc"], bank(("gc",))[:, 0:32]))
            own(("gc",))
            dve.sem_inc(s["gcum_set"], 1)
            dve.wait_ge(s["egc_set"], 1)
            dve.wait_ge(s["beg_set"], 1)
            dve.scalar_tensor_tensor(GSC["nbgc"], GSC["beta"], -1.0, GSC["egc"], ALU.mult, ALU.mult)\
               .then_inc(s["beg_set"], 1)
            link(dve.tensor_scalar(t3("wsc"), small[:, :, 0:8], (H * DH) ** -0.5, None, ALU.mult))
            n = 0
            for b in range(1, TB):
                w = P * (b + 1)
                for h_ in range(H):
                    name = ("idx", b, h_)
                    dve.wait_ge(scalar_took, TURN[name][1])
                    r = Xf[:, (n % 2) * 512:(n % 2) * 512 + w]
                    wt = GSC["wsc"][:, 8 * b + h_:8 * b + h_ + 1]
                    if h_ == 0:
                        ins = dve.tensor_scalar(scores(IS, b), r, wt, None, ALU.mult)
                    else:
                        ins = dve.scalar_tensor_tensor(scores(IS, b), r, wt, scores(IS, b), ALU.mult, ALU.add)
                    ins.then_inc(s["relu_used"], 1)
                    n += 1
                    dve.wait_ge(s["relu_used"], n)
                dia = scores(IS, b)[:, w - P:w]
                link(dve.tensor_tensor(dia, dia, sq[:, M_CAUSAL, :], ALU.add))

            def topk_round(b, r):
                src = scores(IS, b) if r == 0 else scores(IW, b)
                link(dve.max(out=st[:, 24:32], in_=src))
                link(dve.match_replace(out=scores(IW, b), in_to_replace=st[:, 24:32], in_values=src, imm_value=FAR))
                if r == NKEEP // 8 - 1:
                    link(dve.tensor_tensor(scores(IW, b), scores(IW, b), scores(IS, b), ALU.is_equal))
                    link(dve.tensor_scalar(scores(IW, b), scores(IW, b), NEG, None, ALU.mult))
            rounds = [(b, r) for b in range(1, TB) for r in range(NKEEP // 8)]
            dve.wait_ge(s["normed"], 8)

            link(dve.memset(S[:, :, :], 0.0))
            turn = 0
            for c_ in range(TB):
                for g in range(2):
                    u, A = 2 * c_ + g, G[g]
                    name = ("gcb", c_, g)
                    if c_ > 0:
                        dve.wait_ge(s["diff_set"], u)
                    dve.tensor_copy(heads(A["LM"]), scal("g", c_, g).unsqueeze(2).to_broadcast([P, 4, P]))\
                       .then_inc(s["diff_set"], 1)
                    product_ready(dve, name)
                    link(dve.tensor_tensor(heads(A["D"]), heads(bank(name)),
                                           scal("gc", c_, g).unsqueeze(2).to_broadcast([P, 4, P]), ALU.subtract))
                    dve.tensor_scalar(A["XU"], A["D"], 0.0, None, ALU.min).then_inc(s["clip_set"], 1)
                    dve.tensor_scalar(A["XL"], A["D"], 0.0, None, ALU.max).then_inc(s["clip_set"], 1)
                    dve.wait_ge(scalar_took, TURN[name][1])
                    rw = slice(64 * g, 64 * g + 64)
                    dve.tensor_tensor(heads(A["QG"])[rw], C[rw, 0:4, c_ * P:(c_ + 1) * P], heads(A["EG"])[rw], ALU.mult)\
                       .then_inc(s["qg_set"], 1)
                    dve.wait_ge(s["decay_masked"], 2 * u + 2)
                    product_ready(dve, ("qk", c_, g))
                    took(("qk", c_, g), dve.tensor_tensor(A["E1"], bank(("qk", c_, g)), A["E1"], ALU.mult))
                    product_ready(dve, ("kk", c_, g))
                    took(("kk", c_, g), dve.tensor_tensor(A["E2"], bank(("kk", c_, g)), A["E2"], ALU.mult))
                    own(("kk", c_, g))
                    dve.sem_inc(s["l_set"], 1)
                for lv in range(LEVELS):
                    if turn < len(rounds):
                        topk_round(*rounds[turn])
                        turn += 1
                    if turn < len(rounds) and lv % 2 == 0:
                        topk_round(*rounds[turn])
                        turn += 1
                    if lv == 0:
                        continue
                    for g in range(2):
                        name, A = ("Y", c_, lv, g), G[g]
                        product_ready(dve, name)
                        took(name, dve.tensor_copy(A["D"], bank(name)))
                    for g in range(2):
                        name, A = ("Z", c_, lv, g), G[g]
                        product_ready(dve, name)
                        took(name, dve.tensor_tensor(A["XL"], A["XL"], bank(name), ALU.subtract))
                for g in range(2):
                    A, name = G[g], ("vn", c_, g)
                    product_ready(dve, name)
                    took(name, dve.tensor_copy(A["VN"], bank(name)[:, 0:256]))
                    own(name)
                    dve.sem_inc(s["vn_set"], 1)
                    if c_ < TB - 1:
                        name = ("st", c_, g)
                        product_ready(dve, name)
                        bk = bank(name)
                        rw = slice(64 * g, 64 * g + 64)
                        link(dve.tensor_tensor(S[rw], S[rw], heads(A["EG"])[rw, :, P - 1:P].to_broadcast([64, 4, DH]),
                                               ALU.mult))
                        ins = dve.tensor_tensor(S[rw], S[rw], heads(bk[:, 0:256])[rw], ALU.add)
                        took(name, ins)
                        own(name)
                        dve.sem_inc(s["state_set"], 1)
            while turn < len(rounds):
                topk_round(*rounds[turn])
                turn += 1
            def attend(n):
                b, h_ = TODO[n]
                w = P * (b + 1)
                name = ("s", b, h_)
                product_ready(dve, name)
                if n >= 3:
                    dve.wait_ge(s["prob_set"], n - 2)
                mask = sq[:, M_CAUSAL, :] if b == 0 else scores(IW, b)
                ins = dve.tensor_tensor_reduce(SM[n % 3][:, 0:w], bank(name)[:, 0:w], mask, 1.0, FAR, ALU.add, ALU.max,
                                               rmax[:, n % 4:n % 4 + 1])
                took(name, ins)
                own(name)
                dve.tensor_scalar(negm[:, n % 4:n % 4 + 1], rmax[:, n % 4:n % 4 + 1], -DH ** -0.5, None, ALU.mult)\
                   .then_inc(s["neg_set"], 1)
            dve.wait_ge(scalar_took, TURN[("o", 3, 1)][1])
            attend(0)
            for n in range(1, len(TODO) + 2):
                if n < len(TODO):
                    attend(n)
                if n >= 2:
                    m = n - 2
                    b, h_ = TODO[m]
                    dve.wait_ge(s["prob_set"], m + 1)
                    link(dve.reciprocal(rinv[:, m % 4:m % 4 + 1], rsum[:, m % 4:m % 4 + 1]))
                    name = ("pv", b, h_)
                    product_ready(dve, name)
                    took(name, dve.tensor_scalar(OD[:, b, DH * h_:DH * h_ + DH], bank(name)[:, 0:DH],
                                                 rinv[:, m % 4:m % 4 + 1], None, ALU.mult))
                    own(name)
                    dve.sem_inc(s["dsa_set"], 1)
            o4 = OG.rearrange("p t (h n) -> p (t h) n", n=DH)
            dve.wait_ge(s["gdn_sq"], 1)
            dve.tensor_reduce(GSC["osum"], V[:, :, :].rearrange("p t (h n) -> p (t h) n", n=DH), AX.X, ALU.add)\
               .then_inc(s["gdn_sum"], 1)
            dve.wait_ge(s["gdn_root"], 1)
            link(dve.reciprocal(GSC["orr"], GSC["orr"]))
            link(dve.tensor_tensor(o4, o4, GSC["orr"].unsqueeze(2).to_broadcast([P, 32, DH]), ALU.mult))
            link(dve.tensor_tensor(o4, o4, small_in[:, 20:84].unsqueeze(1).to_broadcast([P, 32, DH]), ALU.mult))
            dve.wait_ge(scalar_took, TURN[("z", 3)][1])
            dve.tensor_tensor(OG, OG, SZ[:, :, :], ALU.mult).then_inc(s["gdn_set"], 1)
            for f in range(4):
                product_ready(dve, ("ot", 1, f))
                took(("ot", 1, f), dve.tensor_copy(OGT[:, f, :], bank(("ot", 1, f))))
            for f in range(KD):
                for k, (nm, gt) in enumerate((("ya", "ga"), ("yb", "gb"))):
                    i = 2 * f + k
                    product_ready(dve, (nm, f))
                    dve.wait_ge(scalar_took, TURN[(gt, f)][1])
                    gate = SZ[:, i % 2, :]
                    dst = MT[:, f, :] if k == 0 else gate
                    took((nm, f), dve.tensor_tensor(dst, gate, bank((nm, f)), ALU.mult))
                    if k == 0:
                        own((nm, f))
                        dve.sem_inc(s["merged_set"], 1)
                    else:
                        own((nm, f))
                        dve.tensor_tensor(MT[:, f, :], MT[:, f, :], gate, ALU.add).then_inc(s["merged_set"], 1)
            for t in range(TB):
                for u in range(2):
                    name = ("y", t, u)
                    product_ready(dve, name)
                    took(name, dve.tensor_copy(YS[:, t, 512 * u:512 * u + 512], bank(name)))
                own(("y", t, 1))
                dve.sem_inc(s["y_copied"], 2)
            dve.wait_ge(s["y_root"], 1)
            link(dve.reciprocal(rstd, rstd))
            dve.wait_ge(s["x_again"], 16)
            for t in range(TB):
                link(dve.scalar_tensor_tensor(YS[:, t, :], YS[:, t, :], rstd[:, t:t + 1], g1p[:, :], ALU.mult, ALU.mult))
                dve.tensor_tensor(X[:, t, :], X[:, t, :], YS[:, t, :], ALU.add).then_inc(s["x1_done"], 1)
            dve.wait_ge(s["mse_root"], 1)
            dve.reciprocal(rstd, rstd).then_inc(s["xn2_done"], 1)
            for f in range(0, KD, 2):
                name = ("h2", f)
                product_ready(dve, name)
                took(name, dve.tensor_scalar(HT[:, f, :], bank(name), acol[:, 1, f:f + 1], mod[:, 16 + f:17 + f],
                                             ALU.mult, ALU.add))
            RL = IS[:, 0:80].rearrange("p (t n) -> p t n", n=20)
            R = IS[:, 128:1024].rearrange("p (a t n) -> p a t n", t=TB, n=16)
            def b4(ap):
                return ap.unsqueeze(2).to_broadcast([P, TB, 4])
            tie = col[:, K_TIE:K_TIE + 4].unsqueeze(1).to_broadcast([P, TB, 4])
            sv = lambda n: IW[:, 4 * n:4 * n + 4]
            product_ready(dve, ("router",))
            took(("router",), dve.tensor_tensor(RL, bank(("router",))[:, 0:128].rearrange(
                "p (t n) -> p t n", n=32)[:, :, 0:20], small_in[:, 0:20].unsqueeze(1).to_broadcast([P, TB, 20]), ALU.add))
            own(("router",))

            def one_hot(dst, src, m, top):
                link(dve.tensor_tensor(dst, src, b4(top), ALU.is_equal))
                link(dve.tensor_tensor(dst, dst, tie, ALU.mult))
                link(dve.tensor_reduce(m, dst, AX.X, ALU.max))
                link(dve.tensor_tensor(dst, dst, b4(m), ALU.is_equal))

            gl, el = RL[:, :, 0:4], RL[:, :, 4:20]
            link(dve.tensor_reduce(sv(0), gl, AX.X, ALU.max))
            ghot, ingrp, h1, h2, e2 = (R[:, n, :, 0:4] for n in range(5))
            one_hot(ghot, gl, sv(1), sv(0))
            dve.tensor_tensor(GSC["t1"][:, 0:16].rearrange("p (t n) -> p t n", n=4), gl, b4(sv(0)), ALU.subtract)\
               .then_inc(s["route_exp"], 1)
            t16 = R[:, 5, :, :]
            link(dve.tensor_tensor(t16.rearrange("p t (g e) -> p t g e", e=4), el.rearrange("p t (g e) -> p t g e", e=4),
                                   ghot.unsqueeze(3).to_broadcast([P, TB, 4, 4]), ALU.mult))
            link(dve.tensor_reduce(ingrp, t16.rearrange("p t (g e) -> p t e g", e=4), AX.X, ALU.add))
            link(dve.tensor_reduce(sv(2), ingrp, AX.X, ALU.max))
            one_hot(h1, ingrp, sv(3), sv(2))
            link(dve.scalar_tensor_tensor(e2, h1, NEG, ingrp, ALU.mult, ALU.add))
            link(dve.tensor_reduce(sv(4), e2, AX.X, ALU.max))
            one_hot(h2, e2, sv(5), sv(4))
            dve.tensor_tensor(GSC["t0"][:, 0:4], sv(4), sv(2), ALU.subtract).then_inc(s["route_exp"], 1)
            dve.wait_ge(s["gate_exp"], 5)
            gs = GSC["t2"][:, 0:16].rearrange("p (t n) -> p t n", n=4)
            link(dve.tensor_reduce(sv(6), gs, AX.X, ALU.add))
            link(dve.tensor_scalar(sv(7), GSC["t3"][:, 0:4], 1.0, None, ALU.add))
            link(dve.tensor_tensor(sv(8), sv(6), sv(7), ALU.mult))
            link(dve.reciprocal(sv(8), sv(8)))
            link(dve.tensor_tensor(sv(9), sv(8), GSC["t3"][:, 0:4], ALU.mult))
            link(dve.tensor_tensor(h1, h1, b4(sv(8)), ALU.mult))
            link(dve.tensor_tensor(h2, h2, b4(sv(9)), ALU.mult))
            link(dve.tensor_tensor(h1, h1, h2, ALU.add))
            dg = IW[:, 64:128].rearrange("p (g e t) -> p t g e", g=4, e=4)
            link(dve.tensor_tensor(dg, ghot.unsqueeze(3).to_broadcast([P, TB, 4, 4]),
                                   h1.unsqueeze(2).to_broadcast([P, TB, 4, 4]), ALU.mult))
            link(dve.memset(yacc[:, :, :], 0.0))
            dgates = IW[:, 64:128].rearrange("p (i n) -> p i n", n=8)
            gate_now = st[:, 32:40]
            dve.sem_inc(act_done, 2)
            dve.sem_inc(sum_done, 4)
            with dve.Fori(0, NE // 2) as i:
                dve.tensor_copy(gate_now.unsqueeze(1), dgates[:, bass.ds(i, 1), :]).then_inc(s["route_set"], 1)
                dve.wait_ge(s["route_set"], i + 1)
                for slot in range(2):
                    for f in range(2):
                        dve.wait_ge(gu_done, i * 8 + (4 * slot + 2 * f + 2))
                        dve.wait_ge(silu_done, i * 4 + (2 * slot + f + 1))
                        dve.tensor_tensor(C[:, 2 * slot + f, :], SZ[:, f, :], ps[2 * f + 1][:, :], ALU.mult)\
                           .then_inc(act_done, 1)
                    for t in range(TB):
                        for u in range(2):
                            n = 2 * t + u
                            dve.wait_ge(down_done, i * 16 + (8 * slot + n + 1))
                            y = yacc[:, t, 512 * u:512 * u + 512]
                            dve.scalar_tensor_tensor(y, ps[4 + n % 4][:, :], gate_now[:, 4 * slot + t:4 * slot + t + 1],
                                                     y, ALU.mult, ALU.add).then_inc(sum_done, 1)
                dve.wait_ge(sum_done, i * 16 + 20)
            dve.wait_ge(s["mse_root"], 2)
            link(dve.reciprocal(rstd, rstd))
            for t in range(TB):
                link(dve.scalar_tensor_tensor(yacc[:, t, :], yacc[:, t, :], rstd[:, t:t + 1], g2p[:, :], ALU.mult, ALU.mult))
                dve.tensor_tensor(XN[:, t, :], X[:, t, :], yacc[:, t, :], ALU.add).then_inc(s["post_norm"], 1)

        @block.tensor
        def _(pe):
            at = [0]

            def begin(name):
                n = at[0]
                assert PLAN[n][0] == name, (PLAN[n], name)
                if n >= BANKS:
                    who, turn = TURN[PLAN[n - BANKS][0]]
                    pe.wait_ge(vector_took if who == "v" else scalar_took, turn)
                return ps[n % BANKS]

            def end(ins):
                ins.then_inc(product_done, 1)
                at[0] += 1

            def mm(o, a, b, first=True, last=True):
                return pe.matmul(o, a, b, start=first, stop=last)

            def taken(name):
                who, turn = TURN[name]
                pe.wait_ge(vector_took if who == "v" else scalar_took, turn)

            def four_transposes(name, src):
                b = begin(name)
                for k in range(4):
                    ins = pe.transpose(b[:, k * P:(k + 1) * P], src(k), ident)
                end(ins)

            def ada(n, k):
                b = begin(("ada", n))
                pe.wait_ge(s["ada_summed"], n + 1)
                mm(b[:, :], ones[:, :], ada_sum[:, n % 2, :], True, False)
                end(mm(b[:, :], bsel[:, n, :], bada[:, :], False, True))

            def adac(n, k):
                b = begin(("adac", n))
                taken(("ada", n))
                for j in range(4):
                    ins = mm(b[:, j:j + 1], modrow[0:1, k % 2, j * P:(j + 1) * P], ones[0:1, 0:1])
                end(ins)

            def features(name, w, m):
                b = begin(name)
                for k in range(KD):
                    ins = mm(b[:, :], w[:, k, m * P:(m + 1) * P], HT[:, k, :], k == 0, k == KD - 1)
                end(ins)

            def tokens(name, w, t):
                b = begin(name)
                for k in range(KD):
                    ins = mm(b[:, :], HT[:, k, t * P:(t + 1) * P], w[:, k, :], k == 0, k == KD - 1)
                end(ins)

            def used():
                pe.wait_ge(product_done, at[0])
                pe.sem_inc(weights_used, 1)

            pe.wait_ge(rows_in, 64)
            pe.wait_ge(consts_in, 32)
            b = begin(("rows",))
            end(pe.transpose(b[:, 0:N_ROWS], rows[:, :], sq[0:N_ROWS, M_ID, 0:N_ROWS]))
            pe.wait_ge(s["ones_set"], 1)
            pe.wait_ge(s["bsel_set"], 1)
            pe.wait_ge(bias_in, 16)
            for n in range(4):
                ada(n, n)
                adac(n, n)
            pe.wait_ge(s["xn_done"], TB)
            for f in range(KD):
                four_transposes(("h1", f), lambda t: XN[:, t, f * P:(f + 1) * P])
            taken(("h1", KD - 1))
            taken(("h1", KD - 2))
            seq = rotated()

            def swap(n):
                b = begin(("swap",) + seq[n])
                pe.wait_ge(s["raw_set"], n + 1)
                end(mm(b[:, :], sq[:, M_SWAP, :], raw[:, n % 2, :]))

            for n, it in enumerate(seq):
                kind, m = it
                wname = {"q": "q", "k": "k", "iq": "iq", "ik": "small"}[kind]
                if m == 0:
                    weights_ready(pe, wname)
                features(("rope",) + it, wslot(wname), m)
                if n >= 1:
                    swap(n - 1)
                if m == 3:
                    used()
                if it == ("k", 3):
                    weights_ready(pe, "v")
                    for t in range(TB):
                        tokens(("v", t), wslot("v"), t)
                    used()
            swap(12)
            b = begin(("small",))
            for t in range(TB):
                for k in range(KD):
                    ins = mm(b[:, 32 * t:32 * t + 24], HT[:, k, t * P:(t + 1) * P], wslot("small")[:, k, 128:152],
                             k == 0, k == KD - 1)
            end(ins)
            used()
            k = 4
            for m in range(12):
                wname = ("gq", "gk", "gv")[m // 4]
                if m % 4 == 0:
                    weights_ready(pe, wname)
                features(("conv", m), wslot(wname), m % 4)
                if m % 4 == 3:
                    used()
                if m % 3 == 2:
                    for n in (4 + 2 * (m // 3), 5 + 2 * (m // 3)):
                        ada(n, k)
                        if 6 <= n < 10:
                            adac(n, k)
                            k += 1
            weights_ready(pe, "z")
            for t in range(TB):
                tokens(("z", t), wslot("z"), t)
            used()
            for m in range(8):
                b = begin(("norm", m))
                pe.wait_ge(s["square_set"], m + 1)
                end(mm(b[:, :], sq[:, M_HEADS, :], raw[:, m % 2, :]))
            pe.wait_ge(s["normed"], 8)
            for t in range(TB):
                four_transposes(("ktok", t), lambda m: C[:, 4 + m, t * P:(t + 1) * P])
            for t in range(TB):
                four_transposes(("vtok", t), lambda m: C[:, 8 + m, t * P:(t + 1) * P])
            b = begin(("gc",))
            pe.wait_ge(s["gbeta_set"], 1)
            end(mm(b[:, 0:32], sq[:, M_UPPER, :], GSC["g"]))
            pe.wait_ge(s["rope_set"], 13)
            for qb in range(1, TB):
                for h in range(H):
                    b = begin(("idx", qb, h))
                    rw = slice(64 * (h % 2), 64 * (h % 2) + 64)
                    w = P * (qb + 1)
                    end(mm(b[:, 0:w], IQ[rw, h // 2, qb * P:(qb + 1) * P], KI[rw, 0:w]))
            def four(b, lhs, rhs):
                for hh in range(4):
                    ins = mm(b[:, hh * P:(hh + 1) * P], lhs(hh), rhs(hh))
                return ins

            for c in range(TB):
                tok = slice(c * P, (c + 1) * P)
                for g in range(2):
                    u, A = 2 * c + g, G[g]
                    b = begin(("gcb", c, g))
                    pe.wait_ge(s["diff_set"], u + 1)
                    end(four(b, lambda hh: A["LM"][:, hh * P:(hh + 1) * P], lambda hh: sq[:, M_UPPER, :]))
                    rw = slice(64 * g, 64 * g + 64)
                    b = begin(("qk", c, g))
                    end(four(b, lambda hh: C[rw, 4 + hh, tok], lambda hh: C[rw, hh, tok]))
                    b = begin(("kk", c, g))
                    end(four(b, lambda hh: C[rw, 4 + hh, tok], lambda hh: C[rw, 4 + hh, tok]))
                hp = lambda ap, hh: ap[:, hh * P:(hh + 1) * P]
                for lv in range(LEVELS):
                    if lv > 0:
                        for g in range(2):
                            A = G[g]
                            b = begin(("Y", c, lv, g))
                            pe.wait_ge(s["lm_set"], (2 * c) * (LEVELS - 1) + 2 * (lv - 1) + g + 1)
                            taken(("T", c, lv - 1, g))
                            end(four(b, lambda hh: hp(A["LM"], hh), lambda hh: hp(A["XU"], hh)))
                        for g in range(2):
                            A = G[g]
                            b = begin(("Z", c, lv, g))
                            taken(("Y", c, lv, g))
                            end(four(b, lambda hh: hp(A["D"], hh), lambda hh: hp(A["XL"], hh)))
                    for g in range(2):
                        A = G[g]
                        if lv == 0:
                            pe.wait_ge(s["x0_set"], 2 * c + g + 1)
                        else:
                            taken(("Z", c, lv, g))
                        four_transposes(("T", c, lv, g), lambda hh: hp(A["XL"], hh))
                for g in range(2):
                    A = G[g]
                    b = begin(("nw", c, g))
                    taken(("T", c, LEVELS - 1, g))
                    pe.wait_ge(s["g_operands"], 2 * (2 * c + g) + 2)
                    rw = slice(64 * g, 64 * g + 64)
                    end(four(b[rw, :], lambda hh: A["KBG"][:, hh * DH:(hh + 1) * DH], lambda hh: hp(A["XU"], hh)))
                for g in range(2):
                    u, A = 2 * c + g, G[g]
                    b = begin(("vn", c, g))
                    pe.wait_ge(s["nw_set"], u + 1)
                    if c > 0:
                        pe.wait_ge(s["state_set"], u - 1)
                    for hh in range(4):
                        rw = slice(64 * g, 64 * g + 64)
                        o = b[:, hh * DH:(hh + 1) * DH]
                        mm(o, hp(A["XU"], hh), A["VB"][:, hh * DH:(hh + 1) * DH], True, False)
                        ins = mm(o, heads(A["NW"])[rw, hh, :], S[rw, hh, :], False, True)
                    end(ins)
                    b = begin(("o", c, g))
                    pe.wait_ge(s["vn_set"], u + 1)
                    for hh in range(4):
                        rw = slice(64 * g, 64 * g + 64)
                        o = b[:, hh * DH:(hh + 1) * DH]
                        mm(o, heads(A["QG"])[rw, hh, :], S[rw, hh, :], True, False)
                        ins = mm(o, hp(A["E1"], hh), A["VN"][:, hh * DH:(hh + 1) * DH], False, True)
                    end(ins)
                    if c < TB - 1:
                        b = begin(("st", c, g))
                        pe.wait_ge(s["kd_set"], u + 1)
                        for hh in range(4):
                            hd = slice(hh * DH, (hh + 1) * DH)
                            ins = mm(b[64 * g:64 * g + 64, hd], A["KDEC"][:, hd], A["VN"][:, hd])
                        end(ins)
            for n in range(len(TODO) + 2):
                if n < len(TODO):
                    qb, h = TODO[n]
                    w = P * (qb + 1)
                    rw = slice(64 * (h % 2), 64 * (h % 2) + 64)
                    b = begin(("s", qb, h))
                    end(mm(b[:, 0:w], QT[rw, h // 2, qb * P:(qb + 1) * P], KT[rw, h // 2, 0:w]))
                if 1 <= n <= len(TODO):
                    qb, h = TODO[n - 1]
                    b = begin(("pt", qb, h))
                    pe.wait_ge(s["prob_set"], n)
                    for k in range(qb + 1):
                        ins = pe.transpose(b[:, k * P:(k + 1) * P], PR[(n - 1) % 2][:, k * P:(k + 1) * P], ident)
                    end(ins)
                if n >= 2:
                    qb, h = TODO[n - 2]
                    b = begin(("pv", qb, h))
                    taken(("pt", qb, h))
                    for k in range(qb + 1):
                        ins = mm(b[:, 0:DH], PT[n % 2][:, k * P:(k + 1) * P], V[:, k, h * DH:(h + 1) * DH],
                                 k == 0, k == qb)
                    end(ins)
            pe.wait_ge(s["dsa_set"], len(TODO))
            for f in range(4):
                four_transposes(("ot", 0, f), lambda t: OD[:, t, f * P:(f + 1) * P])
            pe.wait_ge(s["gdn_set"], 1)
            for f in range(4):
                four_transposes(("ot", 1, f), lambda t: OG[:, t, f * P:(f + 1) * P])
            taken(("ot", 0, 3))
            taken(("ot", 1, 3))
            def branch(name, src, w, m):
                b = begin(name)
                for k in range(4):
                    ins = mm(b[:, :], w[:, k, m * P:(m + 1) * P], src[:, k, :], k == 0, k == 3)
                end(ins)

            for f in range(KD):
                half, m = f // 4, f % 4
                if m == 0:
                    for nm in ("ga", "gb", "br"):
                        weights_ready(pe, f"{nm}{half}")
                features(("ga", f), wslot(f"ga{half}"), m)
                branch(("ya", f), OAT, wslot(f"br{half}")[:, 0:4, :], m)
                features(("gb", f), wslot(f"gb{half}"), m)
                branch(("yb", f), OGT, wslot(f"br{half}")[:, 4:8, :], m)
                if m == 3:
                    for _ in range(3):
                        used()
            pe.wait_ge(s["merged_set"], 2 * KD)
            weights_ready(pe, "out0")
            weights_ready(pe, "out1")
            for t in range(TB):
                for u in range(2):
                    b = begin(("y", t, u))
                    for k in range(KD):
                        ins = mm(b[:, :], MT[:, k, t * P:(t + 1) * P], wslot(f"out{u}")[:, k, :], k == 0, k == KD - 1)
                    end(ins)
            used()
            used()
            pe.wait_ge(s["xn_done"], 2 * TB)
            for f in range(KD):
                four_transposes(("h2", f), lambda t: XN[:, t, f * P:(f + 1) * P])
            taken(("h2", KD - 1))
            taken(("h2", KD - 2))
            b = begin(("router",))
            for t in range(TB):
                for k in range(KD):
                    ins = mm(b[:, 32 * t:32 * t + 20], HT[:, k, t * P:(t + 1) * P], wroute[:, k, :], k == 0, k == KD - 1)
            end(ins)
            taken(("router",))
            with pe.Fori(0, NE // 2) as i:
                for slot in range(2):
                    pe.wait_ge(expert_in[slot], i * 48 + 48)
                    gu, dn = expert_gu(slot), expert_d(slot)
                    for f in range(2):
                        for u in range(2):
                            pe.wait_ge(act_done, i * 4 + (2 * slot + f + 1))
                            for k in range(KD):
                                ins = mm(ps[2 * f + u][:, :], gu[:, u, k, f * P:(f + 1) * P], HT[:, k, :],
                                         k == 0, k == KD - 1)
                            ins.then_inc(gu_done, 1)
                    pe.wait_ge(act_done, i * 4 + (2 * slot + 4))
                    for t in range(TB):
                        for u in range(2):
                            n = 2 * t + u
                            pe.wait_ge(sum_done, i * 16 + (8 * slot + n + 1))
                            for k in range(2):
                                ins = mm(ps[4 + n % 4][:, :], C[:, 2 * slot + k, t * P:(t + 1) * P],
                                         dn[:, k, 512 * u:512 * u + 512], k == 0, k == 1)
                            ins.then_inc(down_done, 1)
                    pe.wait_ge(down_done, i * 16 + (8 * slot + 8))
                    pe.sem_inc(expert_used[slot], 1)


_INS = ['x', 'c', 'positions', 'w_ada', 'b_ada', 'mix_norm_pre', 'mix_norm_post', 'w_in', 'conv_w', 'a_log', 'dt_bias',
        'gdn_norm', 'w_branch_dsa', 'w_branch_gdn', 'w_out', 'ffn_norm_pre', 'ffn_norm_post', 'w_router_group',
        'b_router_group', 'w_router_expert', 'b_router_expert', 'w_expert_gate', 'w_expert_up', 'w_expert_down']


def kernel(**inputs):
    import numpy as _np
    import concourse.bacc as _bacc
    from concourse import mybir as _mybir
    from concourse.bass_utils import run_bass_kernel_spmd as _run

    nc = _bacc.Bacc("TRN2", target_bir_lowering=False, num_devices=1, dynamic_dma_scratch_size=1024)
    arrays, args = {}, []
    for name in _INS:
        a = _np.ascontiguousarray(_np.asarray(inputs[name])[0])
        arrays[f"in_{name}"] = a
        args.append(nc.dram_tensor(f"in_{name}", a.shape, _mybir.dt.from_np(a.dtype), kind="ExternalInput").ap())
    for name, a in zip(("squares", "columns"), constants()):
        arrays[name] = a
        args.append(nc.dram_tensor(name, a.shape, _mybir.dt.float32, kind="ExternalInput").ap())
    out = nc.dram_tensor("out", (T, D), _mybir.dt.float32, kind="ExternalOutput").ap()
    layer_kernel(nc, *args, out)
    r = _run(nc, [arrays], core_ids=[0])
    return r.results[0]["out"].reshape(1, T, D)
```

```python
from contextlib import ExitStack

import numpy as np
import concourse.bass as bass
from concourse import mybir
from concourse.alu_op_type import AluOpType as ALU

F32 = mybir.dt.float32
I32 = mybir.dt.int32
ACT = mybir.ActivationFunctionType
AX = mybir.AxisListType

P = 128
D, T = 1024, 512
KD, TB = D // P, T // P
H, DH = 8, 64
HW = H * DH
NKEEP = 128
NEG = -1e30
FAR = -3e38
EPS = 1e-6
NE, DE, NG, EG = 16, 256, 4, 4
BANKS = 8
TILES = 2 * T // P + NE - 1
LEVELS = 7

C_Q, C_K, C_V, C_IQ = 0, HW, 2 * HW, 3 * HW
C_IK = 4 * HW
C_IW = C_IK + DH
C_GQ = C_IW + H
C_Z = C_GQ + 3 * HW
C_B = C_Z + HW
C_GA = C_B + 2 * H
C_GB = C_GA + D

(M_ID, M_UPPER, M_HEADS, M_CAUSAL, M_LOWER, M_SWAP, M_LEVEL) = range(7)
N_SQ = M_LEVEL + LEVELS
(K_FREQ, K_SIGN, K_HALFPI, K_EPS, K_ONE, K_TIE) = range(6)
K_TOKEN = K_TIE + 4
K_ROW = K_TOKEN + TB
N_COL = K_ROW + 32
(R_C, R_PRE1, R_PRE2, R_CONV) = (0, KD, 2 * KD, 3 * KD)
N_ROWS = R_CONV + 4 * 12


def constants():
    i = np.arange(P)
    sq = np.zeros((P, N_SQ, P), np.float32)
    sq[:, M_ID] = np.eye(P)
    sq[:, M_UPPER] = i[:, None] <= i[None, :]
    sq[:, M_HEADS] = i[:, None] // DH == i[None, :] // DH
    sq[:, M_CAUSAL] = np.where(i[None, :] <= i[:, None], 0, NEG)
    sq[:, M_LOWER] = i[:, None] > i[None, :]
    sq[:, M_SWAP] = (i[:, None] ^ (DH // 2)) == i[None, :]
    for k in range(LEVELS):
        b = 1 << k
        same = i[:, None] // (2 * b) == i[None, :] // (2 * b)
        sq[:, M_LEVEL + k] = same & (i[:, None] % (2 * b) >= b) & (i[None, :] % (2 * b) < b)
    col = np.zeros((P, N_COL), np.float32)
    half = DH // 2
    freq = np.float32(10000.0) ** (-np.arange(0, DH, 2, dtype=np.float32) / np.float32(DH))
    col[:, K_FREQ] = freq[i % half]
    col[:, K_SIGN] = np.where(i % DH < half, -1, 1)
    col[:, K_HALFPI] = np.pi / 2
    col[:, K_EPS] = EPS
    col[:, K_ONE] = 1
    col[:, K_TIE:K_TIE + 4] = [4, 3, 2, 1]
    col[:, K_TOKEN:K_TOKEN + TB] = i[:, None] + P * np.arange(TB)
    col[:, K_ROW:] = np.arange(32)
    return sq.reshape(P, N_SQ * P), col


def rotated():
    return [("q", m) for m in range(4)] + [("k", m) for m in range(4)] + [("iq", m) for m in range(4)] + [("ik", 0)]


def attention(n, kind):
    m = n - {"s": 0, "pt": 1, "pv": 2}[kind]
    return [(kind, m // H, m % H)] if 0 <= m < TB * H else []


def plan_products():
    plan = [(("rows",), "v")]
    for n in range(5):
        if n < 4:
            plan.append((("ada", n), "v"))
        if n >= 1:
            plan.append((("adac", n - 1), "v"))
    plan += [(("h1", f), "va"[f % 2]) for f in range(KD)]
    seq = rotated()
    for n, it in enumerate(seq):
        plan.append((("rope",) + it, "a"))
        if n >= 1:
            plan.append((("swap",) + seq[n - 1], "v"))
        if it == ("k", 3):
            plan += [(("v", t), "a") for t in range(TB)]
    plan.append((("swap",) + seq[-1], "v"))
    plan.append((("small",), "v"))
    for m in range(12):
        plan.append((("conv", m), "a"))
        if m % 3 == 2:
            for n in (4 + 2 * (m // 3), 5 + 2 * (m // 3)):
                col = 6 <= n < 10
                plan.append((("ada", n), "a" if col else "v"))
                if col:
                    plan.append((("adac", n), "v"))
    plan += [(("z", t), "a") for t in range(TB)]
    for n in range(3 * H):
        plan.append((("idx", 1 + n // H, n % H), "a"))
        if n % 3 == 2:
            plan.append((("norm", n // 3), "a"))
    plan += [(("ktok", t), "a") for t in range(TB)] + [(("vtok", t), "a") for t in range(TB)]
    plan.append((("gc",), "v"))
    for c in range(TB):
        for g in range(2):
            plan += [(("gcb", c, g), "a"), (("qk", c, g), "v"), (("kk", c, g), "v")]
        for lv in range(LEVELS):
            n = c * LEVELS + lv
            if lv > 0:
                plan += [(("Y", c, lv, g), "a") for g in range(2)]
            plan += [(name, "v") for name in attention(n, "s")]
            if lv > 0:
                plan += [(("Z", c, lv, g), "v") for g in range(2)]
            plan += [(name, "a") for name in attention(n, "pt")]
            plan += [(name, "v") for name in attention(n, "pv")]
            plan += [(("T", c, lv, g), "a") for g in range(2)]
        for g in range(2):
            plan += [(("nw", c, g), "a")]
        for g in range(2):
            plan += [(("vn", c, g), "v"), (("o", c, g), "a")]
            if c < TB - 1:
                plan += [(("st", c, g), "v")]
    for n in range(TB * LEVELS, TB * H + 2):
        plan += [(name, "v") for name in attention(n, "s")]
        plan += [(name, "a") for name in attention(n, "pt")]
        plan += [(name, "v") for name in attention(n, "pv")]
    plan += [(("ot", k, f), "av"[k]) for k in range(2) for f in range(4)]
    for f in range(KD):
        plan += [(("ga", f), "a"), (("ya", f), "v"), (("gb", f), "a"), (("yb", f), "v")]
    plan += [(("y", t, u), "v") for t in range(TB) for u in range(2)]
    plan += [(("h2", f), "va"[f % 2]) for f in range(KD)]
    plan += [(("router",), "v"), (("rank",), "v")]
    return plan


def layer_kernel(nc, x, cond, positions, w_ada, b_ada, mix_pre, mix_post, w_in, conv_w, a_log, dt_bias, gdn_norm,
                 w_bd, w_bg, w_out, ffn_pre, ffn_post, w_rg, b_rg, w_re, b_re, w_eg, w_eu, w_ed, sq_c, col_c, out):
    PLAN = plan_products()
    ORDER = {name: n for n, (name, _) in enumerate(PLAN)}
    TURN, seen = {}, {"v": 0, "a": 0}
    for name, who in PLAN:
        seen[who] += 1
        TURN[name] = (who, seen[who])

    with ExitStack() as ctx:
        def sb(name, shape, dt=F32):
            return ctx.enter_context(nc.sbuf_tensor(name, shape, dt))

        def sem(name):
            return ctx.enter_context(nc.semaphore(name))

        sq = sb("sq", [P, N_SQ, P])
        col = sb("col", [P, N_COL])
        rows = sb("rows", [N_ROWS, P])
        cols = sb("cols", [P, N_ROWS])
        mod = sb("mod", [P, 32])
        modrow = sb("modrow", [1, 2, 512])
        acol = sb("acol", [P, 2, KD])
        ccol = sb("ccol", [P, KD])
        bada = sb("bada", [12, 512])
        ones = sb("ones", [P, P])
        wroute = sb("wroute", [P, KD, 20])
        small_in = sb("small_in", [P, 20 + 64 + 16])
        X = sb("X", [P, TB, D])
        XN = sb("XN", [P, TB, D])
        HT = sb("HT", [P, KD, T])
        QKI = sb("QKI", [P, 12, T])
        KI = sb("KI", [P, T])
        V = sb("V", [P, TB, HW])
        C = sb("C", [P, 12, T])
        SZ = sb("SZ", [P, TB, HW])
        W = sb("W", [P, 3, KD, 512])
        AR = sb("AR", [P, 2, KD, 256])
        g1p = sb("g1p", [P, D])
        g2p = sb("g2p", [P, D])
        IS = sb("IS", [P, 1152])
        IW = sb("IW", [P, 1152])
        sc = sb("sc", [P, 16, 32])
        st = sb("st", [P, 40])
        S = sb("S", [P, 4, DH])
        small = sb("small", [P, TB, 24])

        ps = [ctx.enter_context(nc.psum_tensor(f"ps{n}", [P, 512], F32)) for n in range(BANKS)]

        ident = sq[:, M_ID, :]
        QT, KT, IQ = QKI[:, 0:4, :], QKI[:, 4:8, :], QKI[:, 8:12, :]
        cosT, sinT = SZ[:, 0, :], SZ[:, 1, :]
        ropeT = SZ[:, 2:4, :]
        KTOK = XN[:, 0:2, :].rearrange("p a (b n) -> p (a b) n", n=HW)
        VTOK = XN[:, 2:4, :].rearrange("p a (b n) -> p (a b) n", n=HW)
        Xf = X[:, :, :].rearrange("p a n -> p (a n)")
        ARf = AR[:, :, :, :].rearrange("p a k n -> p (a k n)")
        raw = IS[:, 0:1024].rearrange("p (a n) -> p a n", n=512)
        acc = V

        consts_in, rows_in, x_in, pos_in, bias_in, small_sem = (sem(n) for n in (
            "consts_in", "rows_in", "x_in", "pos_in", "bias_in", "small_sem"))
        post1_in, post2_in = sem("post1_in"), sem("post2_in")
        weights_in = [sem(f"weights_in{n}") for n in range(3)]
        ada_in = [sem(f"ada_in{n}") for n in range(2)]
        product_done, vector_took, scalar_took = sem("product_done"), sem("vector_took"), sem("scalar_took")
        vector_step, scalar_step, pool_step = sem("vector_step"), sem("scalar_step"), sem("pool_step")
        weights_used, ada_used = sem("weights_used"), sem("ada_used")
        names = ("ones_set  ccol_done ada_summed modrow_set mod_set stats1 rms1 rstd1 xn_done acol_done h_set "
                 "angle_set trig_set raw_set cos_part rope_set v_set small_set conv_raw conv_sum conv_set "
                 "z_set square_set root_set normed tok_set gate_exp gate_e gate_ln gbeta_set gcum_set egc_set beg_set relu_set relu_used scores_set "
                 "diff_set clip_set decay_set eg_set decay_masked qg_set aq_set l_set lm_set x0_set inv_set invt_set y_set "
                 "kd_set nw_set vn_set state_set state_fix o_set g_operands neg_set prob_set pt_set dsa_set gdn_sq gdn_sum gdn_root gdn_r gdn_set "
                 "ot_set sig_set merged_set x_again y_copied y_stat y_root y_set xn2_done h2_set "
                 "route_exp route_set out_done post_norm mse_done mse_root x1_done y_sum").split()
        s = {n: sem(n) for n in dict.fromkeys(names)}

        def bank(name):
            return ps[ORDER[name] % BANKS][:, :]

        def product_ready(eng, name):
            eng.wait_ge(product_done, ORDER[name] + 1)

        def took(name, ins):
            who, turn = TURN[name]
            ins.then_inc(vector_took if who == "v" else scalar_took, 1)

        def wcols(c0, n=512):
            return w_in.rearrange("(k p) n -> p k n", p=P)[:, :, c0:c0 + n]

        WBLOCKS = ["q", "k", "v", "iq", "small", "gq", "gk", "gv", "z",
                   "ga0", "gb0", "br0", "ga1", "gb1", "br1", "out0", "out1"]
        WAT = {n: i for i, n in enumerate(WBLOCKS)}
        NW_BLOCKS = len(WBLOCKS)
        WPARTS = {"small": 3, "br0": 2, "br1": 2}
        WREADY = {}
        fill = [0, 0, 0]
        for i, n in enumerate(WBLOCKS):
            fill[i % 3] += 16 * (4 if n == "small" else WPARTS.get(n, 1))
            WREADY[n] = (i % 3, fill[i % 3])
        MOE_READY0 = list(fill)

        def wslot(name):
            return W[:, WAT[name] % 3]

        def weights_ready(eng, name):
            slot, v = WREADY[name]
            eng.wait_ge(weights_in[slot], v)

        Wf = W[:, :, :, :].rearrange("p a k n -> p (a k n)")
        HALF = 3 * KD * 512 // 2
        def expert_gu(slot):
            return Wf[:, slot * HALF:slot * HALF + KD * 512].rearrange("p (k u f) -> p k u f", u=2, k=KD)
        def expert_d(slot):
            return Wf[:, slot * HALF + KD * 512:(slot + 1) * HALF].rearrange("p (k n) -> p k n", k=2)
        tile_stored = [sem(f"tile_stored{n}") for n in range(2)]
        gate_up_in = [sem(f"gate_up_in{n}") for n in range(2)]
        down_in = [sem(f"down_in{n}") for n in range(2)]
        rows_gathered = [sem(f"rows_gathered{n}") for n in range(2)]
        (turned, h_scalar, h_vector, gu_done, silu_done, act_done, act_turned, act_back, down_done, out_scalar,
         out_vector, table_zero, zeros_set, rows_stored, address_set, scattered, order_in, experts_set,
         ) = (sem(n) for n in (
            "turned h_scalar h_vector gu_done silu_done act_done act_turned act_back down_done out_scalar "
            "out_vector table_zero zeros_set rows_stored address_set scattered order_in experts_set").split())
        both_in = [sem(f"both_in{t}") for t in range(TB)]

        xs_d = nc.dram_tensor("xs_rows", (T, D), F32, kind="Internal").ap()
        place_d = nc.dram_tensor("place_token", (P * TILES, 1), I32, kind="Internal").ap()
        yd = nc.dram_tensor("place_rows", (P * TILES, D), F32, kind="Internal").ap()

        def wait_from(eng, what, value):
            if not isinstance(value, int) or value > 0:
                eng.wait_ge(what, value)

        def steps(eng, step):
            for j in range(3):
                step(j, j % 2)
            pairs = (TILES - 5) // 2
            with eng.Fori(0, pairs) as i:
                for k in range(2):
                    step(i * 2 + (3 + k), (3 + k) % 2)
            for j in range(3 + 2 * pairs, TILES):
                step(j, j % 2)

        Y1 = QKI[:, 0:8, :].rearrange("p (t u) n -> p t (u n)", u=2)
        Y2 = Wf[:, 0:TB * D].rearrange("p (t n) -> p t n", n=D)
        GX = V[:, :, :].rearrange("p (s u) n -> p s (u n)", s=2)
        HX = [C[:, 2 * n:2 * n + 2, :].rearrange("p a (k n) -> p (a k) n", n=P) for n in range(2)]
        YT = [C[:, 4 + 2 * n:6 + 2 * n, :].rearrange("p a n -> p (a n)") for n in range(2)]
        SI = [C[:, 8, 256 * n:256 * n + 256] for n in range(2)]
        AC = [C[:, 9, 256 * n:256 * n + 256] for n in range(2)]
        ACT_T = [C[:, 10, 256 * n:256 * n + 256] for n in range(2)]
        eid = sb("eid", [P, 32], I32)
        address = sb("address", [P, 2 * TB], I32)
        token = sb("token", [P, TB], I32)
        order = sb("order", [P, TILES], I32)
        C_raw = IS[:, 0:2 * 515 + 2]
        def conv_raw(m):
            return IS[:, (m % 2) * 516:(m % 2) * 516 + 515]
        ada_acc = V
        ada_sum = IW[:, 0:1024].rearrange("p (a n) -> p a n", n=512)
        cos_out = AR

        def gspace(g):
            base = Xf[:, g * 2048:(g + 1) * 2048]
            b2 = ARf[:, g * 2048:(g + 1) * 2048]
            b3 = C[:, 8 + 2 * g:10 + 2 * g, :].rearrange("p a n -> p (a n)")
            return {
                "E1": base[:, 0:512], "E2": base[:, 512:1024], "XU": base[:, 1024:1536], "XL": base[:, 1536:2048],
                "D": b2[:, 0:512], "LM": b2[:, 512:1024], "EG": b2[:, 1024:1536],
                "QG": ARf[:, 1536:2048], "NW": ARf[:, 3584:4096],
                "KBG": b3[:, 0:256], "VB": b3[:, 256:512], "KDEC": b3[:, 512:768], "VN": b3[:, 768:1024],
            }
        G = [gspace(g) for g in range(2)]

        def heads(ap, n=4):
            return ap.rearrange("p (h n) -> p h n", h=n)

        def of_group(ap, g):
            return ap.rearrange("p (m k n) -> p m k n", k=2, n=DH)[:, :, g, :]

        def scal(name, c, g):
            return GSC[name][:, 8 * c + g:8 * c + 8:2]

        OG = IQ
        OD = W[:, 2, 0:4, :]
        OAT, OGT = C[:, 4:8, :], C[:, 8:12, :]
        MT = QKI[:, 0:8, :]
        YS = XN
        Wa = W[:, 1].rearrange("p k n -> p (k n)")
        SM = [Wa[:, n * 512:(n + 1) * 512] for n in range(3)]
        PR = [Wa[:, (3 + n) * 512:(4 + n) * 512] for n in range(2)]
        PT = [Wa[:, (5 + n) * 512:(6 + n) * 512] for n in range(2)]
        AOFF = {1: 0, 2: 256, 3: 640}
        def scores(t, b):
            return t[:, AOFF[b]:AOFF[b] + P * (b + 1)]
        TODO = [(b, h) for b in range(TB) for h in range(H)]

        GSC = {n: sc[:, i, :] for i, n in enumerate(
            "beta g gc egc bgc nbgc t0 t1 t2 t3 osum orr wsc".split())}
        ssq, rstd = st[:, 0:4], st[:, 4:8]
        negm, rsum, rinv, rmax = st[:, 8:12], st[:, 12:16], st[:, 16:20], st[:, 20:24]

        block = ctx.enter_context(nc.Block())

        @block.sync
        def _(sp):
            def ada(n):
                for k in (2 * n, 2 * n + 1):
                    if k >= 2:
                        sp.wait_ge(ada_used, k - 1)
                    sp.dma_start(AR[:, k % 2], w_ada.rearrange("(k p) n -> p k n", p=P)[:, :, 256 * k:256 * k + 256])\
                      .then_inc(ada_in[k % 2], 16)

            def weights(name):
                i = WAT[name]
                if i >= 3:
                    sp.wait_ge(weights_used, i - 2)
                dst, done = wslot(name), weights_in[i % 3]
                if name == "small":
                    for at, c0, n in ((0, C_IK, DH), (DH, C_IK, DH), (2 * DH, C_IW, H), (2 * DH + H, C_B, 2 * H)):
                        sp.dma_start(dst[:, :, at:at + n], wcols(c0, n)).then_inc(done, 16)
                elif name.startswith("br"):
                    u = int(name[2]) * 512
                    for k, w in enumerate((w_bd, w_bg)):
                        sp.dma_start(dst[:, 4 * k:4 * k + 4, :], w.rearrange("(k p) n -> p k n", p=P)[:, :, u:u + 512])\
                          .then_inc(done, 16)
                elif name.startswith("out"):
                    u = int(name[3]) * 512
                    sp.dma_start(dst, w_out.rearrange("(k p) n -> p k n", p=P)[:, :, u:u + 512]).then_inc(done, 16)
                else:
                    at = {"q": C_Q, "k": C_K, "v": C_V, "iq": C_IQ, "gq": C_GQ, "gk": C_GQ + HW, "gv": C_GQ + 2 * HW,
                          "z": C_Z, "ga0": C_GA, "ga1": C_GA + 512, "gb0": C_GB, "gb1": C_GB + 512}[name]
                    sp.dma_start(dst, wcols(at)).then_inc(done, 16)

            sp.dma_start(rows[R_C:R_C + KD, :], cond.rearrange("(k n) -> k n", n=P)).then_inc(rows_in, 16)
            sp.dma_start(rows[R_PRE1:R_PRE1 + KD, :], mix_pre.rearrange("(k n) -> k n", n=P)).then_inc(rows_in, 16)
            sp.dma_start(rows[R_PRE2:R_PRE2 + KD, :], ffn_pre.rearrange("(k n) -> k n", n=P)).then_inc(rows_in, 16)
            sp.dma_start(rows[R_CONV:N_ROWS, :], conv_w.rearrange("j (m n) -> (j m) n", n=P)).then_inc(rows_in, 16)
            sp.dma_start(sq[:, :, :], sq_c.rearrange("p (a n) -> p a n", n=P)).then_inc(consts_in, 16)
            sp.dma_start(col[:, :], col_c).then_inc(consts_in, 16)
            ada(0)
            sp.dma_start(X[:, 0:2, :], x[0:256, :].rearrange("(t p) d -> p t d", p=P)).then_inc(x_in, 16)
            ada(1)
            sp.dma_start(X[:, 2:4, :], x[256:512, :].rearrange("(t p) d -> p t d", p=P)).then_inc(x_in, 16)
            for n in range(2, 4):
                ada(n)
            for name in ("q", "k", "v"):
                weights(name)
            for before, name in (((), "iq"), ((), "small"), ((), "gq"), ((4, 5), "gk"), ((6, 7), "gv"), ((8, 9), "z")):
                for n in before:
                    ada(n)
                weights(name)
            ada(10)
            ada(11)
            for name in WBLOCKS[WAT["ga0"]:]:
                weights(name)
                if name == "ga0":
                    sp.wait_ge(product_done, ORDER[("ot", 0, 3)] + 1)
                if name == "ga1":
                    sp.wait_ge(s["dsa_set"], TB * H)
                    sp.dma_start(X[:, :, :], x.rearrange("(t p) d -> p t d", p=P)).then_inc(s["x_again"], 16)
            sp.wait_ge(s["xn_done"], 2 * TB)
            sp.dma_start(xs_d.rearrange("(t p) d -> p t d", p=P), XN[:, :, :]).then_inc(rows_stored, 16)
            sp.wait_ge(weights_used, NW_BLOCKS)
            sp.wait_ge(experts_set, 1)
            def expert_of(j):
                at = slice(j, j + 1) if isinstance(j, int) else bass.ds(j, 1)
                return sp.value_load(eid[0:1, at], min_val=0, max_val=NE - 1)

            def load_gate_up(j, slot):
                e = expert_of(j)
                wait_from(sp, gu_done, j - 1)
                for u, w in enumerate((w_eg, w_eu)):
                    sp.dma_start(expert_gu(slot)[:, :, u, :], w[bass.ds(e, 1)].rearrange("i (k p) f -> p (i k) f", p=P))\
                      .then_inc(gate_up_in[slot], 16)

            def load_down(j, slot):
                e = expert_of(j)
                wait_from(sp, down_done, j - 1)
                sp.dma_start(expert_d(slot), w_ed[bass.ds(e, 1)].rearrange("i (k p) n -> p (i k) n", p=P))\
                  .then_inc(down_in[slot], 16)

            def expert(j, slot):
                load_gate_up(j, slot)
                if not isinstance(j, int) or j >= 1:
                    load_down(j - 1, 1 - slot)
            steps(sp, expert)
            load_down(TILES - 1, (TILES - 1) % 2)
            for t in range(TB):
                sp.wait_ge(s["post_norm"], t + 1)
                sp.dma_start(out[t * P:(t + 1) * P, :], XN[:, t, :]).then_inc(s["out_done"], 16)
            sp.wait_ge(s["out_done"], 16 * TB)

        @block.gpsimd
        def _(pool):
            done = [0]

            def link(ins):
                done[0] += 1
                ins.then_inc(pool_step, 1)
                pool.wait_ge(pool_step, done[0])

            pool.memset(ones[:, :], 1.0).then_inc(s["ones_set"], 1)
            pool.wait_ge(consts_in, 32)
            pool.wait_ge(s["trig_set"], 2)
            for n in range(13):
                pool.wait_ge(s["raw_set"], n + 1)
                if n >= 2:
                    pool.wait_ge(s["rope_set"], n - 1)
                pool.tensor_tensor(ropeT[:, n % 2, :], raw[:, n % 2, :], cosT, ALU.mult).then_inc(s["cos_part"], 1)

            for c in range(TB):
                for g in range(2):
                    u = 2 * c + g
                    A = G[g]
                    if u == 0:
                        pool.wait_ge(s["tok_set"], 8)
                        pool.wait_ge(s["beg_set"], 2)
                    if c > 0:
                        pool.wait_ge(s["vn_set"], u - 1)
                        pool.wait_ge(s["nw_set"], u - 1)
                    pool.tensor_tensor(heads(A["KBG"]), of_group(KTOK[:, c, :], g),
                                       scal("nbgc", c, g).unsqueeze(2).to_broadcast([P, 4, DH]), ALU.mult)\
                        .then_inc(s["g_operands"], 1)
                    pool.tensor_tensor(heads(A["VB"]), of_group(VTOK[:, c, :], g),
                                       scal("beta", c, g).unsqueeze(2).to_broadcast([P, 4, DH]), ALU.mult)\
                        .then_inc(s["g_operands"], 1)
                    pool.wait_ge(s["decay_set"], 2 * u + 2)
                    if c > 0:
                        pool.wait_ge(s["state_set"], u - 1) if c < TB else None
                    pool.tensor_tensor(heads(A["KDEC"]), of_group(KTOK[:, c, :], g),
                                       heads(A["E1"])[:, :, P - 1:P].to_broadcast([P, 4, DH]), ALU.mult)\
                        .then_inc(s["kd_set"], 1)
                    pool.wait_ge(s["kd_set"], u + 1)
                    pool.tensor_tensor(heads(A["E1"]), heads(A["E1"]),
                                       sq[:, M_UPPER, :].unsqueeze(1).to_broadcast([P, 4, P]), ALU.mult)\
                        .then_inc(s["decay_masked"], 1)
                    link(pool.tensor_tensor(heads(A["E2"]), heads(A["E2"]),
                                            sq[:, M_LOWER, :].unsqueeze(1).to_broadcast([P, 4, P]), ALU.mult))
                    pool.tensor_tensor(heads(A["E2"]), heads(A["E2"]),
                                       scal("beta", c, g).unsqueeze(2).to_broadcast([P, 4, P]), ALU.mult)\
                        .then_inc(s["decay_masked"], 1)
                for g in range(2):
                    A = G[g]
                    pool.wait_ge(s["l_set"], 2 * c + g + 1)
                    link(pool.tensor_tensor(heads(A["LM"]), heads(A["E2"]),
                                            sq[:, M_LEVEL, :].unsqueeze(1).to_broadcast([P, 4, P]), ALU.mult))
                    pool.tensor_tensor(heads(A["XL"]), ident.unsqueeze(1).to_broadcast([P, 4, P]), heads(A["LM"]),
                                       ALU.subtract).then_inc(s["x0_set"], 1)
                for lv in range(1, LEVELS):
                    for g in range(2):
                        A = G[g]
                        if lv == 1:
                            pool.wait_ge(s["x0_set"], 2 * c + g + 1)
                        else:
                            pool.wait_ge(product_done, ORDER[("Y", c, lv - 1, g)] + 1)
                        pool.tensor_tensor(heads(A["LM"]), heads(A["E2"]),
                                           sq[:, M_LEVEL + lv, :].unsqueeze(1).to_broadcast([P, 4, P]), ALU.mult)\
                            .then_inc(s["lm_set"], 1)

            pool.memset(order[:, :], 0).then_inc(zeros_set, 1)
            pool.wait_ge(zeros_set, 1)
            pool.dma_start(place_d.rearrange("(p j) o -> p (j o)", p=P), order[:, :]).then_inc(table_zero, 16)
            pool.wait_ge(table_zero, 16)
            pool.wait_ge(address_set, 2)
            for k in range(2 * TB):
                pool.indirect_dma_start(place_d, bass.IndirectOffsetOnAxis(address[:, k:k + 1], 0),
                                        token[:, k % TB:k % TB + 1], None).then_inc(scattered, 16)
            pool.wait_ge(scattered, 16 * 2 * TB)
            pool.dma_start(order[:, :], place_d.rearrange("(p j) o -> p (j o)", p=P)).then_inc(order_in, 16)
            pool.wait_ge(order_in, 16)
            pool.wait_ge(rows_stored, 16)
            for j in range(TILES + 2):
                if j < TILES:
                    wait_from(pool, turned, j - 1)
                    pool.indirect_dma_start(GX[:, j % 2, :], None, xs_d,
                                            bass.IndirectOffsetOnAxis(order[:, j:j + 1], 0))\
                        .then_inc(rows_gathered[j % 2], 16)
                if j >= 2:
                    k = j - 2
                    pool.wait_ge(out_scalar, k + 1)
                    pool.wait_ge(out_vector, k + 1)
                    pool.dma_start(yd.rearrange("(p j) d -> j p d", j=TILES)[k], YT[k % 2]).then_inc(tile_stored[k % 2], 16)
            pool.wait_ge(tile_stored[0], 16 * ((TILES + 1) // 2))
            pool.wait_ge(tile_stored[1], 16 * (TILES // 2))
            for t in range(TB):
                for k, dst in enumerate((Y1, Y2)):
                    n = k * TB + t
                    pool.indirect_dma_start(dst[:, t, :], None, yd,
                                            bass.IndirectOffsetOnAxis(address[:, n:n + 1], 0)).then_inc(both_in[t], 16)

        @block.scalar
        def _(act):
            done = [0]

            def link(ins):
                done[0] += 1
                ins.then_inc(scalar_step, 1)
                act.wait_ge(scalar_step, done[0])

            bc = lambda ap, n: ap.unsqueeze(0).to_broadcast([P, n])
            act.dma_start(HT[:, 0, :].bitcast(I32), bc(positions, T)).then_inc(pos_in, 16)
            act.dma_start(bada[:, :], b_ada.rearrange("(k n) -> k n", n=512)).then_inc(bias_in, 16)
            act.dma_start(small_in[:, 0:4], bc(b_rg, NG)).then_inc(small_sem, 16)
            act.dma_start(small_in[:, 4:20], bc(b_re, NE)).then_inc(small_sem, 16)
            act.dma_start(small_in[:, 20:84], bc(gdn_norm, DH)).then_inc(small_sem, 16)
            act.dma_start(small_in[:, 84:92], bc(a_log, H)).then_inc(small_sem, 16)
            act.dma_start(small_in[:, 92:100], bc(dt_bias, H)).then_inc(small_sem, 16)
            act.dma_start(wroute[:, :, 0:4], w_rg.rearrange("(k p) n -> p k n", p=P)).then_inc(small_sem, 16)
            act.dma_start(wroute[:, :, 4:20], w_re.rearrange("(k p) n -> p k n", p=P)).then_inc(small_sem, 16)

            act.wait_ge(vector_took, TURN[("rows",)][1])
            act.activation(ccol[:, :], cols[:, R_C:R_C + KD], ACT.Silu).then_inc(s["ccol_done"], 1)
            act.wait_ge(x_in, 32)
            for t in range(TB):
                act.activation(XN[:, t, :], X[:, t, :], ACT.Square, accum_out=ssq[:, t:t + 1]).then_inc(s["stats1"], 1)
            act.wait_ge(s["stats1"], TB)
            act.wait_ge(consts_in, 32)
            act.activation(rstd, ssq, ACT.Sqrt, bias=col[:, K_EPS:K_EPS + 1], scale=1.0 / D).then_inc(s["rms1"], 1)
            act.wait_ge(s["rstd1"], 1)
            for t in range(TB):
                act.activation(XN[:, t, :], X[:, t, :], ACT.Copy, scale=rstd[:, t:t + 1]).then_inc(s["xn_done"], 1)
            act.dma_start(g1p[:, :], bc(mix_post, D)).then_inc(post1_in, 16)
            act.dma_start(g2p[:, :], bc(ffn_post, D)).then_inc(post2_in, 16)
            act.wait_ge(s["angle_set"], 1)
            act.activation(sinT, HT[:, 1, :], ACT.Sin, scale=col[:, K_SIGN:K_SIGN + 1]).then_inc(s["trig_set"], 1)
            act.activation(cosT, HT[:, 2, :], ACT.Sin, scale=-1.0, bias=col[:, K_HALFPI:K_HALFPI + 1])\
                .then_inc(s["trig_set"], 1)

            def mod_row(n, k):
                product_ready(act, ("ada", n))
                if k >= 2:
                    m = [0, 1, 2, 3, 6, 7, 8, 9][k - 2]
                    act.wait_ge(product_done, ORDER[("adac", m)] + 1)
                ins = act.activation(modrow[0:1, k % 2, :], bank(("ada", n))[0:1, :], ACT.Copy)
                took(("ada", n), ins)

            act.wait_ge(s["acol_done"], 1)
            for f in range(1, KD, 2):
                name = ("h1", f)
                product_ready(act, name)
                if f < 3:
                    act.wait_ge(s["trig_set"], 2)
                ins = act.activation(HT[:, f, :], bank(name), ACT.Identity, scale=acol[:, 0, f:f + 1],
                                     bias=mod[:, f:f + 1])
                took(name, ins)

            seq = rotated()
            for n, it in enumerate(seq):
                name = ("rope",) + it
                product_ready(act, name)
                if n >= 2:
                    act.wait_ge(product_done, ORDER[("swap",) + seq[n - 2]] + 1)
                    act.wait_ge(s["cos_part"], n - 1)
                ins = act.activation(raw[:, n % 2, :], bank(name), ACT.Copy)
                took(name, ins)
                act.wait_ge(scalar_took, TURN[name][1])
                act.engine_nop().then_inc(s["raw_set"], 1) if False else act.sem_inc(s["raw_set"], 1)
                if it == ("k", 3):
                    for t in range(TB):
                        product_ready(act, ("v", t))
                        took(("v", t), act.activation(V[:, t, :], bank(("v", t)), ACT.Copy))
            def conv_silu(m):
                act.wait_ge(s["conv_sum"], m + 1)
                act.activation(C[:, m, :], C[:, m, :], ACT.Silu).then_inc(s["conv_set"], 1)
            k = 4
            act.wait_ge(s["cos_part"], 13)
            act.wait_ge(product_done, ORDER[("swap", "ik", 0)] + 1)
            for m in range(12):
                product_ready(act, ("conv", m))
                act.wait_ge(s["conv_raw"], 1)
                if m >= 2:
                    act.wait_ge(s["conv_sum"], m - 1)
                took(("conv", m), act.activation(conv_raw(m)[:, 3:515], bank(("conv", m)), ACT.Copy))
                if m >= 1:
                    conv_silu(m - 1)
                if m % 3 == 2:
                    for n in (4 + 2 * (m // 3), 5 + 2 * (m // 3)):
                        if 6 <= n < 10:
                            mod_row(n, k)
                            k += 1
            conv_silu(11)
            for t in range(TB):
                product_ready(act, ("z", t))
                if t == 0:
                    act.wait_ge(s["rope_set"], 13)
                took(("z", t), act.activation(SZ[:, t, :], bank(("z", t)), ACT.Silu))
            act.wait_ge(s["conv_set"], 12)
            for n in range(3 * H):
                qb, h = 1 + n // H, n % H
                if n % 3 == 0:
                    m = n // 3
                    if m >= 2:
                        product_ready(act, ("norm", m - 2))
                    act.activation(Xf[:, 1024 + (m % 2) * 512:1536 + (m % 2) * 512], C[:, m, :], ACT.Square)\
                        .then_inc(s["square_set"], 1)
                name = ("idx", qb, h)
                product_ready(act, name)
                if n >= 2:
                    act.wait_ge(s["relu_used"], n - 1)
                w = P * (qb + 1)
                took(name, act.activation(Xf[:, (n % 2) * 512:(n % 2) * 512 + w], bank(name)[:, 0:w], ACT.Relu))
                if n % 3 == 2:
                    m = n // 3
                    name = ("norm", m)
                    product_ready(act, name)
                    if m >= 2:
                        act.wait_ge(s["normed"], m - 1)
                    took(name, act.activation(Xf[:, 2048 + (m % 2) * 512:2560 + (m % 2) * 512], bank(name), ACT.Sqrt,
                                              bias=col[:, K_EPS:K_EPS + 1]))
            for t in range(TB):
                product_ready(act, ("ktok", t))
                ins = act.activation(KTOK[:, t, :], bank(("ktok", t)), ACT.Copy)
                took(("ktok", t), ins)
            for t in range(TB):
                product_ready(act, ("vtok", t))
                took(("vtok", t), act.activation(VTOK[:, t, :], bank(("vtok", t)), ACT.Copy))
            act.wait_ge(scalar_took, TURN[("vtok", 3)][1])
            act.sem_inc(s["tok_set"], 8)
            act.wait_ge(s["gate_e"], 1)
            act.activation(GSC["t1"], GSC["t0"], ACT.Exp, scale=-1.0).then_inc(s["gate_exp"], 1)
            act.activation(GSC["beta"], small[:, :, 8:16], ACT.Exp, scale=-1.0).then_inc(s["gate_exp"], 1)
            act.activation(small_in[:, 84:92], small_in[:, 84:92], ACT.Exp).then_inc(s["gate_exp"], 1)
            act.wait_ge(s["gate_exp"], 1)
            act.activation(GSC["t2"], GSC["t1"], ACT.Ln, bias=1.0).then_inc(s["gate_ln"], 1)
            act.wait_ge(s["gcum_set"], 1)
            act.activation(GSC["egc"], GSC["gc"], ACT.Exp).then_inc(s["egc_set"], 1)
            def attend(n):
                for kind, b, h in attention(n, "s"):
                    w = P * (b + 1)
                    act.wait_ge(s["neg_set"], n + 1)
                    if n >= 2:
                        product_ready(act, attention(n - 1, "pt")[0])
                    act.activation(PR[n % 2][:, 0:w], SM[n % 3][:, 0:w], ACT.Exp, scale=DH ** -0.5,
                                   bias=negm[:, n % 4:n % 4 + 1], accum_out=rsum[:, n % 4:n % 4 + 1])\
                        .then_inc(s["prob_set"], 1)
                for name in attention(n, "pt"):
                    w = P * (name[1] + 1)
                    product_ready(act, name)
                    if n >= 3:
                        product_ready(act, attention(n - 1, "pv")[0])
                    took(name, act.activation(PT[(n - 1) % 2][:, 0:w], bank(name)[:, 0:w], ACT.Copy))

            for c in range(TB):
                for g in range(2):
                    u, A = 2 * c + g, G[g]
                    act.wait_ge(s["clip_set"], 2 * u + 2)
                    if u == 0:
                        act.wait_ge(s["relu_used"], 24)
                    act.activation(A["E1"], A["XU"], ACT.Exp).then_inc(s["decay_set"], 1)
                    act.activation(A["E2"], A["XL"], ACT.Exp, scale=-1.0).then_inc(s["decay_set"], 1)
                    name = ("gcb", c, g)
                    if c > 0:
                        act.wait_ge(s["state_set"], u - 1)
                        act.wait_ge(s["qg_set"], u - 1)
                    took(name, act.activation(A["EG"], bank(name), ACT.Exp))
                for lv in range(LEVELS):
                    if lv > 0:
                        for g in range(2):
                            A, name = G[g], ("Y", c, lv, g)
                            product_ready(act, name)
                            took(name, act.activation(A["D"], bank(name), ACT.Copy))
                    attend(c * LEVELS + lv)
                    for g in range(2):
                        A, name = G[g], ("T", c, lv, g)
                        product_ready(act, name)
                        took(name, act.activation(A["XU"], bank(name), ACT.Copy))
                for g in range(2):
                    A, name = G[g], ("nw", c, g)
                    product_ready(act, name)
                    b = bank(name)
                    rw = slice(64 * g, 64 * g + 64)
                    ins = act.activation(A["NW"][rw, :], b[rw, :], ACT.Copy)
                    took(name, ins)
                    act.wait_ge(scalar_took, TURN[name][1])
                    act.sem_inc(s["nw_set"], 1)
                for g in range(2):
                    name = ("o", c, g)
                    product_ready(act, name)
                    took(name, act.activation(of_group(OG[:, c, :], g), heads(bank(name)[:, 0:256]), ACT.Copy))
            for n in range(TB * LEVELS, TB * H + 2):
                attend(n)
            act.wait_ge(scalar_took, TURN[("o", 3, 1)][1])
            product_ready(act, ("pv",) + TODO[-1])
            act.activation(V[:, :, :], OG, ACT.Square).then_inc(s["gdn_sq"], 1)
            act.wait_ge(s["gdn_sum"], 1)
            act.activation(GSC["orr"], GSC["osum"], ACT.Sqrt, scale=1.0 / DH, bias=col[:, K_EPS:K_EPS + 1])\
                .then_inc(s["gdn_root"], 1)
            for f in range(4):
                product_ready(act, ("ot", 0, f))
                took(("ot", 0, f), act.activation(OAT[:, f, :], bank(("ot", 0, f)), ACT.Copy))
            for f in range(KD):
                for k, nm in enumerate(("ga", "gb")):
                    i = 2 * f + k
                    product_ready(act, (nm, f))
                    if i >= 2:
                        act.wait_ge(s["merged_set"], i - 1)
                    took((nm, f), act.activation(SZ[:, i % 2, :], bank((nm, f)), ACT.Sigmoid))
            scratch = SZ[:, 2:4, :].rearrange("p a n -> p (a n)")
            for t in range(TB):
                act.wait_ge(s["y_copied"], t + 1)
                act.activation(scratch, YS[:, t, :], ACT.Square, accum_out=ssq[:, t:t + 1]).then_inc(s["y_stat"], 1)
                act.wait_ge(s["y_stat"], 2 * t + 1)
                act.activation(rstd[:, t:t + 1], ssq[:, t:t + 1], ACT.Sqrt, bias=col[:, K_EPS:K_EPS + 1], scale=1.0 / D)\
                   .then_inc(s["y_root"], 1)
                act.wait_ge(s["x1_done"], t + 1)
                act.activation(scratch, X[:, t, :], ACT.Square, accum_out=ssq[:, t:t + 1]).then_inc(s["y_stat"], 1)
                act.wait_ge(s["y_stat"], 2 * t + 2)
                act.activation(rstd[:, t:t + 1], ssq[:, t:t + 1], ACT.Sqrt, bias=col[:, K_EPS:K_EPS + 1], scale=1.0 / D)\
                   .then_inc(s["mse_root"], 1)
                act.wait_ge(s["xn2_done"], t + 1)
                act.activation(XN[:, t, :], X[:, t, :], ACT.Copy, scale=rstd[:, t:t + 1]).then_inc(s["xn_done"], 1)
            for f in range(1, KD, 2):
                name = ("h2", f)
                product_ready(act, name)
                took(name, act.activation(HT[:, f, :], bank(name), ACT.Identity, scale=acol[:, 1, f:f + 1],
                                          bias=mod[:, 16 + f:17 + f]))
            act.wait_ge(s["route_exp"], 1)
            act.activation(GSC["t2"], GSC["t1"], ACT.Exp).then_inc(s["gate_exp"], 1)
            act.wait_ge(s["route_exp"], 2)
            act.activation(GSC["t3"][:, 0:4], GSC["t0"][:, 0:4], ACT.Exp).then_inc(s["gate_exp"], 1)
            def evacuate_h(j, slot):
                act.wait_ge(turned, j + 1)
                wait_from(act, gu_done, j - 1)
                for k in range(4):
                    ins = act.activation(HX[slot][:, k, :], ps[0][:, k * P:(k + 1) * P], ACT.Identity,
                                         scale=acol[:, 1, k:k + 1], bias=mod[:, 16 + k:17 + k])
                ins.then_inc(h_scalar, 1)

            def act_back_step(j, slot):
                act.wait_ge(act_turned, j + 1)
                wait_from(act, down_done, j - 1)
                act.activation(ACT_T[slot], ps[4][:, 0:256], ACT.Copy).then_inc(act_back, 1)

            def evacuate_out(j, slot):
                act.wait_ge(down_done, j + 1)
                wait_from(act, tile_stored[slot], 16 * (j // 2) if isinstance(j, int) else (j - slot) * 8)
                act.activation(YT[slot][:, 0:512], ps[5][:, :], ACT.Copy).then_inc(out_scalar, 1)

            def step(j, slot):
                act.wait_ge(gu_done, j + 1)
                wait_from(act, act_done, j - 1)
                act.activation(SI[slot], ps[2 + slot][:, 0:256], ACT.Silu).then_inc(silu_done, 1)
                if not isinstance(j, int) or j >= 1:
                    act_back_step(j - 1, 1 - slot)
                if not isinstance(j, int) or j < TILES - 1:
                    evacuate_h(j + 1, 1 - slot)
                if not isinstance(j, int) or j >= 1:
                    evacuate_out(j - 1, 1 - slot)
            evacuate_h(0, 0)
            steps(act, step)
            act_back_step(TILES - 1, (TILES - 1) % 2)
            evacuate_out(TILES - 1, (TILES - 1) % 2)
            for t in range(TB):
                act.wait_ge(s["y_sum"], t + 1)
                act.activation(scratch, Y1[:, t, :], ACT.Square, accum_out=ssq[:, t:t + 1]).then_inc(s["mse_done"], 1)
                act.wait_ge(s["mse_done"], t + 1)
                act.activation(rstd[:, t:t + 1], ssq[:, t:t + 1], ACT.Sqrt, bias=col[:, K_EPS:K_EPS + 1], scale=1.0 / D)\
                   .then_inc(s["mse_root"], 1)

        @block.vector
        def _(dve):
            done = [0]

            def link(ins):
                done[0] += 1
                ins.then_inc(vector_step, 1)
                dve.wait_ge(vector_step, done[0])

            def own(name):
                dve.wait_ge(vector_took, TURN[name][1])

            product_ready(dve, ("rows",))
            took(("rows",), dve.tensor_copy(cols[:, :], bank(("rows",))[:, 0:N_ROWS]))
            dve.wait_ge(pos_in, 16)
            dve.wait_ge(consts_in, 32)
            h = [HT[:, n, :] for n in range(5)]
            link(dve.tensor_copy(h[3], h[0].bitcast(I32)))
            link(dve.tensor_scalar(h[3], h[3], col[:, K_FREQ:K_FREQ + 1], None, ALU.mult))
            big = 1.5 * 2.0 ** 23
            link(dve.tensor_scalar(h[4], h[3], 1.0 / (2 * np.pi), big, ALU.mult, ALU.add))
            link(dve.tensor_scalar(h[4], h[4], big, None, ALU.subtract))
            c1 = 6.28125
            c2 = float(np.float32(2 * np.pi - c1).view(np.uint32) & np.uint32(0xFFFFF000)) if False else 0.0019340515136718750
            c3 = 2 * np.pi - c1 - c2
            for k in (c1, c2, c3):
                link(dve.scalar_tensor_tensor(h[3], h[4], -k, h[3], ALU.mult, ALU.add))
            lim = 3.1415925
            link(dve.tensor_scalar(h[1], h[3], lim, -lim, ALU.min, ALU.max))
            dve.scalar_tensor_tensor(h[2], h[1], -1.0, h[1], ALU.mult, ALU.max).then_inc(s["angle_set"], 1)

            def ada_sum_block(n):
                for u in range(2):
                    k = 2 * n + u
                    dve.wait_ge(ada_in[k % 2], 16 * (k // 2 + 1))
                    dst = ada_sum[:, n % 2, 256 * u:256 * u + 256]
                    for j in range(KD):
                        w = AR[:, k % 2, j, :]
                        if j == 0:
                            ins = dve.tensor_scalar(dst, w, ccol[:, 0:1], None, ALU.mult)
                        else:
                            ins = dve.scalar_tensor_tensor(dst, w, ccol[:, j:j + 1], dst, ALU.mult, ALU.add)
                        if j == KD - 1:
                            ins.then_inc(ada_used, 1)
                        else:
                            link(ins)
                dve.wait_ge(ada_used, 2 * n + 2)
                dve.sem_inc(s["ada_summed"], 1)

            def mod_cols(n):
                j = n if n < 4 else n - 2
                product_ready(dve, ("adac", n))
                took(("adac", n), dve.tensor_copy(mod[:, 4 * j:4 * j + 4], bank(("adac", n))[:, 0:4]))

            for n in range(5):
                if n < 4:
                    product_ready(dve, ("ada", n))
                    if n >= 2:
                        dve.wait_ge(product_done, ORDER[("adac", n - 2)] + 1)
                    took(("ada", n), dve.tensor_copy(modrow[0:1, n % 2, :], bank(("ada", n))[0:1, :]))
                if n >= 1:
                    mod_cols(n - 1)
                if n == 1:
                    dve.wait_ge(s["rms1"], 1)
                    dve.reciprocal(rstd, rstd).then_inc(s["rstd1"], 1)
            own(("adac", 3))
            dve.scalar_tensor_tensor(acol[:, 0, :], mod[:, 8:16], 1.0, cols[:, R_PRE1:R_PRE1 + KD], ALU.add, ALU.mult)\
                .then_inc(s["acol_done"], 1)
            dve.wait_ge(s["acol_done"], 1)
            dve.wait_ge(s["trig_set"], 2)
            for f in range(0, KD, 2):
                name = ("h1", f)
                product_ready(dve, name)
                took(name, dve.tensor_scalar(HT[:, f, :], bank(name), acol[:, 0, f:f + 1], mod[:, f:f + 1],
                                             ALU.mult, ALU.add))
            dests = [QKI[:, n, :] for n in range(12)] + [KI[:, :]]
            for n, it in enumerate(rotated()):
                name = ("swap",) + it
                product_ready(dve, name)
                ins = dve.tensor_tensor(dests[n], bank(name), sinT, ALU.mult)
                took(name, ins)
                own(name)
                dve.wait_ge(s["cos_part"], n + 1)
                dve.tensor_tensor(dests[n], dests[n], ropeT[:, n % 2, :], ALU.add).then_inc(s["rope_set"], 1)
            product_ready(dve, ("small",))
            took(("small",), dve.tensor_copy(small[:, :, :], bank(("small",))[:, 0:128].rearrange(
                "p (t n) -> p t n", n=32)[:, :, 0:24]))
            dve.wait_ge(s["cos_part"], 13)
            product_ready(dve, ("swap", "ik", 0))
            for m in range(2):
                ins = dve.memset(conv_raw(m)[:, 0:3], 0.0)
                link(ins) if m == 0 else ins.then_inc(s["conv_raw"], 1)
            for m in range(12):
                dve.wait_ge(scalar_took, TURN[("conv", m)][1])
                r = conv_raw(m)
                for j in range(4):
                    w = cols[:, R_CONV + 12 * j + m:R_CONV + 12 * j + m + 1]
                    if j == 0:
                        ins = dve.tensor_scalar(C[:, m, :], r[:, 0:T], w, None, ALU.mult)
                    else:
                        ins = dve.scalar_tensor_tensor(C[:, m, :], r[:, j:j + T], w, C[:, m, :], ALU.mult, ALU.add)
                    link(ins) if j < 3 else ins.then_inc(s["conv_sum"], 1)
                if m % 3 == 0:
                    for n in (4 + 2 * (m // 3), 5 + 2 * (m // 3)):
                        product_ready(dve, ("ada", n - 2))
                        ada_sum_block(n)
                if m % 3 == 2:
                    for n in (4 + 2 * (m // 3), 5 + 2 * (m // 3)):
                        if 6 <= n < 10:
                            mod_cols(n)
                            continue
                        product_ready(dve, ("ada", n))
                        dst = (g1p if n < 6 else g2p)[:, (n % 2) * 512:(n % 2) * 512 + 512]
                        dve.wait_ge(post1_in if n < 6 else post2_in, 16)
                        took(("ada", n), dve.tensor_tensor(dst, bank(("ada", n)), dst, ALU.mult))
            own(("adac", 9))
            link(dve.scalar_tensor_tensor(acol[:, 1, :], mod[:, 24:32], 1.0, cols[:, R_PRE2:R_PRE2 + KD],
                                          ALU.add, ALU.mult))
            t3 = lambda n: GSC[n].rearrange("p (t h) -> p t h", h=H)
            own(("small",))
            link(dve.tensor_scalar(t3("wsc"), small[:, :, 0:8], (H * DH) ** -0.5, None, ALU.mult))
            for n in range(3 * H):
                b, h_ = 1 + n // H, n % H
                w = P * (b + 1)
                name = ("idx", b, h_)
                dve.wait_ge(scalar_took, TURN[name][1])
                r = Xf[:, (n % 2) * 512:(n % 2) * 512 + w]
                wt = GSC["wsc"][:, 8 * b + h_:8 * b + h_ + 1]
                if h_ == 0:
                    ins = dve.tensor_scalar(scores(IS, b), r, wt, None, ALU.mult)
                else:
                    dve.wait_ge(s["relu_used"], n)
                    ins = dve.scalar_tensor_tensor(scores(IS, b), r, wt, scores(IS, b), ALU.mult, ALU.add)
                ins.then_inc(s["relu_used"], 1)
                if h_ == H - 1:
                    dve.wait_ge(s["relu_used"], n + 1)
                    dia = scores(IS, b)[:, w - P:w]
                    link(dve.tensor_tensor(dia, dia, sq[:, M_CAUSAL, :], ALU.add))
                if n % 3 == 2:
                    m = n // 3
                    name = ("norm", m)
                    dve.wait_ge(scalar_took, TURN[name][1])
                    r = Xf[:, 2048 + (m % 2) * 512:2560 + (m % 2) * 512]
                    link(dve.reciprocal(r, r))
                    dve.scalar_tensor_tensor(C[:, m, :], C[:, m, :], DH ** -0.5 if m < 4 else 1.0, r, ALU.mult, ALU.mult)\
                       .then_inc(s["normed"], 1)
            dve.wait_ge(small_sem, 16 * 7)
            link(dve.tensor_tensor(t3("t3"), small[:, :, 16:24], small_in[:, 92:100].unsqueeze(1).to_broadcast([P, TB, H]),
                                   ALU.add))
            dve.scalar_tensor_tensor(GSC["t0"], GSC["t3"], -1.0, GSC["t3"], ALU.mult, ALU.max).then_inc(s["gate_e"], 1)
            dve.wait_ge(s["gate_exp"], 3)
            link(dve.tensor_scalar(GSC["beta"], GSC["beta"], 1.0, None, ALU.add))
            dve.reciprocal(GSC["beta"], GSC["beta"]).then_inc(s["beg_set"], 1)
            dve.wait_ge(s["gate_ln"], 1)
            link(dve.scalar_tensor_tensor(GSC["t3"], GSC["t3"], 0.0, GSC["t2"], ALU.max, ALU.add))
            dve.scalar_tensor_tensor(t3("g"), t3("t3"), -1.0, small_in[:, 84:92].unsqueeze(1).to_broadcast([P, TB, H]),
                                     ALU.mult, ALU.mult).then_inc(s["gbeta_set"], 1)
            product_ready(dve, ("gc",))
            took(("gc",), dve.tensor_copy(GSC["gc"], bank(("gc",))[:, 0:32]))
            own(("gc",))
            dve.sem_inc(s["gcum_set"], 1)
            dve.wait_ge(s["egc_set"], 1)
            dve.wait_ge(s["beg_set"], 1)
            dve.scalar_tensor_tensor(GSC["nbgc"], GSC["beta"], -1.0, GSC["egc"], ALU.mult, ALU.mult)\
               .then_inc(s["beg_set"], 1)
            def topk_round(b, r):
                src = scores(IS, b) if r == 0 else scores(IW, b)
                link(dve.max(out=st[:, 24:32], in_=src))
                link(dve.match_replace(out=scores(IW, b), in_to_replace=st[:, 24:32], in_values=src, imm_value=FAR))
                if r == NKEEP // 8 - 1:
                    link(dve.tensor_tensor(scores(IW, b), scores(IW, b), scores(IS, b), ALU.is_equal))
                    link(dve.tensor_scalar(scores(IW, b), scores(IW, b), NEG, None, ALU.mult))
            rounds = [(b, r) for b in range(1, TB) for r in range(NKEEP // 8)]
            dve.wait_ge(s["normed"], 8)

            def attend(n):
                for name in attention(n, "s"):
                    b = name[1]
                    w = P * (b + 1)
                    product_ready(dve, name)
                    if n >= 3:
                        dve.wait_ge(s["prob_set"], n - 2)
                    mask = sq[:, M_CAUSAL, :] if b == 0 else scores(IW, b)
                    took(name, dve.tensor_tensor_reduce(SM[n % 3][:, 0:w], bank(name)[:, 0:w], mask, 1.0, FAR, ALU.add,
                                                        ALU.max, rmax[:, n % 4:n % 4 + 1]))
                    own(name)
                    dve.tensor_scalar(negm[:, n % 4:n % 4 + 1], rmax[:, n % 4:n % 4 + 1], -DH ** -0.5, None, ALU.mult)\
                       .then_inc(s["neg_set"], 1)

            def finish_attend(n):
                for name in attention(n, "pv"):
                    _, b, h_ = name
                    m = n - 2
                    dve.wait_ge(s["prob_set"], m + 1)
                    link(dve.reciprocal(rinv[:, m % 4:m % 4 + 1], rsum[:, m % 4:m % 4 + 1]))
                    product_ready(dve, name)
                    took(name, dve.tensor_scalar(OD[:, b, DH * h_:DH * h_ + DH], bank(name)[:, 0:DH],
                                                 rinv[:, m % 4:m % 4 + 1], None, ALU.mult))
                    own(name)
                    dve.sem_inc(s["dsa_set"], 1)

            link(dve.memset(S[:, :, :], 0.0))
            turn = 0
            for c_ in range(TB):
                for g in range(2):
                    u, A = 2 * c_ + g, G[g]
                    name = ("gcb", c_, g)
                    if c_ > 0:
                        dve.wait_ge(s["diff_set"], u)
                    dve.tensor_copy(heads(A["LM"]), scal("g", c_, g).unsqueeze(2).to_broadcast([P, 4, P]))\
                       .then_inc(s["diff_set"], 1)
                    product_ready(dve, name)
                    link(dve.tensor_tensor(heads(A["D"]), heads(bank(name)),
                                           scal("gc", c_, g).unsqueeze(2).to_broadcast([P, 4, P]), ALU.subtract))
                    dve.tensor_scalar(A["XU"], A["D"], 0.0, None, ALU.min).then_inc(s["clip_set"], 1)
                    dve.tensor_scalar(A["XL"], A["D"], 0.0, None, ALU.max).then_inc(s["clip_set"], 1)
                    dve.wait_ge(scalar_took, TURN[name][1])
                    rw = slice(64 * g, 64 * g + 64)
                    dve.tensor_tensor(heads(A["QG"])[rw], C[rw, 0:4, c_ * P:(c_ + 1) * P], heads(A["EG"])[rw], ALU.mult)\
                       .then_inc(s["qg_set"], 1)
                    dve.wait_ge(s["decay_masked"], 2 * u + 2)
                    product_ready(dve, ("qk", c_, g))
                    took(("qk", c_, g), dve.tensor_tensor(A["E1"], bank(("qk", c_, g)), A["E1"], ALU.mult))
                    product_ready(dve, ("kk", c_, g))
                    took(("kk", c_, g), dve.tensor_tensor(A["E2"], bank(("kk", c_, g)), A["E2"], ALU.mult))
                    own(("kk", c_, g))
                    dve.sem_inc(s["l_set"], 1)
                for lv in range(LEVELS):
                    attend(c_ * LEVELS + lv)
                    if lv > 0:
                        for g in range(2):
                            name, A = ("Z", c_, lv, g), G[g]
                            product_ready(dve, name)
                            took(name, dve.tensor_tensor(A["XL"], A["XL"], bank(name), ALU.subtract))
                    finish_attend(c_ * LEVELS + lv)
                    for _ in range(2):
                        if turn < len(rounds):
                            topk_round(*rounds[turn])
                            turn += 1
                for g in range(2):
                    A, name = G[g], ("vn", c_, g)
                    product_ready(dve, name)
                    took(name, dve.tensor_copy(A["VN"], bank(name)[:, 0:256]))
                    own(name)
                    dve.sem_inc(s["vn_set"], 1)
                    if c_ < TB - 1:
                        name = ("st", c_, g)
                        product_ready(dve, name)
                        bk = bank(name)
                        rw = slice(64 * g, 64 * g + 64)
                        link(dve.tensor_tensor(S[rw], S[rw], heads(A["EG"])[rw, :, P - 1:P].to_broadcast([64, 4, DH]),
                                               ALU.mult))
                        ins = dve.tensor_tensor(S[rw], S[rw], heads(bk[:, 0:256])[rw], ALU.add)
                        took(name, ins)
                        own(name)
                        dve.sem_inc(s["state_set"], 1)
            assert turn == len(rounds)
            for n in range(TB * LEVELS, TB * H + 2):
                attend(n)
                finish_attend(n)
            o4 = OG.rearrange("p t (h n) -> p (t h) n", n=DH)
            dve.wait_ge(s["gdn_sq"], 1)
            dve.tensor_reduce(GSC["osum"], V[:, :, :].rearrange("p t (h n) -> p (t h) n", n=DH), AX.X, ALU.add)\
               .then_inc(s["gdn_sum"], 1)
            dve.wait_ge(s["gdn_root"], 1)
            link(dve.reciprocal(GSC["orr"], GSC["orr"]))
            link(dve.tensor_tensor(o4, o4, GSC["orr"].unsqueeze(2).to_broadcast([P, 32, DH]), ALU.mult))
            link(dve.tensor_tensor(o4, o4, small_in[:, 20:84].unsqueeze(1).to_broadcast([P, 32, DH]), ALU.mult))
            dve.wait_ge(scalar_took, TURN[("z", 3)][1])
            dve.tensor_tensor(OG, OG, SZ[:, :, :], ALU.mult).then_inc(s["gdn_set"], 1)
            for f in range(4):
                product_ready(dve, ("ot", 1, f))
                took(("ot", 1, f), dve.tensor_copy(OGT[:, f, :], bank(("ot", 1, f))))
            for f in range(KD):
                for k, (nm, gt) in enumerate((("ya", "ga"), ("yb", "gb"))):
                    i = 2 * f + k
                    product_ready(dve, (nm, f))
                    dve.wait_ge(scalar_took, TURN[(gt, f)][1])
                    gate = SZ[:, i % 2, :]
                    dst = MT[:, f, :] if k == 0 else gate
                    took((nm, f), dve.tensor_tensor(dst, gate, bank((nm, f)), ALU.mult))
                    if k == 0:
                        own((nm, f))
                        dve.sem_inc(s["merged_set"], 1)
                    else:
                        own((nm, f))
                        dve.tensor_tensor(MT[:, f, :], MT[:, f, :], gate, ALU.add).then_inc(s["merged_set"], 1)
            dve.wait_ge(s["x_again"], 16)
            for t in range(TB):
                for u in range(2):
                    name = ("y", t, u)
                    product_ready(dve, name)
                    took(name, dve.tensor_copy(YS[:, t, 512 * u:512 * u + 512], bank(name)))
                own(("y", t, 1))
                dve.sem_inc(s["y_copied"], 1)
                dve.wait_ge(s["y_root"], t + 1)
                link(dve.reciprocal(rstd[:, t:t + 1], rstd[:, t:t + 1]))
                link(dve.scalar_tensor_tensor(YS[:, t, :], YS[:, t, :], rstd[:, t:t + 1], g1p[:, :], ALU.mult, ALU.mult))
                dve.tensor_tensor(X[:, t, :], X[:, t, :], YS[:, t, :], ALU.add).then_inc(s["x1_done"], 1)
                dve.wait_ge(s["mse_root"], t + 1)
                dve.reciprocal(rstd[:, t:t + 1], rstd[:, t:t + 1]).then_inc(s["xn2_done"], 1)
            for f in range(0, KD, 2):
                name = ("h2", f)
                product_ready(dve, name)
                took(name, dve.tensor_scalar(HT[:, f, :], bank(name), acol[:, 1, f:f + 1], mod[:, 16 + f:17 + f],
                                             ALU.mult, ALU.add))
            RL = IS[:, 0:80].rearrange("p (t n) -> p t n", n=20)
            R = IS[:, 128:1024].rearrange("p (a t n) -> p a t n", t=TB, n=16)
            def b4(ap):
                return ap.unsqueeze(2).to_broadcast([P, TB, 4])
            tie = col[:, K_TIE:K_TIE + 4].unsqueeze(1).to_broadcast([P, TB, 4])
            sv = lambda n: IW[:, 4 * n:4 * n + 4]
            product_ready(dve, ("router",))
            took(("router",), dve.tensor_tensor(RL, bank(("router",))[:, 0:128].rearrange(
                "p (t n) -> p t n", n=32)[:, :, 0:20], small_in[:, 0:20].unsqueeze(1).to_broadcast([P, TB, 20]), ALU.add))
            own(("router",))

            def one_hot(dst, src, m, top):
                link(dve.tensor_tensor(dst, src, b4(top), ALU.is_equal))
                link(dve.tensor_tensor(dst, dst, tie, ALU.mult))
                link(dve.tensor_reduce(m, dst, AX.X, ALU.max))
                link(dve.tensor_tensor(dst, dst, b4(m), ALU.is_equal))

            gl, el = RL[:, :, 0:4], RL[:, :, 4:20]
            link(dve.tensor_reduce(sv(0), gl, AX.X, ALU.max))
            ghot, ingrp, h1, h2, e2 = (R[:, n, :, 0:4] for n in range(5))
            one_hot(ghot, gl, sv(1), sv(0))
            dve.tensor_tensor(GSC["t1"][:, 0:16].rearrange("p (t n) -> p t n", n=4), gl, b4(sv(0)), ALU.subtract)\
               .then_inc(s["route_exp"], 1)
            t16 = R[:, 5, :, :]
            link(dve.tensor_tensor(t16.rearrange("p t (g e) -> p t g e", e=4), el.rearrange("p t (g e) -> p t g e", e=4),
                                   ghot.unsqueeze(3).to_broadcast([P, TB, 4, 4]), ALU.mult))
            link(dve.tensor_reduce(ingrp, t16.rearrange("p t (g e) -> p t e g", e=4), AX.X, ALU.add))
            link(dve.tensor_reduce(sv(2), ingrp, AX.X, ALU.max))
            one_hot(h1, ingrp, sv(3), sv(2))
            link(dve.scalar_tensor_tensor(e2, h1, NEG, ingrp, ALU.mult, ALU.add))
            link(dve.tensor_reduce(sv(4), e2, AX.X, ALU.max))
            one_hot(h2, e2, sv(5), sv(4))
            dve.tensor_tensor(GSC["t0"][:, 0:4], sv(4), sv(2), ALU.subtract).then_inc(s["route_exp"], 1)
            dve.wait_ge(s["gate_exp"], 5)
            gs = GSC["t2"][:, 0:16].rearrange("p (t n) -> p t n", n=4)
            link(dve.tensor_reduce(sv(6), gs, AX.X, ALU.add))
            link(dve.tensor_scalar(sv(7), GSC["t3"][:, 0:4], 1.0, None, ALU.add))
            link(dve.tensor_tensor(sv(8), sv(6), sv(7), ALU.mult))
            link(dve.reciprocal(sv(8), sv(8)))
            link(dve.tensor_tensor(sv(9), sv(8), GSC["t3"][:, 0:4], ALU.mult))
            o1, o2, both, pos = (IW[:, 64 * n:64 * n + 64].rearrange("p (t n) -> p t n", n=NE) for n in (1, 2, 3, 4))
            for dst, hot in ((o1, h1), (o2, h2)):
                link(dve.tensor_tensor(dst.rearrange("p t (g e) -> p t g e", e=4),
                                       ghot.unsqueeze(3).to_broadcast([P, TB, 4, 4]),
                                       hot.unsqueeze(2).to_broadcast([P, TB, 4, 4]), ALU.mult))
            dve.tensor_tensor(both, o1, o2, ALU.add).then_inc(s["route_set"], 1)
            product_ready(dve, ("rank",))
            rk = bank(("rank",))
            incl = rk[:, 0:64].rearrange("p (t n) -> p t n", n=NE)
            count = IW[:, 320:336]
            sums = [IW[:, 336:352], IW[:, 352:368]]
            tiles = IW[:, 368:384]
            link(dve.tensor_copy(count, rk[:, 64:80]))
            link(dve.tensor_scalar(tiles, count, 0.0, None, ALU.is_gt))
            for k in range(1, T // P):
                link(dve.scalar_tensor_tensor(tiles, count, float(P * k), tiles, ALU.is_gt, ALU.add))
            link(dve.tensor_copy(sums[0], tiles))
            for k in range(4):
                a, b, w = sums[k % 2], sums[1 - k % 2], 1 << k
                link(dve.tensor_copy(b[:, 0:w], a[:, 0:w]))
                link(dve.tensor_tensor(b[:, w:NE], a[:, w:NE], a[:, 0:NE - w], ALU.add))
            ends = sums[0]
            cmp = IS[:, 0:512].rearrange("p (j n) -> p j n", n=NE)
            rowj = col[:, K_ROW:K_ROW + 32]
            link(dve.tensor_tensor(cmp, ends.unsqueeze(1).to_broadcast([P, 32, NE]),
                                   rowj.unsqueeze(2).to_broadcast([P, 32, NE]), ALU.is_le))
            e_of = IW[:, 384:416]
            link(dve.tensor_reduce(e_of, cmp, AX.X, ALU.add))
            dve.tensor_scalar(eid[:, :], e_of, float(NE - 1), None, ALU.min).then_inc(experts_set, 1)
            link(dve.tensor_tensor(tiles, ends, tiles, ALU.subtract))
            link(dve.tensor_scalar(pos, incl, float(P), -float(P * TILES - 1), ALU.is_gt, ALU.mult))
            over = IW[:, 448:512].rearrange("p (t n) -> p t n", n=NE)
            for k in range(2, T // P):
                link(dve.tensor_scalar(over, incl, float(P * k), -float(P * TILES - 1), ALU.is_gt, ALU.mult))
                link(dve.tensor_tensor(pos, pos, over, ALU.add))
            link(dve.scalar_tensor_tensor(pos, incl, float(TILES), pos, ALU.mult, ALU.add))
            took(("rank",), dve.scalar_tensor_tensor(pos, pos, -float(TILES),
                                                     tiles.unsqueeze(1).to_broadcast([P, TB, NE]), ALU.add, ALU.add))
            own(("rank",))
            fad = IW[:, 512:520]
            for n, o in enumerate((o1, o2)):
                link(dve.tensor_tensor(over, o, pos, ALU.mult))
                link(dve.tensor_reduce(fad[:, TB * n:TB * n + TB], over, AX.X, ALU.add))
            dve.tensor_copy(token[:, :], col[:, K_TOKEN:K_TOKEN + TB]).then_inc(address_set, 1)
            dve.tensor_copy(address[:, :], fad).then_inc(address_set, 1)

            def evacuate_h(j, slot):
                dve.wait_ge(turned, j + 1)
                wait_from(dve, gu_done, j - 1)
                for k in range(4, KD):
                    ins = dve.tensor_scalar(HX[slot][:, k, :], ps[1][:, (k - 4) * P:(k - 3) * P], acol[:, 1, k:k + 1],
                                            mod[:, 16 + k:17 + k], ALU.mult, ALU.add)
                ins.then_inc(h_vector, 1)

            def evacuate_out(j, slot):
                dve.wait_ge(down_done, j + 1)
                wait_from(dve, tile_stored[slot], 16 * (j // 2) if isinstance(j, int) else (j - slot) * 8)
                dve.tensor_copy(YT[slot][:, 512:1024], ps[6][:, :]).then_inc(out_vector, 1)

            def step(j, slot):
                dve.wait_ge(silu_done, j + 1)
                wait_from(dve, act_turned, j - 1)
                dve.tensor_tensor(AC[slot], SI[slot], ps[2 + slot][:, 256:512], ALU.mult).then_inc(act_done, 1)
                if not isinstance(j, int) or j < TILES - 1:
                    evacuate_h(j + 1, 1 - slot)
                if not isinstance(j, int) or j >= 1:
                    evacuate_out(j - 1, 1 - slot)
            evacuate_h(0, 0)
            steps(dve, step)
            evacuate_out(TILES - 1, (TILES - 1) % 2)
            for t in range(TB):
                dve.wait_ge(both_in[t], 32)
                link(dve.tensor_scalar(Y1[:, t, :], Y1[:, t, :], sv(8)[:, t:t + 1], None, ALU.mult))
                dve.scalar_tensor_tensor(Y1[:, t, :], Y2[:, t, :], sv(9)[:, t:t + 1], Y1[:, t, :], ALU.mult, ALU.add)\
                   .then_inc(s["y_sum"], 1)
            for t in range(TB):
                dve.wait_ge(s["mse_root"], TB + t + 1)
                link(dve.reciprocal(rstd[:, t:t + 1], rstd[:, t:t + 1]))
                link(dve.scalar_tensor_tensor(Y1[:, t, :], Y1[:, t, :], rstd[:, t:t + 1], g2p[:, :], ALU.mult, ALU.mult))
                dve.tensor_tensor(XN[:, t, :], X[:, t, :], Y1[:, t, :], ALU.add).then_inc(s["post_norm"], 1)

        @block.tensor
        def _(pe):
            at = [0]

            def begin(name):
                n = at[0]
                assert PLAN[n][0] == name, (PLAN[n], name)
                if n >= BANKS:
                    who, turn = TURN[PLAN[n - BANKS][0]]
                    pe.wait_ge(vector_took if who == "v" else scalar_took, turn)
                return ps[n % BANKS]

            def end(ins):
                ins.then_inc(product_done, 1)
                at[0] += 1

            def mm(o, a, b, first=True, last=True):
                return pe.matmul(o, a, b, start=first, stop=last)

            def taken(name):
                who, turn = TURN[name]
                pe.wait_ge(vector_took if who == "v" else scalar_took, turn)

            def four_transposes(name, src):
                b = begin(name)
                for k in range(4):
                    ins = pe.transpose(b[:, k * P:(k + 1) * P], src(k), ident)
                end(ins)

            def ada_row(n):
                b = begin(("ada", n))
                for u in range(2):
                    k = 2 * n + u
                    pe.wait_ge(ada_in[k % 2], 16 * (k // 2 + 1))
                    for j in range(KD):
                        ins = mm(b[0:1, 256 * u:256 * u + 256], ccol[:, j:j + 1], AR[:, k % 2, j, :], j == 0, False)
                    ins.then_inc(ada_used, 1)
                    ins = mm(b[0:1, 256 * u:256 * u + 256], sq[0:12, M_ID, n:n + 1],
                             bada[:, 256 * u:256 * u + 256], False, True)
                end(ins)

            def ada(n, k):
                b = begin(("ada", n))
                pe.wait_ge(s["ada_summed"], n - 3)
                mm(b[:, :], ones[:, :], ada_sum[:, n % 2, :], True, False)
                end(mm(b[:, :], sq[0:12, M_ID, n:n + 1].to_broadcast([12, P]), bada[:, :], False, True))

            def adac(n, k):
                b = begin(("adac", n))
                taken(("ada", n))
                for j in range(4):
                    ins = mm(b[:, j:j + 1], modrow[0:1, k % 2, j * P:(j + 1) * P], ones[0:1, 0:1])
                end(ins)

            def features(name, w, m):
                b = begin(name)
                for k in range(KD):
                    ins = mm(b[:, :], w[:, k, m * P:(m + 1) * P], HT[:, k, :], k == 0, k == KD - 1)
                end(ins)

            def tokens(name, w, t):
                b = begin(name)
                for k in range(KD):
                    ins = mm(b[:, :], HT[:, k, t * P:(t + 1) * P], w[:, k, :], k == 0, k == KD - 1)
                end(ins)

            def used():
                pe.wait_ge(product_done, at[0])
                pe.sem_inc(weights_used, 1)

            pe.wait_ge(rows_in, 64)
            pe.wait_ge(consts_in, 32)
            b = begin(("rows",))
            end(pe.transpose(b[:, 0:N_ROWS], rows[:, :], sq[0:N_ROWS, M_ID, 0:N_ROWS]))
            pe.wait_ge(s["ones_set"], 1)
            pe.wait_ge(bias_in, 16)
            pe.wait_ge(s["ccol_done"], 1)
            for n in range(5):
                if n < 4:
                    ada_row(n)
                if n >= 1:
                    adac(n - 1, n - 1)
            pe.wait_ge(s["xn_done"], TB)
            for f in range(KD):
                four_transposes(("h1", f), lambda t: XN[:, t, f * P:(f + 1) * P])
            taken(("h1", KD - 1))
            taken(("h1", KD - 2))
            seq = rotated()

            def swap(n):
                b = begin(("swap",) + seq[n])
                pe.wait_ge(s["raw_set"], n + 1)
                end(mm(b[:, :], sq[:, M_SWAP, :], raw[:, n % 2, :]))

            for n, it in enumerate(seq):
                kind, m = it
                wname = {"q": "q", "k": "k", "iq": "iq", "ik": "small"}[kind]
                if m == 0:
                    weights_ready(pe, wname)
                features(("rope",) + it, wslot(wname), m)
                if n >= 1:
                    swap(n - 1)
                if m == 3:
                    used()
                if it == ("k", 3):
                    weights_ready(pe, "v")
                    for t in range(TB):
                        tokens(("v", t), wslot("v"), t)
                    used()
            swap(12)
            b = begin(("small",))
            for t in range(TB):
                for k in range(KD):
                    ins = mm(b[:, 32 * t:32 * t + 24], HT[:, k, t * P:(t + 1) * P], wslot("small")[:, k, 128:152],
                             k == 0, k == KD - 1)
            end(ins)
            used()
            k = 4
            for m in range(12):
                wname = ("gq", "gk", "gv")[m // 4]
                if m % 4 == 0:
                    weights_ready(pe, wname)
                features(("conv", m), wslot(wname), m % 4)
                if m % 4 == 3:
                    used()
                if m % 3 == 2:
                    for n in (4 + 2 * (m // 3), 5 + 2 * (m // 3)):
                        ada(n, k)
                        if 6 <= n < 10:
                            adac(n, k)
                            k += 1
            weights_ready(pe, "z")
            for t in range(TB):
                tokens(("z", t), wslot("z"), t)
            used()
            pe.wait_ge(s["rope_set"], 13)
            for n in range(3 * H):
                qb, h = 1 + n // H, n % H
                b = begin(("idx", qb, h))
                rw = slice(64 * (h % 2), 64 * (h % 2) + 64)
                w = P * (qb + 1)
                end(mm(b[:, 0:w], IQ[rw, h // 2, qb * P:(qb + 1) * P], KI[rw, 0:w]))
                if n % 3 == 2:
                    m = n // 3
                    b = begin(("norm", m))
                    pe.wait_ge(s["square_set"], m + 1)
                    end(mm(b[:, :], sq[:, M_HEADS, :], Xf[:, 1024 + (m % 2) * 512:1536 + (m % 2) * 512]))
            pe.wait_ge(s["normed"], 8)
            for t in range(TB):
                four_transposes(("ktok", t), lambda m: C[:, 4 + m, t * P:(t + 1) * P])
            for t in range(TB):
                four_transposes(("vtok", t), lambda m: C[:, 8 + m, t * P:(t + 1) * P])
            b = begin(("gc",))
            pe.wait_ge(s["gbeta_set"], 1)
            end(mm(b[:, 0:32], sq[:, M_UPPER, :], GSC["g"]))
            def four(b, lhs, rhs):
                for hh in range(4):
                    ins = mm(b[:, hh * P:(hh + 1) * P], lhs(hh), rhs(hh))
                return ins

            def attend(n, want):
                for name in attention(n, want):
                    _, qb, h = name
                    w = P * (qb + 1)
                    b = begin(name)
                    if want == "s":
                        rw = slice(64 * (h % 2), 64 * (h % 2) + 64)
                        ins = mm(b[:, 0:w], QT[rw, h // 2, qb * P:(qb + 1) * P], KT[rw, h // 2, 0:w])
                    elif want == "pt":
                        pe.wait_ge(s["prob_set"], n)
                        for k in range(qb + 1):
                            ins = pe.transpose(b[:, k * P:(k + 1) * P], PR[(n - 1) % 2][:, k * P:(k + 1) * P], ident)
                    else:
                        taken(("pt", qb, h))
                        for k in range(qb + 1):
                            ins = mm(b[:, 0:DH], PT[n % 2][:, k * P:(k + 1) * P], V[:, k, h * DH:(h + 1) * DH],
                                     k == 0, k == qb)
                    end(ins)

            for c in range(TB):
                tok = slice(c * P, (c + 1) * P)
                for g in range(2):
                    u, A = 2 * c + g, G[g]
                    b = begin(("gcb", c, g))
                    pe.wait_ge(s["diff_set"], u + 1)
                    end(four(b, lambda hh: A["LM"][:, hh * P:(hh + 1) * P], lambda hh: sq[:, M_UPPER, :]))
                    rw = slice(64 * g, 64 * g + 64)
                    b = begin(("qk", c, g))
                    end(four(b, lambda hh: C[rw, 4 + hh, tok], lambda hh: C[rw, hh, tok]))
                    b = begin(("kk", c, g))
                    end(four(b, lambda hh: C[rw, 4 + hh, tok], lambda hh: C[rw, 4 + hh, tok]))
                hp = lambda ap, hh: ap[:, hh * P:(hh + 1) * P]
                for lv in range(LEVELS):
                    if lv > 0:
                        for g in range(2):
                            A = G[g]
                            b = begin(("Y", c, lv, g))
                            pe.wait_ge(s["lm_set"], (2 * c) * (LEVELS - 1) + 2 * (lv - 1) + g + 1)
                            taken(("T", c, lv - 1, g))
                            end(four(b, lambda hh: hp(A["LM"], hh), lambda hh: hp(A["XU"], hh)))
                    attend(c * LEVELS + lv, "s")
                    if lv > 0:
                        for g in range(2):
                            A = G[g]
                            b = begin(("Z", c, lv, g))
                            taken(("Y", c, lv, g))
                            end(four(b, lambda hh: hp(A["D"], hh), lambda hh: hp(A["XL"], hh)))
                    attend(c * LEVELS + lv, "pt")
                    attend(c * LEVELS + lv, "pv")
                    for g in range(2):
                        A = G[g]
                        if lv == 0:
                            pe.wait_ge(s["x0_set"], 2 * c + g + 1)
                        else:
                            taken(("Z", c, lv, g))
                        four_transposes(("T", c, lv, g), lambda hh: hp(A["XL"], hh))
                for g in range(2):
                    A = G[g]
                    b = begin(("nw", c, g))
                    taken(("T", c, LEVELS - 1, g))
                    pe.wait_ge(s["g_operands"], 2 * (2 * c + g) + 2)
                    rw = slice(64 * g, 64 * g + 64)
                    end(four(b[rw, :], lambda hh: A["KBG"][:, hh * DH:(hh + 1) * DH], lambda hh: hp(A["XU"], hh)))
                for g in range(2):
                    u, A = 2 * c + g, G[g]
                    b = begin(("vn", c, g))
                    pe.wait_ge(s["nw_set"], u + 1)
                    if c > 0:
                        pe.wait_ge(s["state_set"], u - 1)
                    for hh in range(4):
                        rw = slice(64 * g, 64 * g + 64)
                        o = b[:, hh * DH:(hh + 1) * DH]
                        mm(o, hp(A["XU"], hh), A["VB"][:, hh * DH:(hh + 1) * DH], True, False)
                        ins = mm(o, heads(A["NW"])[rw, hh, :], S[rw, hh, :], False, True)
                    end(ins)
                    b = begin(("o", c, g))
                    pe.wait_ge(s["vn_set"], u + 1)
                    for hh in range(4):
                        rw = slice(64 * g, 64 * g + 64)
                        o = b[:, hh * DH:(hh + 1) * DH]
                        mm(o, heads(A["QG"])[rw, hh, :], S[rw, hh, :], True, False)
                        ins = mm(o, hp(A["E1"], hh), A["VN"][:, hh * DH:(hh + 1) * DH], False, True)
                    end(ins)
                    if c < TB - 1:
                        b = begin(("st", c, g))
                        pe.wait_ge(s["kd_set"], u + 1)
                        for hh in range(4):
                            hd = slice(hh * DH, (hh + 1) * DH)
                            ins = mm(b[64 * g:64 * g + 64, hd], A["KDEC"][:, hd], A["VN"][:, hd])
                        end(ins)
            for n in range(TB * LEVELS, TB * H + 2):
                for kind in ("s", "pt", "pv"):
                    attend(n, kind)
            pe.wait_ge(s["dsa_set"], len(TODO))
            for f in range(4):
                four_transposes(("ot", 0, f), lambda t: OD[:, t, f * P:(f + 1) * P])
            pe.wait_ge(s["gdn_set"], 1)
            for f in range(4):
                four_transposes(("ot", 1, f), lambda t: OG[:, t, f * P:(f + 1) * P])
            taken(("ot", 0, 3))
            taken(("ot", 1, 3))
            def branch(name, src, w, m):
                b = begin(name)
                for k in range(4):
                    ins = mm(b[:, :], w[:, k, m * P:(m + 1) * P], src[:, k, :], k == 0, k == 3)
                end(ins)

            for f in range(KD):
                half, m = f // 4, f % 4
                if m == 0:
                    for nm in ("ga", "gb", "br"):
                        weights_ready(pe, f"{nm}{half}")
                features(("ga", f), wslot(f"ga{half}"), m)
                branch(("ya", f), OAT, wslot(f"br{half}")[:, 0:4, :], m)
                features(("gb", f), wslot(f"gb{half}"), m)
                branch(("yb", f), OGT, wslot(f"br{half}")[:, 4:8, :], m)
                if m == 3:
                    for _ in range(3):
                        used()
            pe.wait_ge(s["merged_set"], 2 * KD)
            weights_ready(pe, "out0")
            weights_ready(pe, "out1")
            for t in range(TB):
                for u in range(2):
                    b = begin(("y", t, u))
                    for k in range(KD):
                        ins = mm(b[:, :], MT[:, k, t * P:(t + 1) * P], wslot(f"out{u}")[:, k, :], k == 0, k == KD - 1)
                    end(ins)
            used()
            used()
            pe.wait_ge(s["xn_done"], 2 * TB)
            for f in range(KD):
                four_transposes(("h2", f), lambda t: XN[:, t, f * P:(f + 1) * P])
            taken(("h2", KD - 1))
            taken(("h2", KD - 2))
            b = begin(("router",))
            for t in range(TB):
                for k in range(KD):
                    ins = mm(b[:, 32 * t:32 * t + 20], HT[:, k, t * P:(t + 1) * P], wroute[:, k, :], k == 0, k == KD - 1)
            end(ins)
            taken(("router",))
            b = begin(("rank",))
            pe.wait_ge(s["route_set"], 1)
            both = IW[:, 192:256].rearrange("p (t n) -> p t n", n=NE)
            for t in range(TB):
                for k in range(t + 1):
                    mm(b[:, NE * t:NE * t + NE], sq[:, M_UPPER, :] if k == t else ones[:, :], both[:, k, :],
                       k == 0, k == t)
            for k in range(TB):
                ins = mm(b[:, 64:80], ones[:, :], both[:, k, :], k == 0, k == TB - 1)
            end(ins)
            taken(("rank",))

            def turn_rows(j, slot):
                n = j // 2 if isinstance(j, int) else None
                pe.wait_ge(rows_gathered[slot], 16 * (j // 2 + 1) if n is not None else (j - slot) * 8 + 16)
                wait_from(pe, h_scalar, j)
                wait_from(pe, h_vector, j)
                for k in range(KD):
                    ins = pe.transpose(ps[k // 4][:, (k % 4) * P:(k % 4 + 1) * P], GX[:, slot, k * P:(k + 1) * P], ident)
                ins.then_inc(turned, 1)

            def gate_up(j, slot):
                pe.wait_ge(gate_up_in[slot], 32 * (j // 2 + 1) if isinstance(j, int) else (j - slot) * 16 + 32)
                pe.wait_ge(h_scalar, j + 1)
                pe.wait_ge(h_vector, j + 1)
                wait_from(pe, act_done, j - 1)
                gu = expert_gu(slot)
                for k in range(KD):
                    ins = mm(ps[2 + slot][:, :], HX[slot][:, k, :], gu[:, k].rearrange("p u f -> p (u f)"),
                             k == 0, k == KD - 1)
                ins.then_inc(gu_done, 1)

            def turn_act(j, slot):
                pe.wait_ge(act_done, j + 1)
                wait_from(pe, act_back, j)
                for k in range(2):
                    ins = pe.transpose(ps[4][:, k * P:(k + 1) * P], AC[slot][:, k * P:(k + 1) * P], ident)
                ins.then_inc(act_turned, 1)

            def down(j, slot):
                pe.wait_ge(down_in[slot], 16 * (j // 2 + 1) if isinstance(j, int) else (j - slot) * 8 + 16)
                pe.wait_ge(act_back, j + 1)
                wait_from(pe, out_scalar, j)
                wait_from(pe, out_vector, j)
                dn = expert_d(slot)
                for u in range(2):
                    for k in range(2):
                        ins = mm(ps[5 + u][:, :], ACT_T[slot][:, k * P:(k + 1) * P], dn[:, k, 512 * u:512 * u + 512],
                                 k == 0, k == 1)
                ins.then_inc(down_done, 1)

            def step(j, slot):
                gate_up(j, slot)
                if not isinstance(j, int) or j >= 1:
                    turn_act(j - 1, 1 - slot)
                if not isinstance(j, int) or j < TILES - 1:
                    turn_rows(j + 1, 1 - slot)
                if not isinstance(j, int) or j >= 1:
                    down(j - 1, 1 - slot)
            turn_rows(0, 0)
            steps(pe, step)
            turn_act(TILES - 1, (TILES - 1) % 2)
            down(TILES - 1, (TILES - 1) % 2)


_INS = ['x', 'c', 'positions', 'w_ada', 'b_ada', 'mix_norm_pre', 'mix_norm_post', 'w_in', 'conv_w', 'a_log', 'dt_bias',
        'gdn_norm', 'w_branch_dsa', 'w_branch_gdn', 'w_out', 'ffn_norm_pre', 'ffn_norm_post', 'w_router_group',
        'b_router_group', 'w_router_expert', 'b_router_expert', 'w_expert_gate', 'w_expert_up', 'w_expert_down']


def kernel(**inputs):
    import numpy as _np
    import concourse.bacc as _bacc
    from concourse import mybir as _mybir
    from concourse.bass_utils import run_bass_kernel_spmd as _run

    nc = _bacc.Bacc("TRN2", target_bir_lowering=False, num_devices=1, dynamic_dma_scratch_size=4096)
    arrays, args = {}, []
    for name in _INS:
        a = _np.ascontiguousarray(_np.asarray(inputs[name])[0])
        arrays[f"in_{name}"] = a
        args.append(nc.dram_tensor(f"in_{name}", a.shape, _mybir.dt.from_np(a.dtype), kind="ExternalInput").ap())
    for name, a in zip(("squares", "columns"), constants()):
        arrays[name] = a
        args.append(nc.dram_tensor(name, a.shape, _mybir.dt.float32, kind="ExternalInput").ap())
    out = nc.dram_tensor("out", (T, D), _mybir.dt.float32, kind="ExternalOutput").ap()
    layer_kernel(nc, *args, out)
    r = _run(nc, [arrays], core_ids=[0])
    return r.results[0]["out"].reshape(1, T, D)
```

```python
from contextlib import ExitStack

import numpy as np
import concourse.bass as bass
from concourse import mybir
from concourse.alu_op_type import AluOpType as ALU

F32 = mybir.dt.float32
I32 = mybir.dt.int32
ACT = mybir.ActivationFunctionType
AX = mybir.AxisListType

P = 128
D, T = 1024, 512
KD, TB = D // P, T // P
H, DH = 8, 64
HW = H * DH
NKEEP = 128
NEG = -1e30
FAR = -3e38
EPS = 1e-6
NE, DE, NG, EG = 16, 256, 4, 4
BANKS = 8
TILES = 2 * T // P + NE - 1
LEVELS = 7

C_Q, C_K, C_V, C_IQ = 0, HW, 2 * HW, 3 * HW
C_IK = 4 * HW
C_IW = C_IK + DH
C_GQ = C_IW + H
C_Z = C_GQ + 3 * HW
C_B = C_Z + HW
C_GA = C_B + 2 * H
C_GB = C_GA + D

(M_ID, M_UPPER, M_HEADS, M_CAUSAL, M_LOWER, M_SWAP, M_LEVEL) = range(7)
N_SQ = M_LEVEL + LEVELS
(K_FREQ, K_SIGN, K_HALFPI, K_EPS, K_ONE, K_TIE) = range(6)
K_TOKEN = K_TIE + 4
K_ROW = K_TOKEN + TB
N_COL = K_ROW + 32
(R_C, R_PRE1, R_PRE2, R_CONV) = (0, KD, 2 * KD, 3 * KD)
N_ROWS = R_CONV + 4 * 12


def constants():
    i = np.arange(P)
    sq = np.zeros((P, N_SQ, P), np.float32)
    sq[:, M_ID] = np.eye(P)
    sq[:, M_UPPER] = i[:, None] <= i[None, :]
    sq[:, M_HEADS] = i[:, None] // DH == i[None, :] // DH
    sq[:, M_CAUSAL] = np.where(i[None, :] <= i[:, None], 0, NEG)
    sq[:, M_LOWER] = i[:, None] > i[None, :]
    sq[:, M_SWAP] = (i[:, None] ^ (DH // 2)) == i[None, :]
    for k in range(LEVELS):
        b = 1 << k
        same = i[:, None] // (2 * b) == i[None, :] // (2 * b)
        sq[:, M_LEVEL + k] = same & (i[:, None] % (2 * b) >= b) & (i[None, :] % (2 * b) < b)
    col = np.zeros((P, N_COL), np.float32)
    half = DH // 2
    freq = np.float32(10000.0) ** (-np.arange(0, DH, 2, dtype=np.float32) / np.float32(DH))
    col[:, K_FREQ] = freq[i % half]
    col[:, K_SIGN] = np.where(i % DH < half, -1, 1)
    col[:, K_HALFPI] = np.pi / 2
    col[:, K_EPS] = EPS
    col[:, K_ONE] = 1
    col[:, K_TIE:K_TIE + 4] = [4, 3, 2, 1]
    col[:, K_TOKEN:K_TOKEN + TB] = i[:, None] + P * np.arange(TB)
    col[:, K_ROW:] = np.arange(32)
    return sq.reshape(P, N_SQ * P), col


def rotated():
    return [("q", m) for m in range(4)] + [("k", m) for m in range(4)] + [("iq", m) for m in range(4)] + [("ik", 0)]


def attention(n, kind):
    m = n - {"s": 0, "pt": 1, "pv": 2}[kind]
    return [(kind, m // H, m % H)] if 0 <= m < TB * H else []


EARLY_GATES = [(nm, m) for nm in ("ga", "gb") for m in range(4)]


TAIL = [("y", 0), ("y", 1), ("h2", 0), ("y", 2), ("router", 0), ("h2", 1), ("y", 3), ("router", 1), ("h2", 2), ("h2", 3),
        ("router", 2), ("router", 3)]


def first_step(c, lv):
    return c * LEVELS + lv * (2 if c == TB - 1 else 1)


def second_step(c, lv):
    return [first_step(c, lv) + 1] if c == TB - 1 else []


assert first_step(TB - 1, LEVELS - 1) + 1 >= TB * H + 1


def plan_products():
    plan = [(("rows",), "v")]
    for n in range(5):
        if n < 4:
            plan.append((("ada", n), "v"))
        if n >= 1:
            plan.append((("adac", n - 1), "v"))
    plan += [(("h1", f), "va"[f % 2]) for f in range(KD)]
    seq = rotated()
    for n, it in enumerate(seq):
        plan.append((("rope",) + it, "a"))
        if n >= 1:
            plan.append((("swap",) + seq[n - 1], "v"))
        if it == ("k", 3):
            plan += [(("v", t), "a") for t in range(TB)]
    plan.append((("swap",) + seq[-1], "v"))
    plan.append((("small",), "v"))
    for m in range(12):
        plan.append((("conv", m), "a"))
        if m in (6, 9):
            plan += [(("adac", n), "v") for n in (2 * (m // 3) + 2, 2 * (m // 3) + 3)]
        if m % 3 == 2:
            for n in (4 + 2 * (m // 3), 5 + 2 * (m // 3)):
                col = 6 <= n < 10
                plan.append((("ada", n), "a" if col else "v"))
    plan += [(("z", 0), "a"), (("gc",), "v")]
    for n in range(3 * H):
        plan.append((("idx", 1 + n // H, n % H), "a"))
        if n % 3 == 2:
            plan.append((("norm", n // 3), "a"))
    plan.append((("z", 1), "a"))
    plan += [(("ktok", t), "a") for t in range(TB)] + [(("vtok", t), "a") for t in range(TB)]
    plan += [(("z", t), "a") for t in (2, 3)]
    for c in range(TB):
        plan += [(("gcb", c, g), "a") for g in range(2)]
        plan += [((nm, c, g), "v") for nm in ("kk", "qk") for g in range(2)]
        for lv in range(LEVELS):
            n = first_step(c, lv)
            if lv > 0:
                plan += [(("Y", c, lv, g), "a") for g in range(2)]
            plan += [(name, "v") for name in attention(n, "s")]
            if lv > 0:
                plan += [(("Z", c, lv, g), "v") for g in range(2)]
            plan += [(name, "a") for name in attention(n, "pt")]
            plan += [(name, "v") for name in attention(n, "pv")]
            if lv == 0:
                plan.append((EARLY_GATES[2 * c], "a"))
            plan += [(("T", c, lv, g), "a") for g in range(2)]
            for n in second_step(c, lv):
                plan += [(name, "v") for name in attention(n, "s")]
                plan += [(name, "a") for name in attention(n, "pt")]
                plan += [(name, "v") for name in attention(n, "pv")]
        for g in range(2):
            plan += [(("nw", c, g), "a")]
        plan.append((EARLY_GATES[2 * c + 1], "a"))
        plan += [(("vn", c, g), "v") for g in range(2)]
        for g in range(2):
            plan += [(("o", c, g), "a")]
            if c < TB - 1:
                plan += [(("st", c, g), "v")]
    for k, nm in enumerate(("ya", "yb")):
        plan += [(("ot", k, f), "av"[k]) for f in range(4)]
        plan += [((nm, f), "v") for f in range(4)]
    plan += [((nm, m), "a") for nm in ("ga", "gb") for m in range(4, KD)]
    for f in range(4, KD):
        plan += [(("ya", f), "v"), (("yb", f), "v")]
    for nm, t in TAIL:
        if nm == "y":
            plan += [((nm, t, u), "v") for u in range(2)]
        elif nm == "h2":
            plan += [((nm, t, u), "va"[u]) for u in range(2)]
        else:
            plan.append(((nm, t), "v"))
    plan.append((("rank",), "v"))
    return plan


def layer_kernel(nc, x, cond, positions, w_ada, b_ada, mix_pre, mix_post, w_in, conv_w, a_log, dt_bias, gdn_norm,
                 w_bd, w_bg, w_out, ffn_pre, ffn_post, w_rg, b_rg, w_re, b_re, w_eg, w_eu, w_ed, sq_c, col_c, out):
    PLAN = plan_products()
    ORDER = {name: n for n, (name, _) in enumerate(PLAN)}
    TURN, seen = {}, {"v": 0, "a": 0}
    for name, who in PLAN:
        seen[who] += 1
        TURN[name] = (who, seen[who])

    with ExitStack() as ctx:
        def sb(name, shape, dt=F32):
            return ctx.enter_context(nc.sbuf_tensor(name, shape, dt))

        def sem(name):
            return ctx.enter_context(nc.semaphore(name))

        sq = sb("sq", [P, N_SQ, P])
        col = sb("col", [P, N_COL])
        rows = sb("rows", [N_ROWS, P])
        cols = sb("cols", [P, N_ROWS])
        mod = sb("mod", [P, 32])
        GATE = sb("GATE", [P, 3, 512])
        acol = sb("acol", [P, 2, KD])
        ccol = sb("ccol", [P, KD])
        bada = sb("bada", [12, 512])
        ones = sb("ones", [P, P])
        wroute = sb("wroute", [P, KD, 20])
        small_in = sb("small_in", [P, 20 + 64 + 16])
        X = sb("X", [P, TB, D])
        XN = sb("XN", [P, TB, D])
        HT = sb("HT", [P, KD, T])
        QKI = sb("QKI", [P, 12, T])
        KI = sb("KI", [P, T])
        V = sb("V", [P, TB, HW])
        C = sb("C", [P, 12, T])
        SZ = sb("SZ", [P, TB, HW])
        W = sb("W", [P, 3, KD, 512])
        AR = sb("AR", [P, 2, KD, 256])
        g1p = sb("g1p", [P, D])
        g2p = sb("g2p", [P, D])
        IS = sb("IS", [P, 1152])
        IW = sb("IW", [P, 1152])
        sc = sb("sc", [P, 16, 32])
        st = sb("st", [P, 40])
        S = sb("S", [P, 4, DH])
        small = sb("small", [P, TB, 24])

        ps = [ctx.enter_context(nc.psum_tensor(f"ps{n}", [P, 512], F32)) for n in range(BANKS)]

        ident = sq[:, M_ID, :]
        QT, KT, IQ = QKI[:, 0:4, :], QKI[:, 4:8, :], QKI[:, 8:12, :]
        cosT, sinT = SZ[:, 0, :], SZ[:, 1, :]
        ropeT = SZ[:, 2:4, :]
        KTOK = XN[:, 0:2, :].rearrange("p a (b n) -> p (a b) n", n=HW)
        VTOK = XN[:, 2:4, :].rearrange("p a (b n) -> p (a b) n", n=HW)
        Xf = X[:, :, :].rearrange("p a n -> p (a n)")
        ARf = AR[:, :, :, :].rearrange("p a k n -> p (a k n)")
        raw = IS[:, 0:1024].rearrange("p (a n) -> p a n", n=512)

        consts_in, rows_in, x_in, pos_in, bias_in, small_sem = (sem(n) for n in (
            "consts_in", "rows_in", "x_in", "pos_in", "bias_in", "small_sem"))
        post1_in, post2_in = sem("post1_in"), sem("post2_in")
        weights_in = [sem(f"weights_in{n}") for n in range(3)]
        ada_in = [sem(f"ada_in{n}") for n in range(2)]
        ada_early = [sem(f"ada_early{n}") for n in range(2)]
        product_done, vector_took, scalar_took = sem("product_done"), sem("vector_took"), sem("scalar_took")
        vector_step, scalar_step, pool_step = sem("vector_step"), sem("scalar_step"), sem("pool_step")
        weights_used, ada_used = sem("weights_used"), sem("ada_used")
        names = ("ones_set ccol_done ada_summed stats1 rms1 rstd1 xn_done acol_done angle_set trig_set "
                 "raw_set cos_part rope_set conv_raw conv_sum conv_set z_set square_set normed tok_set "
                 "gate_exp gate_e gate_ln gbeta_set gcum_set egc_set beg_set relu_used diff_set clip_set "
                 "decay_set decay_masked qg_set l_set lm_set x0_set y_set kd_set nw_set vn_set state_set "
                 "g_operands neg_set prob_set dsa_set gdn_sq gdn_sum gdn_root gdn_set qk_set sig_set "
                 "merged_set x_again y_copied y_stat y_root xn2_done route_exp route_set out_done post_norm "
                 "mse_done mse_root x1_done y_sum").split()
        s = {n: sem(n) for n in names}

        def bank(name):
            return ps[ORDER[name] % BANKS][:, :]

        def product_ready(eng, name):
            eng.wait_ge(product_done, ORDER[name] + 1)

        def took(name, ins):
            who, turn = TURN[name]
            ins.then_inc(vector_took if who == "v" else scalar_took, 1)

        def wcols(c0, n=512):
            return w_in.rearrange("(k p) n -> p k n", p=P)[:, :, c0:c0 + n]

        WBLOCKS = ["q", "k", "v", "iq", "small", "gq", "gk", "gv", "z",
                   "ga0", "gb0", "br0", "ga1", "gb1", "br1", "out0", "out1"]
        WSLOTS = [0, 1, 2, 0, 1, 2, 0, 1, 2, 0, 0, 0, 1, 2, 0, 1, 2]
        WAT = {n: i for i, n in enumerate(WBLOCKS)}
        NW_BLOCKS = len(WBLOCKS)
        WPARTS = {"small": 3, "br0": 2, "br1": 2}
        WREADY = {}
        fill = [0, 0, 0]
        for n, k in zip(WBLOCKS, WSLOTS):
            fill[k] += 16 * (4 if n == "small" else WPARTS.get(n, 1))
            WREADY[n] = (k, fill[k])

        def wslot(name):
            return W[:, WSLOTS[WAT[name]]]

        def weights_ready(eng, name):
            slot, v = WREADY[name]
            eng.wait_ge(weights_in[slot], v)

        Wf = W[:, :, :, :].rearrange("p a k n -> p (a k n)")
        HALF = 3 * KD * 512 // 2
        def expert_gu(slot):
            return Wf[:, slot * HALF:slot * HALF + KD * 512].rearrange("p (k u f) -> p k u f", u=2, k=KD)
        def expert_d(slot):
            return Wf[:, slot * HALF + KD * 512:(slot + 1) * HALF].rearrange("p (k n) -> p k n", k=2)
        tile_stored = [sem(f"tile_stored{n}") for n in range(2)]
        gate_up_in = [sem(f"gate_up_in{n}") for n in range(2)]
        down_in = [sem(f"down_in{n}") for n in range(2)]
        rows_gathered = [sem(f"rows_gathered{n}") for n in range(2)]
        (turned, h_scalar, h_vector, gu_done, silu_done, act_done, act_turned, act_back, down_done, out_scalar,
         out_vector, table_zero, zeros_set, rows_stored, address_set, scattered, order_in, experts_set,
         ) = (sem(n) for n in (
            "turned h_scalar h_vector gu_done silu_done act_done act_turned act_back down_done out_scalar "
            "out_vector table_zero zeros_set rows_stored address_set scattered order_in experts_set").split())
        both_in = [sem(f"both_in{t}") for t in range(TB)]

        xs_d = nc.dram_tensor("xs_rows", (T, D), F32, kind="Internal").ap()
        place_d = nc.dram_tensor("place_token", (P * TILES, 1), I32, kind="Internal").ap()
        yd = nc.dram_tensor("place_rows", (P * TILES, D), F32, kind="Internal").ap()

        def wait_from(eng, what, value):
            if not isinstance(value, int) or value > 0:
                eng.wait_ge(what, value)

        def steps(eng, step):
            for j in range(3):
                step(j, j % 2)
            pairs = (TILES - 5) // 2
            with eng.Fori(0, pairs) as i:
                for k in range(2):
                    step(i * 2 + (3 + k), (3 + k) % 2)
            for j in range(3 + 2 * pairs, TILES):
                step(j, j % 2)

        Y1 = QKI[:, 0:8, :].rearrange("p (t u) n -> p t (u n)", u=2)
        Y2 = Wf[:, 0:TB * D].rearrange("p (t n) -> p t n", n=D)
        GX = V[:, :, :].rearrange("p (s u) n -> p s (u n)", s=2)
        HX = [C[:, 2 * n:2 * n + 2, :].rearrange("p a (k n) -> p (a k) n", n=P) for n in range(2)]
        YT = [C[:, 4 + 2 * n:6 + 2 * n, :].rearrange("p a n -> p (a n)") for n in range(2)]
        SI = [C[:, 8, 256 * n:256 * n + 256] for n in range(2)]
        AC = [C[:, 9, 256 * n:256 * n + 256] for n in range(2)]
        ACT_T = [C[:, 10, 256 * n:256 * n + 256] for n in range(2)]
        eid = sb("eid", [P, 32], I32)
        address = sb("address", [P, 2 * TB], I32)
        token = sb("token", [P, TB], I32)
        order = sb("order", [P, TILES], I32)
        def conv_raw(m):
            return IS[:, (m % 2) * 516:(m % 2) * 516 + 515]
        early = [W[:, 2, 4 * n:4 * n + 4, :].rearrange("p k (u n) -> p (k u) n", u=2) for n in range(2)]
        def ada_slot(k):
            return early[k % 2] if k in (2, 3, 6, 7) else AR[:, k % 2]
        def ada_sem(k):
            return ada_early[k % 2] if k in (2, 3, 6, 7) else ada_in[k % 2]
        def ada_ready(eng, k):
            loads = k // 4 + 1 if k < 8 else k // 2 - 1
            eng.wait_ge(ada_sem(k), 16 * loads)
        def modrow(n, k):
            return (HT[0:1, 6 + k % 2, :] if n < 4 else XN[0:1, k % 2, 0:512])
        sv = lambda n: IW[:, 4 * n:4 * n + 4]
        ada_sum = IW[:, 0:1024].rearrange("p (a n) -> p a n", n=512)

        def gspace(g):
            base = Xf[:, g * 2048:(g + 1) * 2048]
            b2 = ARf[:, g * 2048:(g + 1) * 2048]
            b3 = C[:, 8 + 2 * g:10 + 2 * g, :].rearrange("p a n -> p (a n)")
            return {
                "E1": base[:, 0:512], "E2": base[:, 512:1024], "XU": base[:, 1024:1536], "XL": base[:, 1536:2048],
                "D": b2[:, 0:512], "LM": b2[:, 512:1024], "EG": b2[:, 1024:1536],
                "QG": ARf[:, 1536:2048], "NW": ARf[:, 3584:4096],
                "KBG": b3[:, 0:256], "VB": b3[:, 256:512], "KDEC": b3[:, 512:768], "VN": b3[:, 768:1024],
            }
        G = [gspace(g) for g in range(2)]

        def heads(ap, n=4):
            return ap.rearrange("p (h n) -> p h n", h=n)

        def of_group(ap, g):
            return ap.rearrange("p (m k n) -> p m k n", k=2, n=DH)[:, :, g, :]

        def scal(name, c, g):
            return GSC[name][:, 8 * c + g:8 * c + 8:2]

        OG = IQ
        OD = W[:, 2, 0:4, :]
        OAT, OGT = C[:, 4:8, :], C[:, 8:12, :]
        GATES = {("ga", m): W[:, 2, 4 + m, :] for m in range(4)}
        GATES.update({("gb", m): GATE[:, m, :] if m < 3 else KI[:, :] for m in range(4)})
        GATES.update({("ga", 4 + m): ARf[:, 512 * m:512 * m + 512] for m in range(4)})
        GATES.update({("gb", 4 + m): ARf[:, 2048 + 512 * m:2560 + 512 * m] for m in range(4)})
        MT = QKI[:, 0:8, :]
        YS = XN
        Wa = W[:, 1].rearrange("p k n -> p (k n)")
        SM = [Wa[:, n * 512:(n + 1) * 512] for n in range(3)]
        PR = [Wa[:, (3 + n) * 512:(4 + n) * 512] for n in range(2)]
        PT = [Wa[:, (5 + n) * 512:(6 + n) * 512] for n in range(2)]
        AOFF = {1: 0, 2: 256, 3: 640}
        def scores(t, b):
            return t[:, AOFF[b]:AOFF[b] + P * (b + 1)]
        TODO = [(b, h) for b in range(TB) for h in range(H)]

        GSC = {n: sc[:, i, :] for i, n in enumerate(
            "beta g gc egc bgc nbgc t0 t1 t2 t3 osum orr wsc".split())}
        ssq, rstd = st[:, 0:4], st[:, 4:8]
        negm, rsum, rinv, rmax = st[:, 8:12], st[:, 12:16], st[:, 16:20], st[:, 20:24]

        block = ctx.enter_context(nc.Block())

        @block.sync
        def _(sp):
            def ada(n):
                for k in (2 * n, 2 * n + 1):
                    last = k - 4 if k < 10 else k - 2
                    if last >= 0:
                        sp.wait_ge(ada_used, last + 1)
                    sp.dma_start(ada_slot(k), w_ada.rearrange("(k p) n -> p k n", p=P)[:, :, 256 * k:256 * k + 256])\
                      .then_inc(ada_sem(k), 16)

            def weights(name):
                i = WAT[name]
                before = [j for j in range(i) if WSLOTS[j] == WSLOTS[i]]
                if before:
                    sp.wait_ge(weights_used, before[-1] + 1)
                dst, done = wslot(name), weights_in[WSLOTS[i]]
                if name == "small":
                    for at, c0, n in ((0, C_IK, DH), (DH, C_IK, DH), (2 * DH, C_IW, H), (2 * DH + H, C_B, 2 * H)):
                        sp.dma_start(dst[:, :, at:at + n], wcols(c0, n)).then_inc(done, 16)
                elif name.startswith("br"):
                    u = int(name[2]) * 512
                    for k, w in enumerate((w_bd, w_bg)):
                        sp.dma_start(dst[:, 4 * k:4 * k + 4, :], w.rearrange("(k p) n -> p k n", p=P)[:, :, u:u + 512])\
                          .then_inc(done, 16)
                elif name.startswith("out"):
                    u = int(name[3]) * 512
                    sp.dma_start(dst, w_out.rearrange("(k p) n -> p k n", p=P)[:, :, u:u + 512]).then_inc(done, 16)
                else:
                    at = {"q": C_Q, "k": C_K, "v": C_V, "iq": C_IQ, "gq": C_GQ, "gk": C_GQ + HW, "gv": C_GQ + 2 * HW,
                          "z": C_Z, "ga0": C_GA, "ga1": C_GA + 512, "gb0": C_GB, "gb1": C_GB + 512}[name]
                    sp.dma_start(dst, wcols(at)).then_inc(done, 16)

            sp.dma_start(rows[R_C:R_C + KD, :], cond.rearrange("(k n) -> k n", n=P)).then_inc(rows_in, 16)
            sp.dma_start(rows[R_PRE1:R_PRE1 + KD, :], mix_pre.rearrange("(k n) -> k n", n=P)).then_inc(rows_in, 16)
            sp.dma_start(rows[R_PRE2:R_PRE2 + KD, :], ffn_pre.rearrange("(k n) -> k n", n=P)).then_inc(rows_in, 16)
            sp.dma_start(rows[R_CONV:N_ROWS, :], conv_w.rearrange("j (m n) -> (j m) n", n=P)).then_inc(rows_in, 16)
            sp.dma_start(sq[:, :, :], sq_c.rearrange("p (a n) -> p a n", n=P)).then_inc(consts_in, 16)
            sp.dma_start(col[:, :], col_c).then_inc(consts_in, 16)
            ada(0)
            sp.dma_start(X[:, 0:2, :], x[0:256, :].rearrange("(t p) d -> p t d", p=P)).then_inc(x_in, 16)
            ada(1)
            sp.dma_start(X[:, 2:4, :], x[256:512, :].rearrange("(t p) d -> p t d", p=P)).then_inc(x_in, 16)
            for n in range(2, 4):
                ada(n)
            for name in ("q", "k"):
                weights(name)
            sp.wait_ge(ada_used, 8)
            weights("v")
            for before, name in (((), "iq"), ((), "small"), ((), "gq"), ((4, 5), "gk"), ((6, 7), "gv"), ((8, 9), "z")):
                for n in before:
                    ada(n)
                weights(name)
            ada(10)
            ada(11)
            for name in ("ga0", "gb0", "br0"):
                weights(name)
            sp.wait_ge(product_done, ORDER[("ot", 0, 3)] + 1)
            weights("ga1")
            sp.wait_ge(s["gdn_set"], 1)
            sp.dma_start(X[:, :, :], x.rearrange("(t p) d -> p t d", p=P)).then_inc(s["x_again"], 16)
            sp.wait_ge(s["merged_set"], 8)
            for name in ("gb1", "br1", "out0", "out1"):
                weights(name)
            sp.wait_ge(s["xn_done"], 2 * TB)
            sp.dma_start(xs_d.rearrange("(t p) d -> p t d", p=P), XN[:, :, :]).then_inc(rows_stored, 16)
            sp.wait_ge(weights_used, NW_BLOCKS)
            sp.wait_ge(experts_set, 1)
            def expert_of(j):
                at = slice(j, j + 1) if isinstance(j, int) else bass.ds(j, 1)
                return sp.value_load(eid[0:1, at], min_val=0, max_val=NE - 1)

            def load_gate_up(j, slot):
                e = expert_of(j)
                wait_from(sp, gu_done, j - 1)
                for u, w in enumerate((w_eg, w_eu)):
                    sp.dma_start(expert_gu(slot)[:, :, u, :], w[bass.ds(e, 1)].rearrange("i (k p) f -> p (i k) f", p=P))\
                      .then_inc(gate_up_in[slot], 16)

            def load_down(j, slot):
                e = expert_of(j)
                wait_from(sp, down_done, j - 1)
                sp.dma_start(expert_d(slot), w_ed[bass.ds(e, 1)].rearrange("i (k p) n -> p (i k) n", p=P))\
                  .then_inc(down_in[slot], 16)

            def expert(j, slot):
                if isinstance(j, int) and j == 1:
                    sp.wait_ge(rows_gathered[1], 16)
                load_gate_up(j, slot)
                if not isinstance(j, int) or j >= 1:
                    load_down(j - 1, 1 - slot)
            steps(sp, expert)
            load_down(TILES - 1, (TILES - 1) % 2)
            for t in range(TB):
                sp.wait_ge(s["post_norm"], t + 1)
                sp.dma_start(out[t * P:(t + 1) * P, :], XN[:, t, :]).then_inc(s["out_done"], 16)
            sp.wait_ge(s["out_done"], 16 * TB)

        @block.gpsimd
        def _(pool):
            done = [0]

            def link(ins):
                done[0] += 1
                ins.then_inc(pool_step, 1)
                pool.wait_ge(pool_step, done[0])

            pool.memset(ones[:, :], 1.0).then_inc(s["ones_set"], 1)
            pool.wait_ge(consts_in, 32)
            pool.wait_ge(s["trig_set"], 2)
            for n in range(13):
                pool.wait_ge(s["raw_set"], n + 1)
                if n >= 2:
                    pool.wait_ge(s["rope_set"], n - 1)
                pool.tensor_tensor(ropeT[:, n % 2, :], raw[:, n % 2, :], cosT, ALU.mult).then_inc(s["cos_part"], 1)

            for c in range(TB):
                for g in range(2):
                    u = 2 * c + g
                    A = G[g]
                    if u == 0:
                        pool.wait_ge(s["tok_set"], 8)
                        pool.wait_ge(s["beg_set"], 2)
                    if c > 0:
                        pool.wait_ge(s["vn_set"], u - 1)
                        pool.wait_ge(s["nw_set"], u - 1)
                    pool.tensor_tensor(heads(A["KBG"]), of_group(KTOK[:, c, :], g),
                                       scal("nbgc", c, g).unsqueeze(2).to_broadcast([P, 4, DH]), ALU.mult)\
                        .then_inc(s["g_operands"], 1)
                    pool.tensor_tensor(heads(A["VB"]), of_group(VTOK[:, c, :], g),
                                       scal("beta", c, g).unsqueeze(2).to_broadcast([P, 4, DH]), ALU.mult)\
                        .then_inc(s["g_operands"], 1)
                for g in range(2):
                    u = 2 * c + g
                    A = G[g]
                    pool.wait_ge(s["decay_set"], 4 * c + 3 + g)
                    if c > 0:
                        pool.wait_ge(s["state_set"], u - 1)
                    pool.tensor_tensor(heads(A["KDEC"]), of_group(KTOK[:, c, :], g),
                                       heads(A["E1"])[:, :, P - 1:P].to_broadcast([P, 4, DH]), ALU.mult)\
                        .then_inc(s["kd_set"], 1)
                    pool.wait_ge(s["kd_set"], u + 1)
                    pool.tensor_tensor(heads(A["E1"]), heads(A["E1"]),
                                       sq[:, M_UPPER, :].unsqueeze(1).to_broadcast([P, 4, P]), ALU.mult)\
                        .then_inc(s["decay_masked"], 1)
                for lv in range(1, LEVELS):
                    for g in range(2):
                        A = G[g]
                        if lv == 1:
                            pool.wait_ge(s["l_set"], 2 * c + g + 1)
                        else:
                            pool.wait_ge(product_done, ORDER[("Y", c, lv - 1, g)] + 1)
                        pool.tensor_tensor(heads(A["LM"]), heads(A["E2"]),
                                           sq[:, M_LEVEL + lv, :].unsqueeze(1).to_broadcast([P, 4, P]), ALU.mult)\
                            .then_inc(s["lm_set"], 1)
                if c == 2:
                    pool.wait_ge(s["z_set"], 1)
                    z4 = SZ[:, :, :].rearrange("p t (h n) -> p (t h) n", n=DH)
                    pool.tensor_tensor(z4, z4, small_in[:, 20:84].unsqueeze(1).to_broadcast([P, 32, DH]), ALU.mult)\
                        .then_inc(s["z_set"], 1)

            pool.memset(order[:, :], 0).then_inc(zeros_set, 1)
            pool.wait_ge(zeros_set, 1)
            pool.dma_start(place_d.rearrange("(p j) o -> p (j o)", p=P), order[:, :]).then_inc(table_zero, 16)
            pool.wait_ge(table_zero, 16)
            pool.wait_ge(address_set, 2)
            for k in range(2 * TB):
                pool.indirect_dma_start(place_d, bass.IndirectOffsetOnAxis(address[:, k:k + 1], 0),
                                        token[:, k % TB:k % TB + 1], None).then_inc(scattered, 16)
            pool.wait_ge(scattered, 16 * 2 * TB)
            pool.dma_start(order[:, :], place_d.rearrange("(p j) o -> p (j o)", p=P)).then_inc(order_in, 16)
            pool.wait_ge(order_in, 16)
            pool.wait_ge(rows_stored, 16)
            for j in range(TILES + 4):
                if j < TILES:
                    wait_from(pool, turned, j - 1)
                    pool.indirect_dma_start(GX[:, j % 2, :], None, xs_d,
                                            bass.IndirectOffsetOnAxis(order[:, j:j + 1], 0))\
                        .then_inc(rows_gathered[j % 2], 16)
                if j >= 4:
                    k = j - 4
                    pool.wait_ge(out_scalar, k + 1)
                    pool.wait_ge(out_vector, k + 1)
                    pool.dma_start(yd.rearrange("(p j) d -> j p d", j=TILES)[k], YT[k % 2]).then_inc(tile_stored[k % 2], 16)
            pool.wait_ge(tile_stored[0], 16 * ((TILES + 1) // 2))
            pool.wait_ge(tile_stored[1], 16 * (TILES // 2))
            for t in range(TB):
                for k, dst in enumerate((Y1, Y2)):
                    n = k * TB + t
                    pool.indirect_dma_start(dst[:, t, :], None, yd,
                                            bass.IndirectOffsetOnAxis(address[:, n:n + 1], 0)).then_inc(both_in[t], 16)

        @block.scalar
        def _(act):
            done = [0]

            def link(ins):
                done[0] += 1
                ins.then_inc(scalar_step, 1)
                act.wait_ge(scalar_step, done[0])

            bc = lambda ap, n: ap.unsqueeze(0).to_broadcast([P, n])
            act.dma_start(HT[:, 0, :].bitcast(I32), bc(positions, T)).then_inc(pos_in, 16)
            act.dma_start(bada[:, :], b_ada.rearrange("(k n) -> k n", n=512)).then_inc(bias_in, 16)
            act.dma_start(small_in[:, 0:4], bc(b_rg, NG)).then_inc(small_sem, 16)
            act.dma_start(small_in[:, 4:20], bc(b_re, NE)).then_inc(small_sem, 16)
            act.dma_start(small_in[:, 20:84], bc(gdn_norm, DH)).then_inc(small_sem, 16)
            act.dma_start(small_in[:, 84:92], bc(a_log, H)).then_inc(small_sem, 16)
            act.dma_start(small_in[:, 92:100], bc(dt_bias, H)).then_inc(small_sem, 16)
            act.dma_start(wroute[:, :, 0:4], w_rg.rearrange("(k p) n -> p k n", p=P)).then_inc(small_sem, 16)
            act.dma_start(wroute[:, :, 4:20], w_re.rearrange("(k p) n -> p k n", p=P)).then_inc(small_sem, 16)

            act.wait_ge(vector_took, TURN[("rows",)][1])
            act.activation(ccol[:, :], cols[:, R_C:R_C + KD], ACT.Silu).then_inc(s["ccol_done"], 1)
            act.wait_ge(x_in, 32)
            for t in range(TB):
                act.activation(XN[:, t, :], X[:, t, :], ACT.Square, accum_out=ssq[:, t:t + 1]).then_inc(s["stats1"], 1)
            act.wait_ge(s["stats1"], TB)
            act.wait_ge(consts_in, 32)
            act.activation(rstd, ssq, ACT.Sqrt, bias=col[:, K_EPS:K_EPS + 1], scale=1.0 / D).then_inc(s["rms1"], 1)
            act.wait_ge(s["rstd1"], 1)
            for t in range(TB):
                act.activation(XN[:, t, :], X[:, t, :], ACT.Copy, scale=rstd[:, t:t + 1]).then_inc(s["xn_done"], 1)
            act.dma_start(g1p[:, :], bc(mix_post, D)).then_inc(post1_in, 16)
            act.dma_start(g2p[:, :], bc(ffn_post, D)).then_inc(post2_in, 16)
            act.wait_ge(s["angle_set"], 1)
            act.activation(sinT, HT[:, 1, :], ACT.Sin, scale=col[:, K_SIGN:K_SIGN + 1]).then_inc(s["trig_set"], 1)
            act.activation(cosT, HT[:, 2, :], ACT.Sin, scale=-1.0, bias=col[:, K_HALFPI:K_HALFPI + 1])\
                .then_inc(s["trig_set"], 1)

            def mod_row(n, k):
                product_ready(act, ("ada", n))
                if k >= 2:
                    m = [0, 1, 2, 3, 6, 7, 8, 9][k - 2]
                    act.wait_ge(product_done, ORDER[("adac", m)] + 1)
                ins = act.activation(modrow(n, k), bank(("ada", n))[0:1, :], ACT.Copy)
                took(("ada", n), ins)

            act.wait_ge(s["acol_done"], 1)
            for f in range(1, KD, 2):
                name = ("h1", f)
                product_ready(act, name)
                if f < 3:
                    act.wait_ge(s["trig_set"], 2)
                ins = act.activation(HT[:, f, :], bank(name), ACT.Identity, scale=acol[:, 0, f:f + 1],
                                     bias=mod[:, f:f + 1])
                took(name, ins)

            seq = rotated()
            for n, it in enumerate(seq):
                name = ("rope",) + it
                product_ready(act, name)
                if n >= 2:
                    act.wait_ge(product_done, ORDER[("swap",) + seq[n - 2]] + 1)
                    act.wait_ge(s["cos_part"], n - 1)
                ins = act.activation(raw[:, n % 2, :], bank(name), ACT.Copy)
                took(name, ins)
                act.wait_ge(scalar_took, TURN[name][1])
                act.sem_inc(s["raw_set"], 1)
                if it == ("k", 3):
                    for t in range(TB):
                        product_ready(act, ("v", t))
                        took(("v", t), act.activation(V[:, t, :], bank(("v", t)), ACT.Copy))
            def conv_silu(m):
                act.wait_ge(s["conv_sum"], m + 1)
                act.activation(C[:, m, :], C[:, m, :], ACT.Silu).then_inc(s["conv_set"], 1)
            k = 4
            act.wait_ge(s["cos_part"], 13)
            act.wait_ge(product_done, ORDER[("swap", "ik", 0)] + 1)
            for m in range(12):
                product_ready(act, ("conv", m))
                act.wait_ge(s["conv_raw"], 1)
                if m >= 2:
                    act.wait_ge(s["conv_sum"], m - 1)
                took(("conv", m), act.activation(conv_raw(m)[:, 3:515], bank(("conv", m)), ACT.Copy))
                if m >= 1:
                    conv_silu(m - 1)
                if m % 3 == 2:
                    for n in (4 + 2 * (m // 3), 5 + 2 * (m // 3)):
                        if 6 <= n < 10:
                            mod_row(n, k)
                            k += 1
            conv_silu(11)
            act.wait_ge(s["gate_e"], 1)
            act.activation(GSC["t1"], GSC["t0"], ACT.Exp, scale=-1.0).then_inc(s["gate_exp"], 1)
            act.activation(GSC["beta"], small[:, :, 8:16], ACT.Exp, scale=-1.0).then_inc(s["gate_exp"], 1)
            act.activation(small_in[:, 84:92], small_in[:, 84:92], ACT.Exp).then_inc(s["gate_exp"], 1)
            act.wait_ge(s["gate_exp"], 1)
            act.activation(GSC["t2"], GSC["t1"], ACT.Ln, bias=1.0).then_inc(s["gate_ln"], 1)
            def take_z(t):
                product_ready(act, ("z", t))
                took(("z", t), act.activation(SZ[:, t, :], bank(("z", t)), ACT.Copy))

            act.wait_ge(s["rope_set"], 13)
            take_z(0)
            act.wait_ge(s["conv_set"], 12)
            for n in range(3 * H):
                qb, h = 1 + n // H, n % H
                if n % 3 == 0:
                    m = n // 3
                    if m >= 2:
                        product_ready(act, ("norm", m - 2))
                    act.activation(Xf[:, 1024 + (m % 2) * 512:1536 + (m % 2) * 512], C[:, m, :], ACT.Square)\
                        .then_inc(s["square_set"], 1)
                name = ("idx", qb, h)
                product_ready(act, name)
                if n >= 2:
                    act.wait_ge(s["relu_used"], n - 1)
                w = P * (qb + 1)
                took(name, act.activation(Xf[:, (n % 2) * 512:(n % 2) * 512 + w], bank(name)[:, 0:w], ACT.Relu))
                if n % 3 == 2:
                    m = n // 3
                    name = ("norm", m)
                    product_ready(act, name)
                    if m >= 2:
                        act.wait_ge(s["normed"], m - 1)
                    took(name, act.activation(Xf[:, 2048 + (m % 2) * 512:2560 + (m % 2) * 512], bank(name), ACT.Sqrt,
                                              bias=col[:, K_EPS:K_EPS + 1]))
            take_z(1)
            for t in range(TB):
                product_ready(act, ("ktok", t))
                ins = act.activation(KTOK[:, t, :], bank(("ktok", t)), ACT.Copy)
                took(("ktok", t), ins)
            for t in range(TB):
                product_ready(act, ("vtok", t))
                took(("vtok", t), act.activation(VTOK[:, t, :], bank(("vtok", t)), ACT.Copy))
            act.wait_ge(scalar_took, TURN[("vtok", 3)][1])
            act.sem_inc(s["tok_set"], 8)
            take_z(2)
            take_z(3)
            act.wait_ge(s["gcum_set"], 1)
            act.activation(GSC["egc"], GSC["gc"], ACT.Exp).then_inc(s["egc_set"], 1)
            def attend(n):
                for kind, b, h in attention(n, "s"):
                    w = P * (b + 1)
                    act.wait_ge(s["neg_set"], n + 1)
                    if n >= 2:
                        product_ready(act, attention(n - 1, "pt")[0])
                    act.activation(PR[n % 2][:, 0:w], SM[n % 3][:, 0:w], ACT.Exp, scale=DH ** -0.5,
                                   bias=negm[:, n % 4:n % 4 + 1], accum_out=rsum[:, n % 4:n % 4 + 1])\
                        .then_inc(s["prob_set"], 1)
                for name in attention(n, "pt"):
                    w = P * (name[1] + 1)
                    product_ready(act, name)
                    if n >= 3:
                        product_ready(act, attention(n - 1, "pv")[0])
                    took(name, act.activation(PT[(n - 1) % 2][:, 0:w], bank(name)[:, 0:w], ACT.Copy))

            def early_gate(n):
                name = EARLY_GATES[n]
                product_ready(act, name)
                took(name, act.activation(GATES[name], bank(name), ACT.Copy))

            for c in range(TB):
                for g in range(2):
                    act.wait_ge(s["clip_set"], 4 * c + 2 * g + 1)
                    if c + g == 0:
                        act.wait_ge(s["relu_used"], 24)
                    act.activation(G[g]["E2"], G[g]["XL"], ACT.Exp, scale=-1.0).then_inc(s["decay_set"], 1)
                for g in range(2):
                    u, A = 2 * c + g, G[g]
                    act.wait_ge(s["clip_set"], 4 * c + 2 * g + 2)
                    act.activation(A["E1"], A["XU"], ACT.Exp).then_inc(s["decay_set"], 1)
                for g in range(2):
                    u, A = 2 * c + g, G[g]
                    name = ("gcb", c, g)
                    product_ready(act, name)
                    if c > 0:
                        act.wait_ge(s["state_set"], u - 1)
                        act.wait_ge(s["qg_set"], u - 1)
                    took(name, act.activation(A["EG"], bank(name), ACT.Exp))
                for lv in range(LEVELS):
                    if lv > 0:
                        for g in range(2):
                            A, name = G[g], ("Y", c, lv, g)
                            product_ready(act, name)
                            took(name, act.activation(A["D"], bank(name), ACT.Copy))
                    attend(first_step(c, lv))
                    if lv == 0:
                        early_gate(2 * c)
                    for g in range(2):
                        A, name = G[g], ("T", c, lv, g)
                        product_ready(act, name)
                        took(name, act.activation(A["XU"], bank(name), ACT.Copy))
                    for n in second_step(c, lv):
                        attend(n)
                for g in range(2):
                    A, name = G[g], ("nw", c, g)
                    product_ready(act, name)
                    b = bank(name)
                    rw = slice(64 * g, 64 * g + 64)
                    ins = act.activation(A["NW"][rw, :], b[rw, :], ACT.Copy)
                    took(name, ins)
                    act.wait_ge(scalar_took, TURN[name][1])
                    act.sem_inc(s["nw_set"], 1)
                if c == 0:
                    act.activation(SZ[:, :, :], SZ[:, :, :], ACT.Silu).then_inc(s["z_set"], 1)
                if c == 2:
                    for m in range(4):
                        act.activation(GATES[("ga", m)], GATES[("ga", m)], ACT.Sigmoid).then_inc(s["sig_set"], 1)
                early_gate(2 * c + 1)
                for g in range(2):
                    name = ("o", c, g)
                    product_ready(act, name)
                    took(name, act.activation(of_group(OG[:, c, :], g), heads(bank(name)[:, 0:256]), ACT.Copy))
            act.wait_ge(scalar_took, TURN[("o", 3, 1)][1])
            product_ready(act, ("pv",) + TODO[-1])
            act.activation(V[:, :, :], OG, ACT.Square).then_inc(s["gdn_sq"], 1)
            act.wait_ge(s["gdn_sum"], 1)
            act.activation(GSC["orr"], GSC["osum"], ACT.Sqrt, scale=1.0 / DH, bias=col[:, K_EPS:K_EPS + 1])\
                .then_inc(s["gdn_root"], 1)
            for f in range(4):
                product_ready(act, ("ot", 0, f))
                took(("ot", 0, f), act.activation(OAT[:, f, :], bank(("ot", 0, f)), ACT.Copy))
            for name in (("gb", m) for m in range(4)):
                act.activation(GATES[name], GATES[name], ACT.Sigmoid).then_inc(s["sig_set"], 1)
            for name in ((nm, m) for nm in ("ga", "gb") for m in range(4, KD)):
                product_ready(act, name)
                took(name, act.activation(GATES[name], bank(name), ACT.Sigmoid))
            scratch = SZ[:, 2:4, :].rearrange("p a n -> p (a n)")
            for nm, t in TAIL:
                if nm == "y":
                    act.wait_ge(s["y_copied"], t + 1)
                    act.activation(scratch, YS[:, t, :], ACT.Square, accum_out=ssq[:, t:t + 1]).then_inc(s["y_stat"], 1)
                    act.wait_ge(s["y_stat"], 2 * t + 1)
                    act.activation(rstd[:, t:t + 1], ssq[:, t:t + 1], ACT.Sqrt, bias=col[:, K_EPS:K_EPS + 1],
                                   scale=1.0 / D).then_inc(s["y_root"], 1)
                    act.wait_ge(s["x1_done"], t + 1)
                    act.activation(scratch, X[:, t, :], ACT.Square, accum_out=ssq[:, t:t + 1]).then_inc(s["y_stat"], 1)
                    act.wait_ge(s["y_stat"], 2 * t + 2)
                    act.activation(rstd[:, t:t + 1], ssq[:, t:t + 1], ACT.Sqrt, bias=col[:, K_EPS:K_EPS + 1],
                                   scale=1.0 / D).then_inc(s["mse_root"], 1)
                    act.wait_ge(s["xn2_done"], t + 1)
                    act.activation(XN[:, t, :], X[:, t, :], ACT.Copy, scale=rstd[:, t:t + 1]).then_inc(s["xn_done"], 1)
                elif nm == "h2":
                    name = ("h2", t, 1)
                    product_ready(act, name)
                    for k in range(4):
                        f = 4 + k
                        ins = act.activation(HT[:, f, t * P:(t + 1) * P], bank(name)[:, k * P:(k + 1) * P], ACT.Identity,
                                             scale=acol[:, 1, f:f + 1], bias=mod[:, 16 + f:17 + f])
                    took(name, ins)
            act.wait_ge(s["route_exp"], 1)
            act.activation(GSC["t2"], GSC["t1"], ACT.Exp).then_inc(s["gate_exp"], 1)
            act.wait_ge(s["route_exp"], 2)
            act.activation(GSC["t3"][:, 0:4], GSC["t0"][:, 0:4], ACT.Exp).then_inc(s["gate_exp"], 1)
            def evacuate_h(j, slot):
                act.wait_ge(turned, j + 1)
                wait_from(act, gu_done, j - 1)
                for k in range(4):
                    ins = act.activation(HX[slot][:, k, :], ps[0][:, k * P:(k + 1) * P], ACT.Identity,
                                         scale=acol[:, 1, k:k + 1], bias=mod[:, 16 + k:17 + k])
                ins.then_inc(h_scalar, 1)

            def act_back_step(j, slot):
                act.wait_ge(act_turned, j + 1)
                wait_from(act, down_done, j - 1)
                act.activation(ACT_T[slot], ps[4][:, 0:256], ACT.Copy).then_inc(act_back, 1)

            def evacuate_out(j, slot):
                act.wait_ge(down_done, j + 1)
                wait_from(act, tile_stored[slot], 16 * (j // 2) if isinstance(j, int) else (j - slot) * 8)
                act.activation(YT[slot][:, 0:512], ps[5][:, :], ACT.Copy).then_inc(out_scalar, 1)

            def step(j, slot):
                act.wait_ge(gu_done, j + 1)
                wait_from(act, act_done, j - 1)
                act.activation(SI[slot], ps[2 + slot][:, 0:256], ACT.Silu).then_inc(silu_done, 1)
                if not isinstance(j, int) or j >= 1:
                    act_back_step(j - 1, 1 - slot)
                if not isinstance(j, int) or j < TILES - 1:
                    evacuate_h(j + 1, 1 - slot)
                if not isinstance(j, int) or j >= 1:
                    evacuate_out(j - 1, 1 - slot)
            evacuate_h(0, 0)
            steps(act, step)
            act_back_step(TILES - 1, (TILES - 1) % 2)
            evacuate_out(TILES - 1, (TILES - 1) % 2)
            for t in range(TB + 1):
                if t < TB:
                    act.wait_ge(both_in[t], 32)
                    act.activation(Y1[:, t, :], Y1[:, t, :], ACT.Copy, scale=sv(8)[:, t:t + 1]).then_inc(s["y_set"], 1)
                if t >= 1:
                    act.wait_ge(s["y_sum"], t)
                    act.activation(scratch, Y1[:, t - 1, :], ACT.Square, accum_out=ssq[:, t - 1:t]).then_inc(s["mse_done"], 1)
                    act.wait_ge(s["mse_done"], t)
                    act.activation(rstd[:, t - 1:t], ssq[:, t - 1:t], ACT.Sqrt, bias=col[:, K_EPS:K_EPS + 1], scale=1.0 / D)\
                       .then_inc(s["mse_root"], 1)

        @block.vector
        def _(dve):
            done = [0]

            def link(ins):
                done[0] += 1
                ins.then_inc(vector_step, 1)
                dve.wait_ge(vector_step, done[0])

            def own(name):
                dve.wait_ge(vector_took, TURN[name][1])

            product_ready(dve, ("rows",))
            took(("rows",), dve.tensor_copy(cols[:, :], bank(("rows",))[:, 0:N_ROWS]))
            dve.wait_ge(pos_in, 16)
            dve.wait_ge(consts_in, 32)
            h = [HT[:, n, :] for n in range(5)]
            link(dve.tensor_copy(h[3], h[0].bitcast(I32)))
            link(dve.tensor_scalar(h[3], h[3], col[:, K_FREQ:K_FREQ + 1], None, ALU.mult))
            big = 1.5 * 2.0 ** 23
            link(dve.tensor_scalar(h[4], h[3], 1.0 / (2 * np.pi), big, ALU.mult, ALU.add))
            link(dve.tensor_scalar(h[4], h[4], big, None, ALU.subtract))
            c1 = 6.28125
            c2 = 0.0019340515136718750
            c3 = 2 * np.pi - c1 - c2
            for k in (c1, c2, c3):
                link(dve.scalar_tensor_tensor(h[3], h[4], -k, h[3], ALU.mult, ALU.add))
            lim = 3.1415925
            link(dve.tensor_scalar(h[1], h[3], lim, -lim, ALU.min, ALU.max))
            dve.scalar_tensor_tensor(h[2], h[1], -1.0, h[1], ALU.mult, ALU.max).then_inc(s["angle_set"], 1)

            def ada_sum_block(n):
                for u in range(2):
                    k = 2 * n + u
                    ada_ready(dve, k)
                    dst = ada_sum[:, n % 2, 256 * u:256 * u + 256]
                    for j in range(KD):
                        w = AR[:, k % 2, j, :]
                        if j == 0:
                            ins = dve.tensor_scalar(dst, w, ccol[:, 0:1], None, ALU.mult)
                        else:
                            ins = dve.scalar_tensor_tensor(dst, w, ccol[:, j:j + 1], dst, ALU.mult, ALU.add)
                        if j == KD - 1:
                            ins.then_inc(ada_used, 1)
                        else:
                            link(ins)
                dve.wait_ge(ada_used, 2 * n + 2)
                dve.sem_inc(s["ada_summed"], 1)

            def mod_cols(n):
                j = n if n < 4 else n - 2
                product_ready(dve, ("adac", n))
                took(("adac", n), dve.tensor_copy(mod[:, 4 * j:4 * j + 4], bank(("adac", n))[:, 0:4]))

            for n in range(5):
                if n < 4:
                    product_ready(dve, ("ada", n))
                    if n >= 2:
                        dve.wait_ge(product_done, ORDER[("adac", n - 2)] + 1)
                    took(("ada", n), dve.tensor_copy(modrow(n, n), bank(("ada", n))[0:1, :]))
                if n >= 1:
                    mod_cols(n - 1)
                if n == 1:
                    dve.wait_ge(s["rms1"], 1)
                    dve.reciprocal(rstd, rstd).then_inc(s["rstd1"], 1)
            own(("adac", 3))
            dve.scalar_tensor_tensor(acol[:, 0, :], mod[:, 8:16], 1.0, cols[:, R_PRE1:R_PRE1 + KD], ALU.add, ALU.mult)\
                .then_inc(s["acol_done"], 1)
            dve.wait_ge(s["acol_done"], 1)
            dve.wait_ge(s["trig_set"], 2)
            for f in range(0, KD, 2):
                name = ("h1", f)
                product_ready(dve, name)
                took(name, dve.tensor_scalar(HT[:, f, :], bank(name), acol[:, 0, f:f + 1], mod[:, f:f + 1],
                                             ALU.mult, ALU.add))
            dests = [QKI[:, n, :] for n in range(12)] + [KI[:, :]]
            for n, it in enumerate(rotated()):
                name = ("swap",) + it
                product_ready(dve, name)
                ins = dve.tensor_tensor(dests[n], bank(name), sinT, ALU.mult)
                took(name, ins)
                own(name)
                dve.wait_ge(s["cos_part"], n + 1)
                dve.tensor_tensor(dests[n], dests[n], ropeT[:, n % 2, :], ALU.add).then_inc(s["rope_set"], 1)
            product_ready(dve, ("small",))
            took(("small",), dve.tensor_copy(small[:, :, :], bank(("small",))[:, 0:128].rearrange(
                "p (t n) -> p t n", n=32)[:, :, 0:24]))
            dve.wait_ge(s["cos_part"], 13)
            product_ready(dve, ("swap", "ik", 0))
            for m in range(2):
                ins = dve.memset(conv_raw(m)[:, 0:3], 0.0)
                link(ins) if m == 0 else ins.then_inc(s["conv_raw"], 1)
            for m in range(12):
                dve.wait_ge(scalar_took, TURN[("conv", m)][1])
                r = conv_raw(m)
                for j in range(4):
                    w = cols[:, R_CONV + 12 * j + m:R_CONV + 12 * j + m + 1]
                    if j == 0:
                        ins = dve.tensor_scalar(C[:, m, :], r[:, 0:T], w, None, ALU.mult)
                    else:
                        ins = dve.scalar_tensor_tensor(C[:, m, :], r[:, j:j + T], w, C[:, m, :], ALU.mult, ALU.add)
                    link(ins) if j < 3 else ins.then_inc(s["conv_sum"], 1)
                if m in (6, 9):
                    for n in (2 * (m // 3) + 2, 2 * (m // 3) + 3):
                        mod_cols(n)
                if m % 3 == 0:
                    for n in (4 + 2 * (m // 3), 5 + 2 * (m // 3)):
                        product_ready(dve, ("ada", n - 2))
                        ada_sum_block(n)
                if m % 3 == 2:
                    for n in (4 + 2 * (m // 3), 5 + 2 * (m // 3)):
                        if 6 <= n < 10:
                            continue
                        product_ready(dve, ("ada", n))
                        dst = (g1p if n < 6 else g2p)[:, (n % 2) * 512:(n % 2) * 512 + 512]
                        dve.wait_ge(post1_in if n < 6 else post2_in, 16)
                        took(("ada", n), dve.tensor_tensor(dst, bank(("ada", n)), dst, ALU.mult))
            own(("adac", 9))
            link(dve.scalar_tensor_tensor(acol[:, 1, :], mod[:, 24:32], 1.0, cols[:, R_PRE2:R_PRE2 + KD],
                                          ALU.add, ALU.mult))
            t3 = lambda n: GSC[n].rearrange("p (t h) -> p t h", h=H)
            own(("small",))
            link(dve.tensor_scalar(t3("wsc"), small[:, :, 0:8], (H * DH) ** -0.5, None, ALU.mult))
            dve.wait_ge(small_sem, 16 * 7)
            link(dve.tensor_tensor(t3("t3"), small[:, :, 16:24], small_in[:, 92:100].unsqueeze(1).to_broadcast([P, TB, H]),
                                   ALU.add))
            dve.scalar_tensor_tensor(GSC["t0"], GSC["t3"], -1.0, GSC["t3"], ALU.mult, ALU.max).then_inc(s["gate_e"], 1)
            dve.wait_ge(s["gate_exp"], 3)
            link(dve.tensor_scalar(GSC["beta"], GSC["beta"], 1.0, None, ALU.add))
            dve.reciprocal(GSC["beta"], GSC["beta"]).then_inc(s["beg_set"], 1)
            dve.wait_ge(s["gate_ln"], 1)
            link(dve.scalar_tensor_tensor(GSC["t3"], GSC["t3"], 0.0, GSC["t2"], ALU.max, ALU.add))
            dve.scalar_tensor_tensor(t3("g"), t3("t3"), -1.0, small_in[:, 84:92].unsqueeze(1).to_broadcast([P, TB, H]),
                                     ALU.mult, ALU.mult).then_inc(s["gbeta_set"], 1)
            product_ready(dve, ("gc",))
            took(("gc",), dve.tensor_copy(GSC["gc"], bank(("gc",))[:, 0:32]))
            own(("gc",))
            dve.sem_inc(s["gcum_set"], 1)
            for n in range(3 * H):
                b, h_ = 1 + n // H, n % H
                w = P * (b + 1)
                name = ("idx", b, h_)
                dve.wait_ge(scalar_took, TURN[name][1])
                r = Xf[:, (n % 2) * 512:(n % 2) * 512 + w]
                wt = GSC["wsc"][:, 8 * b + h_:8 * b + h_ + 1]
                if h_ == 0:
                    ins = dve.tensor_scalar(scores(IS, b), r, wt, None, ALU.mult)
                else:
                    dve.wait_ge(s["relu_used"], n)
                    ins = dve.scalar_tensor_tensor(scores(IS, b), r, wt, scores(IS, b), ALU.mult, ALU.add)
                ins.then_inc(s["relu_used"], 1)
                if h_ == H - 1:
                    dve.wait_ge(s["relu_used"], n + 1)
                    dia = scores(IS, b)[:, w - P:w]
                    link(dve.tensor_tensor(dia, dia, sq[:, M_CAUSAL, :], ALU.add))
                if n % 3 == 2:
                    m = n // 3
                    name = ("norm", m)
                    dve.wait_ge(scalar_took, TURN[name][1])
                    r = Xf[:, 2048 + (m % 2) * 512:2560 + (m % 2) * 512]
                    link(dve.reciprocal(r, r))
                    dve.scalar_tensor_tensor(C[:, m, :], C[:, m, :], DH ** -0.5 if m < 4 else 1.0, r, ALU.mult, ALU.mult)\
                       .then_inc(s["normed"], 1)
            dve.wait_ge(s["egc_set"], 1)
            dve.wait_ge(s["beg_set"], 1)
            dve.scalar_tensor_tensor(GSC["nbgc"], GSC["beta"], -1.0, GSC["egc"], ALU.mult, ALU.mult)\
               .then_inc(s["beg_set"], 1)
            def topk_round(b, r):
                src = scores(IS, b) if r == 0 else scores(IW, b)
                link(dve.max(out=st[:, 24:32], in_=src))
                link(dve.match_replace(out=scores(IW, b), in_to_replace=st[:, 24:32], in_values=src, imm_value=FAR))
                if r == NKEEP // 8 - 1:
                    link(dve.tensor_tensor(scores(IW, b), scores(IW, b), scores(IS, b), ALU.is_equal))
                    link(dve.tensor_scalar(scores(IW, b), scores(IW, b), NEG, None, ALU.mult))
            rounds = [(b, r) for b in range(1, TB) for r in range(NKEEP // 8)]
            dve.wait_ge(s["normed"], 8)

            def attend(n):
                for name in attention(n, "s"):
                    b = name[1]
                    w = P * (b + 1)
                    product_ready(dve, name)
                    if n >= 3:
                        dve.wait_ge(s["prob_set"], n - 2)
                    mask = sq[:, M_CAUSAL, :] if b == 0 else scores(IW, b)
                    took(name, dve.tensor_tensor_reduce(SM[n % 3][:, 0:w], bank(name)[:, 0:w], mask, 1.0, FAR, ALU.add,
                                                        ALU.max, rmax[:, n % 4:n % 4 + 1]))
                    own(name)
                    dve.tensor_scalar(negm[:, n % 4:n % 4 + 1], rmax[:, n % 4:n % 4 + 1], -DH ** -0.5, None, ALU.mult)\
                       .then_inc(s["neg_set"], 1)

            def finish_attend(n):
                for name in attention(n, "pv"):
                    _, b, h_ = name
                    m = n - 2
                    dve.wait_ge(s["prob_set"], m + 1)
                    link(dve.reciprocal(rinv[:, m % 4:m % 4 + 1], rsum[:, m % 4:m % 4 + 1]))
                    product_ready(dve, name)
                    took(name, dve.tensor_scalar(OD[:, b, DH * h_:DH * h_ + DH], bank(name)[:, 0:DH],
                                                 rinv[:, m % 4:m % 4 + 1], None, ALU.mult))
                    own(name)
                    dve.sem_inc(s["dsa_set"], 1)

            link(dve.memset(S[:, :, :], 0.0))
            turn = 0
            for c_ in range(TB):
                for g in range(2):
                    u, A = 2 * c_ + g, G[g]
                    if c_ > 0:
                        dve.wait_ge(s["diff_set"], u)
                    dve.tensor_copy(heads(A["LM"]), scal("g", c_, g).unsqueeze(2).to_broadcast([P, 4, P]))\
                       .then_inc(s["diff_set"], 1)
                for g in range(2):
                    A, name = G[g], ("gcb", c_, g)
                    product_ready(dve, name)
                    link(dve.tensor_tensor(heads(A["D"]), heads(bank(name)),
                                           scal("gc", c_, g).unsqueeze(2).to_broadcast([P, 4, P]), ALU.subtract))
                    dve.tensor_scalar(A["XL"], A["D"], 0.0, None, ALU.max).then_inc(s["clip_set"], 1)
                    dve.tensor_scalar(A["XU"], A["D"], 0.0, None, ALU.min).then_inc(s["clip_set"], 1)
                for g in range(2):
                    A, name = G[g], ("kk", c_, g)
                    product_ready(dve, name)
                    dve.wait_ge(s["decay_set"], 4 * c_ + g + 1)
                    for hh in range(4):
                        hp = slice(hh * P, hh * P + P)
                        ins = dve.scalar_tensor_tensor(A["E2"][:, hp], bank(name)[:, hp], scal("beta", c_, g)[:, hh:hh + 1],
                                                       A["E2"][:, hp], ALU.mult, ALU.mult)
                    took(name, ins)
                    own(name)
                    dve.sem_inc(s["l_set"], 1)
                    link(dve.tensor_tensor(heads(A["XL"]), heads(A["E2"]),
                                           sq[:, M_LEVEL, :].unsqueeze(1).to_broadcast([P, 4, P]), ALU.mult))
                    dve.tensor_tensor(heads(A["XL"]), ident.unsqueeze(1).to_broadcast([P, 4, P]), heads(A["XL"]),
                                      ALU.subtract).then_inc(s["x0_set"], 1)
                for g in range(2):
                    u, A = 2 * c_ + g, G[g]
                    dve.wait_ge(scalar_took, TURN[("gcb", c_, g)][1])
                    rw = slice(64 * g, 64 * g + 64)
                    dve.tensor_tensor(heads(A["QG"])[rw], C[rw, 0:4, c_ * P:(c_ + 1) * P], heads(A["EG"])[rw], ALU.mult)\
                       .then_inc(s["qg_set"], 1)
                for g in range(2):
                    u, A = 2 * c_ + g, G[g]
                    name = ("qk", c_, g)
                    product_ready(dve, name)
                    dve.wait_ge(s["decay_masked"], u + 1)
                    took(name, dve.tensor_tensor(A["E1"], bank(name), A["E1"], ALU.mult))
                own(("qk", c_, 1))
                dve.sem_inc(s["qk_set"], 1)
                for lv in range(LEVELS):
                    attend(first_step(c_, lv))
                    if lv > 0:
                        for g in range(2):
                            name, A = ("Z", c_, lv, g), G[g]
                            product_ready(dve, name)
                            took(name, dve.tensor_tensor(A["XL"], A["XL"], bank(name), ALU.subtract))
                    finish_attend(first_step(c_, lv))
                    for n in second_step(c_, lv):
                        attend(n)
                        finish_attend(n)
                    for _ in range(3 if lv > 0 else 1):
                        if turn < len(rounds):
                            topk_round(*rounds[turn])
                            turn += 1
                for g in range(2):
                    A, name = G[g], ("vn", c_, g)
                    product_ready(dve, name)
                    took(name, dve.tensor_copy(A["VN"], bank(name)[:, 0:256]))
                    own(name)
                    dve.sem_inc(s["vn_set"], 1)
                for g in range(2):
                    if c_ < TB - 1:
                        A = G[g]
                        name = ("st", c_, g)
                        product_ready(dve, name)
                        bk = bank(name)
                        rw = slice(64 * g, 64 * g + 64)
                        link(dve.tensor_tensor(S[rw], S[rw], heads(A["EG"])[rw, :, P - 1:P].to_broadcast([64, 4, DH]),
                                               ALU.mult))
                        ins = dve.tensor_tensor(S[rw], S[rw], heads(bk[:, 0:256])[rw], ALU.add)
                        took(name, ins)
                        own(name)
                        dve.sem_inc(s["state_set"], 1)
            assert turn == len(rounds)
            o4 = OG.rearrange("p t (h n) -> p (t h) n", n=DH)
            dve.wait_ge(s["gdn_sq"], 1)
            dve.tensor_reduce(GSC["osum"], V[:, :, :].rearrange("p t (h n) -> p (t h) n", n=DH), AX.X, ALU.add)\
               .then_inc(s["gdn_sum"], 1)
            dve.wait_ge(s["gdn_root"], 1)
            link(dve.reciprocal(GSC["orr"], GSC["orr"]))
            link(dve.tensor_tensor(o4, o4, GSC["orr"].unsqueeze(2).to_broadcast([P, 32, DH]), ALU.mult))
            dve.wait_ge(s["z_set"], 2)
            dve.tensor_tensor(OG, OG, SZ[:, :, :], ALU.mult).then_inc(s["gdn_set"], 1)
            def merge(nm, f):
                gt = "g" + nm[1]
                product_ready(dve, (nm, f))
                if f < 4:
                    dve.wait_ge(s["sig_set"], (1 if nm == "ya" else 5) + f)
                else:
                    dve.wait_ge(scalar_took, TURN[(gt, f)][1])
                gate = GATES[(gt, f)]
                took((nm, f), dve.tensor_tensor(MT[:, f, :] if nm == "ya" else gate, gate, bank((nm, f)), ALU.mult))
                own((nm, f))
                if nm == "ya":
                    dve.sem_inc(s["merged_set"], 1)
                else:
                    dve.tensor_tensor(MT[:, f, :], MT[:, f, :], gate, ALU.add).then_inc(s["merged_set"], 1)

            for f in range(4):
                merge("ya", f)
            for f in range(4):
                product_ready(dve, ("ot", 1, f))
                took(("ot", 1, f), dve.tensor_copy(OGT[:, f, :], bank(("ot", 1, f))))
            for f in range(4):
                merge("yb", f)
            for f in range(4, KD):
                merge("ya", f)
                merge("yb", f)
            dve.wait_ge(s["x_again"], 16)
            RL = IS[:, 0:80].rearrange("p (t n) -> p t n", n=20)
            for nm, t in TAIL:
                if nm == "y":
                    for u in range(2):
                        name = ("y", t, u)
                        product_ready(dve, name)
                        took(name, dve.tensor_copy(YS[:, t, 512 * u:512 * u + 512], bank(name)))
                    own(("y", t, 1))
                    dve.sem_inc(s["y_copied"], 1)
                    dve.wait_ge(s["y_root"], t + 1)
                    r = rstd[:, t:t + 1]
                    link(dve.reciprocal(r, r))
                    link(dve.scalar_tensor_tensor(YS[:, t, :], YS[:, t, :], r, g1p[:, :], ALU.mult, ALU.mult))
                    dve.tensor_tensor(X[:, t, :], X[:, t, :], YS[:, t, :], ALU.add).then_inc(s["x1_done"], 1)
                    dve.wait_ge(s["mse_root"], t + 1)
                    dve.reciprocal(r, r).then_inc(s["xn2_done"], 1)
                elif nm == "h2":
                    name = ("h2", t, 0)
                    product_ready(dve, name)
                    for f in range(4):
                        ins = dve.tensor_scalar(HT[:, f, t * P:(t + 1) * P], bank(name)[:, f * P:(f + 1) * P],
                                                acol[:, 1, f:f + 1], mod[:, 16 + f:17 + f], ALU.mult, ALU.add)
                    took(name, ins)
                else:
                    name = ("router", t)
                    product_ready(dve, name)
                    took(name, dve.tensor_tensor(RL[:, t, :], bank(name)[:, 0:20], small_in[:, 0:20], ALU.add))
            R = IS[:, 128:1024].rearrange("p (a t n) -> p a t n", t=TB, n=16)
            def b4(ap):
                return ap.unsqueeze(2).to_broadcast([P, TB, 4])
            tie = col[:, K_TIE:K_TIE + 4].unsqueeze(1).to_broadcast([P, TB, 4])
            own(("router", TB - 1))

            def one_hot(dst, src, m, top):
                link(dve.tensor_tensor(dst, src, b4(top), ALU.is_equal))
                link(dve.tensor_tensor(dst, dst, tie, ALU.mult))
                link(dve.tensor_reduce(m, dst, AX.X, ALU.max))
                link(dve.tensor_tensor(dst, dst, b4(m), ALU.is_equal))

            gl, el = RL[:, :, 0:4], RL[:, :, 4:20]
            link(dve.tensor_reduce(sv(0), gl, AX.X, ALU.max))
            ghot, ingrp, h1, h2, e2 = (R[:, n, :, 0:4] for n in range(5))
            one_hot(ghot, gl, sv(1), sv(0))
            dve.tensor_tensor(GSC["t1"][:, 0:16].rearrange("p (t n) -> p t n", n=4), gl, b4(sv(0)), ALU.subtract)\
               .then_inc(s["route_exp"], 1)
            t16 = R[:, 5, :, :]
            link(dve.tensor_tensor(t16.rearrange("p t (g e) -> p t g e", e=4), el.rearrange("p t (g e) -> p t g e", e=4),
                                   ghot.unsqueeze(3).to_broadcast([P, TB, 4, 4]), ALU.mult))
            link(dve.tensor_reduce(ingrp, t16.rearrange("p t (g e) -> p t e g", e=4), AX.X, ALU.add))
            link(dve.tensor_reduce(sv(2), ingrp, AX.X, ALU.max))
            one_hot(h1, ingrp, sv(3), sv(2))
            link(dve.scalar_tensor_tensor(e2, h1, NEG, ingrp, ALU.mult, ALU.add))
            link(dve.tensor_reduce(sv(4), e2, AX.X, ALU.max))
            one_hot(h2, e2, sv(5), sv(4))
            dve.tensor_tensor(GSC["t0"][:, 0:4], sv(4), sv(2), ALU.subtract).then_inc(s["route_exp"], 1)
            dve.wait_ge(s["gate_exp"], 5)
            gs = GSC["t2"][:, 0:16].rearrange("p (t n) -> p t n", n=4)
            link(dve.tensor_reduce(sv(6), gs, AX.X, ALU.add))
            link(dve.tensor_scalar(sv(7), GSC["t3"][:, 0:4], 1.0, None, ALU.add))
            link(dve.tensor_tensor(sv(8), sv(6), sv(7), ALU.mult))
            link(dve.reciprocal(sv(8), sv(8)))
            link(dve.tensor_tensor(sv(9), sv(8), GSC["t3"][:, 0:4], ALU.mult))
            o1, o2, both, pos = (IW[:, 64 * n:64 * n + 64].rearrange("p (t n) -> p t n", n=NE) for n in (1, 2, 3, 4))
            for dst, hot in ((o1, h1), (o2, h2)):
                link(dve.tensor_tensor(dst.rearrange("p t (g e) -> p t g e", e=4),
                                       ghot.unsqueeze(3).to_broadcast([P, TB, 4, 4]),
                                       hot.unsqueeze(2).to_broadcast([P, TB, 4, 4]), ALU.mult))
            dve.tensor_tensor(both, o1, o2, ALU.add).then_inc(s["route_set"], 1)
            product_ready(dve, ("rank",))
            rk = bank(("rank",))
            incl = rk[:, 0:64].rearrange("p (t n) -> p t n", n=NE)
            count = IW[:, 320:336]
            sums = [IW[:, 336:352], IW[:, 352:368]]
            tiles = IW[:, 368:384]
            link(dve.tensor_copy(count, rk[:, 64:80]))
            link(dve.tensor_scalar(tiles, count, 0.0, None, ALU.is_gt))
            for k in range(1, T // P):
                link(dve.scalar_tensor_tensor(tiles, count, float(P * k), tiles, ALU.is_gt, ALU.add))
            link(dve.tensor_copy(sums[0], tiles))
            for k in range(4):
                a, b, w = sums[k % 2], sums[1 - k % 2], 1 << k
                link(dve.tensor_copy(b[:, 0:w], a[:, 0:w]))
                link(dve.tensor_tensor(b[:, w:NE], a[:, w:NE], a[:, 0:NE - w], ALU.add))
            ends = sums[0]
            cmp = IS[:, 0:512].rearrange("p (j n) -> p j n", n=NE)
            rowj = col[:, K_ROW:K_ROW + 32]
            link(dve.tensor_tensor(cmp, ends.unsqueeze(1).to_broadcast([P, 32, NE]),
                                   rowj.unsqueeze(2).to_broadcast([P, 32, NE]), ALU.is_le))
            e_of = IW[:, 384:416]
            link(dve.tensor_reduce(e_of, cmp, AX.X, ALU.add))
            dve.tensor_scalar(eid[:, :], e_of, float(NE - 1), None, ALU.min).then_inc(experts_set, 1)
            link(dve.tensor_tensor(tiles, ends, tiles, ALU.subtract))
            link(dve.tensor_scalar(pos, incl, float(P), -float(P * TILES - 1), ALU.is_gt, ALU.mult))
            over = IW[:, 448:512].rearrange("p (t n) -> p t n", n=NE)
            for k in range(2, T // P):
                link(dve.tensor_scalar(over, incl, float(P * k), -float(P * TILES - 1), ALU.is_gt, ALU.mult))
                link(dve.tensor_tensor(pos, pos, over, ALU.add))
            link(dve.scalar_tensor_tensor(pos, incl, float(TILES), pos, ALU.mult, ALU.add))
            took(("rank",), dve.scalar_tensor_tensor(pos, pos, -float(TILES),
                                                     tiles.unsqueeze(1).to_broadcast([P, TB, NE]), ALU.add, ALU.add))
            own(("rank",))
            fad = IW[:, 512:520]
            for n, o in enumerate((o1, o2)):
                link(dve.tensor_tensor(over, o, pos, ALU.mult))
                link(dve.tensor_reduce(fad[:, TB * n:TB * n + TB], over, AX.X, ALU.add))
            dve.tensor_copy(token[:, :], col[:, K_TOKEN:K_TOKEN + TB]).then_inc(address_set, 1)
            dve.tensor_copy(address[:, :], fad).then_inc(address_set, 1)

            def evacuate_h(j, slot):
                dve.wait_ge(turned, j + 1)
                wait_from(dve, gu_done, j - 1)
                for k in range(4, KD):
                    ins = dve.tensor_scalar(HX[slot][:, k, :], ps[1][:, (k - 4) * P:(k - 3) * P], acol[:, 1, k:k + 1],
                                            mod[:, 16 + k:17 + k], ALU.mult, ALU.add)
                ins.then_inc(h_vector, 1)

            def evacuate_out(j, slot):
                dve.wait_ge(down_done, j + 1)
                wait_from(dve, tile_stored[slot], 16 * (j // 2) if isinstance(j, int) else (j - slot) * 8)
                dve.tensor_copy(YT[slot][:, 512:1024], ps[6][:, :]).then_inc(out_vector, 1)

            def step(j, slot):
                dve.wait_ge(silu_done, j + 1)
                wait_from(dve, act_turned, j - 1)
                dve.tensor_tensor(AC[slot], SI[slot], ps[2 + slot][:, 256:512], ALU.mult).then_inc(act_done, 1)
                if not isinstance(j, int) or j < TILES - 1:
                    evacuate_h(j + 1, 1 - slot)
                if not isinstance(j, int) or j >= 1:
                    evacuate_out(j - 1, 1 - slot)
            evacuate_h(0, 0)
            steps(dve, step)
            evacuate_out(TILES - 1, (TILES - 1) % 2)
            for t in range(TB + 1):
                if t < TB:
                    dve.wait_ge(both_in[t], 32)
                    dve.wait_ge(s["y_set"], t + 1)
                    dve.scalar_tensor_tensor(Y1[:, t, :], Y2[:, t, :], sv(9)[:, t:t + 1], Y1[:, t, :], ALU.mult, ALU.add)\
                       .then_inc(s["y_sum"], 1)
                if t >= 1:
                    dve.wait_ge(s["mse_root"], TB + t)
                    r = rstd[:, t - 1:t]
                    link(dve.reciprocal(r, r))
                    link(dve.scalar_tensor_tensor(Y1[:, t - 1, :], Y1[:, t - 1, :], r, g2p[:, :], ALU.mult, ALU.mult))
                    dve.tensor_tensor(XN[:, t - 1, :], X[:, t - 1, :], Y1[:, t - 1, :], ALU.add).then_inc(s["post_norm"], 1)

        @block.tensor
        def _(pe):
            at = [0]

            def begin(name):
                n = at[0]
                assert PLAN[n][0] == name, (PLAN[n], name)
                if n >= BANKS:
                    who, turn = TURN[PLAN[n - BANKS][0]]
                    pe.wait_ge(vector_took if who == "v" else scalar_took, turn)
                return ps[n % BANKS]

            def end(ins):
                ins.then_inc(product_done, 1)
                at[0] += 1

            def mm(o, a, b, first=True, last=True):
                return pe.matmul(o, a, b, start=first, stop=last)

            def taken(name):
                who, turn = TURN[name]
                pe.wait_ge(vector_took if who == "v" else scalar_took, turn)

            def four_transposes(name, src):
                b = begin(name)
                for k in range(4):
                    ins = pe.transpose(b[:, k * P:(k + 1) * P], src(k), ident)
                end(ins)

            def ada_row(n):
                b = begin(("ada", n))
                for u in range(2):
                    k = 2 * n + u
                    ada_ready(pe, k)
                    for j in range(KD):
                        ins = mm(b[0:1, 256 * u:256 * u + 256], ccol[:, j:j + 1], ada_slot(k)[:, j, :], j == 0, False)
                    ins.then_inc(ada_used, 1)
                    ins = mm(b[0:1, 256 * u:256 * u + 256], sq[0:12, M_ID, n:n + 1],
                             bada[:, 256 * u:256 * u + 256], False, True)
                end(ins)

            def ada(n, k):
                b = begin(("ada", n))
                pe.wait_ge(s["ada_summed"], n - 3)
                mm(b[:, :], ones[:, :], ada_sum[:, n % 2, :], True, False)
                end(mm(b[:, :], sq[0:12, M_ID, n:n + 1].to_broadcast([12, P]), bada[:, :], False, True))

            def adac(n, k):
                b = begin(("adac", n))
                taken(("ada", n))
                for j in range(4):
                    ins = mm(b[:, j:j + 1], modrow(n, k)[:, j * P:(j + 1) * P], ones[0:1, 0:1])
                end(ins)

            def features(name, w, m):
                b = begin(name)
                for k in range(KD):
                    ins = mm(b[:, :], w[:, k, m * P:(m + 1) * P], HT[:, k, :], k == 0, k == KD - 1)
                end(ins)

            def tokens(name, w, t):
                b = begin(name)
                for k in range(KD):
                    ins = mm(b[:, :], HT[:, k, t * P:(t + 1) * P], w[:, k, :], k == 0, k == KD - 1)
                end(ins)

            def used():
                pe.wait_ge(product_done, at[0])
                pe.sem_inc(weights_used, 1)

            pe.wait_ge(rows_in, 64)
            pe.wait_ge(consts_in, 32)
            b = begin(("rows",))
            end(pe.transpose(b[:, 0:N_ROWS], rows[:, :], sq[0:N_ROWS, M_ID, 0:N_ROWS]))
            pe.wait_ge(s["ones_set"], 1)
            pe.wait_ge(bias_in, 16)
            pe.wait_ge(s["ccol_done"], 1)
            for n in range(5):
                if n < 4:
                    ada_row(n)
                if n >= 1:
                    adac(n - 1, n - 1)
            pe.wait_ge(s["xn_done"], TB)
            for f in range(KD):
                four_transposes(("h1", f), lambda t: XN[:, t, f * P:(f + 1) * P])
            taken(("h1", KD - 1))
            taken(("h1", KD - 2))
            seq = rotated()

            def swap(n):
                b = begin(("swap",) + seq[n])
                pe.wait_ge(s["raw_set"], n + 1)
                end(mm(b[:, :], sq[:, M_SWAP, :], raw[:, n % 2, :]))

            for n, it in enumerate(seq):
                kind, m = it
                wname = {"q": "q", "k": "k", "iq": "iq", "ik": "small"}[kind]
                if m == 0:
                    weights_ready(pe, wname)
                features(("rope",) + it, wslot(wname), m)
                if n >= 1:
                    swap(n - 1)
                if m == 3:
                    used()
                if it == ("k", 3):
                    weights_ready(pe, "v")
                    for t in range(TB):
                        tokens(("v", t), wslot("v"), t)
                    used()
            swap(12)
            b = begin(("small",))
            for t in range(TB):
                for k in range(KD):
                    ins = mm(b[:, 32 * t:32 * t + 24], HT[:, k, t * P:(t + 1) * P], wslot("small")[:, k, 128:152],
                             k == 0, k == KD - 1)
            end(ins)
            used()
            k = 4
            for m in range(12):
                wname = ("gq", "gk", "gv")[m // 4]
                if m % 4 == 0:
                    weights_ready(pe, wname)
                features(("conv", m), wslot(wname), m % 4)
                if m % 4 == 3:
                    used()
                if m in (6, 9):
                    for n in (2 * (m // 3) + 2, 2 * (m // 3) + 3):
                        adac(n, k)
                        k += 1
                if m % 3 == 2:
                    for n in (4 + 2 * (m // 3), 5 + 2 * (m // 3)):
                        ada(n, k)
            weights_ready(pe, "z")
            tokens(("z", 0), wslot("z"), 0)
            b = begin(("gc",))
            pe.wait_ge(s["gbeta_set"], 1)
            end(mm(b[:, 0:32], sq[:, M_UPPER, :], GSC["g"]))
            pe.wait_ge(s["rope_set"], 13)
            for n in range(3 * H):
                qb, h = 1 + n // H, n % H
                b = begin(("idx", qb, h))
                rw = slice(64 * (h % 2), 64 * (h % 2) + 64)
                w = P * (qb + 1)
                end(mm(b[:, 0:w], IQ[rw, h // 2, qb * P:(qb + 1) * P], KI[rw, 0:w]))
                if n % 3 == 2:
                    m = n // 3
                    b = begin(("norm", m))
                    pe.wait_ge(s["square_set"], m + 1)
                    end(mm(b[:, :], sq[:, M_HEADS, :], Xf[:, 1024 + (m % 2) * 512:1536 + (m % 2) * 512]))
            tokens(("z", 1), wslot("z"), 1)
            pe.wait_ge(s["normed"], 8)
            for t in range(TB):
                four_transposes(("ktok", t), lambda m: C[:, 4 + m, t * P:(t + 1) * P])
            for t in range(TB):
                four_transposes(("vtok", t), lambda m: C[:, 8 + m, t * P:(t + 1) * P])
            tokens(("z", 2), wslot("z"), 2)
            tokens(("z", 3), wslot("z"), 3)
            used()
            def four(b, lhs, rhs):
                for hh in range(4):
                    ins = mm(b[:, hh * P:(hh + 1) * P], lhs(hh), rhs(hh))
                return ins

            def attend(n, want):
                for name in attention(n, want):
                    _, qb, h = name
                    w = P * (qb + 1)
                    b = begin(name)
                    if want == "s":
                        rw = slice(64 * (h % 2), 64 * (h % 2) + 64)
                        ins = mm(b[:, 0:w], QT[rw, h // 2, qb * P:(qb + 1) * P], KT[rw, h // 2, 0:w])
                    elif want == "pt":
                        pe.wait_ge(s["prob_set"], n)
                        for k in range(qb + 1):
                            ins = pe.transpose(b[:, k * P:(k + 1) * P], PR[(n - 1) % 2][:, k * P:(k + 1) * P], ident)
                    else:
                        taken(("pt", qb, h))
                        for k in range(qb + 1):
                            ins = mm(b[:, 0:DH], PT[n % 2][:, k * P:(k + 1) * P], V[:, k, h * DH:(h + 1) * DH],
                                     k == 0, k == qb)
                    end(ins)

            def early_gate(n):
                nm, m = EARLY_GATES[n]
                if m == 0:
                    weights_ready(pe, f"{nm}0")
                features((nm, m), wslot(f"{nm}0"), m)
                if m == 3:
                    used()

            for c in range(TB):
                tok = slice(c * P, (c + 1) * P)
                for g in range(2):
                    u, A = 2 * c + g, G[g]
                    b = begin(("gcb", c, g))
                    pe.wait_ge(s["diff_set"], u + 1)
                    end(four(b, lambda hh: A["LM"][:, hh * P:(hh + 1) * P], lambda hh: sq[:, M_UPPER, :]))
                for nm, at_ in (("kk", 4), ("qk", 0)):
                    for g in range(2):
                        rw = slice(64 * g, 64 * g + 64)
                        b = begin((nm, c, g))
                        end(four(b, lambda hh: C[rw, 4 + hh, tok], lambda hh: C[rw, at_ + hh, tok]))
                hp = lambda ap, hh: ap[:, hh * P:(hh + 1) * P]
                for lv in range(LEVELS):
                    if lv > 0:
                        for g in range(2):
                            A = G[g]
                            b = begin(("Y", c, lv, g))
                            pe.wait_ge(s["lm_set"], (2 * c) * (LEVELS - 1) + 2 * (lv - 1) + g + 1)
                            taken(("T", c, lv - 1, g))
                            end(four(b, lambda hh: hp(A["LM"], hh), lambda hh: hp(A["XU"], hh)))
                    attend(first_step(c, lv), "s")
                    if lv > 0:
                        for g in range(2):
                            A = G[g]
                            b = begin(("Z", c, lv, g))
                            taken(("Y", c, lv, g))
                            end(four(b, lambda hh: hp(A["D"], hh), lambda hh: hp(A["XL"], hh)))
                    attend(first_step(c, lv), "pt")
                    attend(first_step(c, lv), "pv")
                    if lv == 0:
                        early_gate(2 * c)
                    for g in range(2):
                        A = G[g]
                        if lv == 0:
                            pe.wait_ge(s["x0_set"], 2 * c + g + 1)
                        else:
                            taken(("Z", c, lv, g))
                        four_transposes(("T", c, lv, g), lambda hh: hp(A["XL"], hh))
                    for n in second_step(c, lv):
                        for kind in ("s", "pt", "pv"):
                            attend(n, kind)
                for g in range(2):
                    A = G[g]
                    b = begin(("nw", c, g))
                    taken(("T", c, LEVELS - 1, g))
                    pe.wait_ge(s["g_operands"], 2 * (2 * c + g) + 2)
                    rw = slice(64 * g, 64 * g + 64)
                    end(four(b[rw, :], lambda hh: A["KBG"][:, hh * DH:(hh + 1) * DH], lambda hh: hp(A["XU"], hh)))
                early_gate(2 * c + 1)
                for g in range(2):
                    u, A = 2 * c + g, G[g]
                    b = begin(("vn", c, g))
                    pe.wait_ge(s["nw_set"], u + 1)
                    if c > 0:
                        pe.wait_ge(s["state_set"], u - 1)
                    for hh in range(4):
                        rw = slice(64 * g, 64 * g + 64)
                        o = b[:, hh * DH:(hh + 1) * DH]
                        mm(o, hp(A["XU"], hh), A["VB"][:, hh * DH:(hh + 1) * DH], True, False)
                        ins = mm(o, heads(A["NW"])[rw, hh, :], S[rw, hh, :], False, True)
                    end(ins)
                for g in range(2):
                    u, A = 2 * c + g, G[g]
                    b = begin(("o", c, g))
                    pe.wait_ge(s["vn_set"], u + 1)
                    pe.wait_ge(s["qk_set"], c + 1)
                    for hh in range(4):
                        rw = slice(64 * g, 64 * g + 64)
                        o = b[:, hh * DH:(hh + 1) * DH]
                        mm(o, heads(A["QG"])[rw, hh, :], S[rw, hh, :], True, False)
                        ins = mm(o, hp(A["E1"], hh), A["VN"][:, hh * DH:(hh + 1) * DH], False, True)
                    end(ins)
                    if c < TB - 1:
                        b = begin(("st", c, g))
                        pe.wait_ge(s["kd_set"], u + 1)
                        for hh in range(4):
                            hd = slice(hh * DH, (hh + 1) * DH)
                            ins = mm(b[64 * g:64 * g + 64, hd], A["KDEC"][:, hd], A["VN"][:, hd])
                        end(ins)
            def branch(name, src, w, m):
                b = begin(name)
                for k in range(4):
                    ins = mm(b[:, :], w[:, k, m * P:(m + 1) * P], src[:, k, :], k == 0, k == 3)
                end(ins)

            pe.wait_ge(s["dsa_set"], len(TODO))
            for f in range(4):
                four_transposes(("ot", 0, f), lambda t: OD[:, t, f * P:(f + 1) * P])
            taken(("ot", 0, 3))
            weights_ready(pe, "br0")
            for m in range(4):
                branch(("ya", m), OAT, wslot("br0")[:, 0:4, :], m)
            pe.wait_ge(s["gdn_set"], 1)
            for f in range(4):
                four_transposes(("ot", 1, f), lambda t: OG[:, t, f * P:(f + 1) * P])
            taken(("ot", 1, 3))
            for m in range(4):
                branch(("yb", m), OGT, wslot("br0")[:, 4:8, :], m)
            used()
            for nm in ("ga", "gb"):
                weights_ready(pe, nm + "1")
                for m in range(4):
                    features((nm, 4 + m), wslot(nm + "1"), m)
                used()
            weights_ready(pe, "br1")
            for m in range(4):
                branch(("ya", 4 + m), OAT, wslot("br1")[:, 0:4, :], m)
                branch(("yb", 4 + m), OGT, wslot("br1")[:, 4:8, :], m)
            used()
            pe.wait_ge(s["merged_set"], 2 * KD)
            weights_ready(pe, "out0")
            weights_ready(pe, "out1")
            for nm, t in TAIL:
                if nm == "y":
                    for u in range(2):
                        b = begin(("y", t, u))
                        for k in range(KD):
                            ins = mm(b[:, :], MT[:, k, t * P:(t + 1) * P], wslot(f"out{u}")[:, k, :], k == 0, k == KD - 1)
                        end(ins)
                    if t == TB - 1:
                        used()
                        used()
                elif nm == "h2":
                    pe.wait_ge(s["xn_done"], TB + t + 1)
                    for u in range(2):
                        four_transposes(("h2", t, u), lambda k: XN[:, t, (4 * u + k) * P:(4 * u + k + 1) * P])
                else:
                    b = begin(("router", t))
                    taken(("h2", t, 0))
                    taken(("h2", t, 1))
                    for k in range(KD):
                        ins = mm(b[:, 0:20], HT[:, k, t * P:(t + 1) * P], wroute[:, k, :], k == 0, k == KD - 1)
                    end(ins)
            b = begin(("rank",))
            pe.wait_ge(s["route_set"], 1)
            both = IW[:, 192:256].rearrange("p (t n) -> p t n", n=NE)
            mm(b[:, 0:NE * TB], sq[:, M_UPPER, :], both, True, False)
            for k in range(TB - 1):
                mm(b[:, NE * (k + 1):NE * TB], ones[:, :], both[:, k, :].unsqueeze(1).to_broadcast([P, TB - 1 - k, NE]),
                   False, k == TB - 2)
            for k in range(TB):
                ins = mm(b[:, 64:80], ones[:, :], both[:, k, :], k == 0, k == TB - 1)
            end(ins)
            taken(("rank",))

            def turn_rows(j, slot):
                pe.wait_ge(rows_gathered[slot], 16 * (j // 2 + 1) if isinstance(j, int) else (j - slot) * 8 + 16)
                wait_from(pe, h_scalar, j)
                wait_from(pe, h_vector, j)
                for k in range(KD):
                    ins = pe.transpose(ps[k // 4][:, (k % 4) * P:(k % 4 + 1) * P], GX[:, slot, k * P:(k + 1) * P], ident)
                ins.then_inc(turned, 1)

            def gate_up(j, slot):
                pe.wait_ge(gate_up_in[slot], 32 * (j // 2 + 1) if isinstance(j, int) else (j - slot) * 16 + 32)
                pe.wait_ge(h_scalar, j + 1)
                pe.wait_ge(h_vector, j + 1)
                wait_from(pe, act_done, j - 1)
                gu = expert_gu(slot)
                for k in range(KD):
                    ins = mm(ps[2 + slot][:, :], HX[slot][:, k, :], gu[:, k].rearrange("p u f -> p (u f)"),
                             k == 0, k == KD - 1)
                ins.then_inc(gu_done, 1)

            def turn_act(j, slot):
                pe.wait_ge(act_done, j + 1)
                wait_from(pe, act_back, j)
                for k in range(2):
                    ins = pe.transpose(ps[4][:, k * P:(k + 1) * P], AC[slot][:, k * P:(k + 1) * P], ident)
                ins.then_inc(act_turned, 1)

            def down(j, slot):
                pe.wait_ge(down_in[slot], 16 * (j // 2 + 1) if isinstance(j, int) else (j - slot) * 8 + 16)
                pe.wait_ge(act_back, j + 1)
                wait_from(pe, out_scalar, j)
                wait_from(pe, out_vector, j)
                dn = expert_d(slot)
                for u in range(2):
                    for k in range(2):
                        ins = mm(ps[5 + u][:, :], ACT_T[slot][:, k * P:(k + 1) * P], dn[:, k, 512 * u:512 * u + 512],
                                 k == 0, k == 1)
                ins.then_inc(down_done, 1)

            def step(j, slot):
                gate_up(j, slot)
                if not isinstance(j, int) or j >= 1:
                    turn_act(j - 1, 1 - slot)
                if not isinstance(j, int) or j < TILES - 1:
                    turn_rows(j + 1, 1 - slot)
                if not isinstance(j, int) or j >= 1:
                    down(j - 1, 1 - slot)
            turn_rows(0, 0)
            steps(pe, step)
            turn_act(TILES - 1, (TILES - 1) % 2)
            down(TILES - 1, (TILES - 1) % 2)


_INS = ['x', 'c', 'positions', 'w_ada', 'b_ada', 'mix_norm_pre', 'mix_norm_post', 'w_in', 'conv_w', 'a_log', 'dt_bias',
        'gdn_norm', 'w_branch_dsa', 'w_branch_gdn', 'w_out', 'ffn_norm_pre', 'ffn_norm_post', 'w_router_group',
        'b_router_group', 'w_router_expert', 'b_router_expert', 'w_expert_gate', 'w_expert_up', 'w_expert_down']


def kernel(**inputs):
    import numpy as _np
    import concourse.bacc as _bacc
    from concourse import mybir as _mybir
    from concourse.bass_utils import run_bass_kernel_spmd as _run

    nc = _bacc.Bacc("TRN2", target_bir_lowering=False, num_devices=1, dynamic_dma_scratch_size=4096)
    arrays, args = {}, []
    for name in _INS:
        a = _np.ascontiguousarray(_np.asarray(inputs[name])[0])
        arrays[f"in_{name}"] = a
        args.append(nc.dram_tensor(f"in_{name}", a.shape, _mybir.dt.from_np(a.dtype), kind="ExternalInput").ap())
    for name, a in zip(("squares", "columns"), constants()):
        arrays[name] = a
        args.append(nc.dram_tensor(name, a.shape, _mybir.dt.float32, kind="ExternalInput").ap())
    out = nc.dram_tensor("out", (T, D), _mybir.dt.float32, kind="ExternalOutput").ap()
    layer_kernel(nc, *args, out)
    r = _run(nc, [arrays], core_ids=[0])
    return r.results[0]["out"].reshape(1, T, D)
```
